# Optimizing a Trainium2 kernel written in Bass

```python
import math
import jax, jax.numpy as jnp
from jax import lax
import numpy as np

D_MODEL = 1024
BATCH = 1
SEQ = 256
DEPTH = 1

N_MIXERS = 3
N_LAYERS_A = len(range(0, DEPTH, N_MIXERS))
N_LAYERS_B = len(range(1, DEPTH, N_MIXERS))
N_LAYERS_C = len(range(2, DEPTH, N_MIXERS))

DEEPNORM_ALPHA = (2.0 * DEPTH) ** 0.25
DEEPNORM_BETA = (8.0 * DEPTH) ** -0.25
LN_EPS = 1e-5

A_HEADS = 8
A_HEAD_DIM = D_MODEL // A_HEADS
MOBA_BLOCK = 256
MOBA_TOPK = 3
MOBA_Q_CHUNK = 16
REL_BUCKETS = 32
REL_MAX_DIST = 128

B_GROUPS = 8
B_WIDTH = 2 * D_MODEL
B_CHUNK = 128

C_HEADS = 4
C_KEY_DIM = D_MODEL // 2
C_VAL_DIM = D_MODEL
C_DK = C_KEY_DIM // C_HEADS
C_DV = C_VAL_DIM // C_HEADS
C_GATE_RANK = 16
C_GATE_NORMALIZER = 16.0
C_CHUNK = 64
C_IN_WIDTH = 2 * C_KEY_DIM + 2 * C_VAL_DIM + C_GATE_RANK

N_EXPERTS = 32
TOP_K = 4
D_EXPERT = D_MODEL
SWIGLU_LIMIT = 7.0
SWIGLU_ALPHA = 1.702
MOE_ROW_BLOCK = 128


def layer_norm(x, g, b):
    xf = x.astype(jnp.float32)
    mu = xf.mean(-1, keepdims=True)
    var = jnp.square(xf - mu).mean(-1, keepdims=True)
    y = (xf - mu) * lax.rsqrt(var + LN_EPS) * g.astype(jnp.float32) + b.astype(jnp.float32)
    return y.astype(x.dtype)

def rms_norm(x, g):
    xf = x.astype(jnp.float32)
    return xf * lax.rsqrt(jnp.mean(xf * xf, -1, keepdims=True) + LN_EPS) * g.astype(jnp.float32)

def t5_bucket(rel):
    n = jnp.maximum(rel, 0)
    max_exact = REL_BUCKETS // 2
    nf = jnp.maximum(n, 1).astype(jnp.float32)
    large = max_exact + (jnp.log(nf / max_exact) / math.log(REL_MAX_DIST / max_exact)
                         * (REL_BUCKETS - max_exact)).astype(jnp.int32)
    large = jnp.minimum(large, REL_BUCKETS - 1)
    return jnp.where(n < max_exact, n, large)

def moba_attention(x, w_in, w_out, rel_bias):
    B, S, _ = x.shape
    H, Dh, BLK, QC = A_HEADS, A_HEAD_DIM, MOBA_BLOCK, MOBA_Q_CHUNK
    qkv = (x @ w_in).reshape(B, S, 3, H, Dh)
    q = qkv[:, :, 0].transpose(0, 2, 1, 3)
    k = qkv[:, :, 1].transpose(0, 2, 1, 3)
    v = qkv[:, :, 2].transpose(0, 2, 1, 3)
    nb = -(-S // BLK)
    pad = nb * BLK - S
    kb = jnp.pad(k, ((0, 0), (0, 0), (0, pad), (0, 0))).reshape(B, H, nb, BLK, Dh)
    vb = jnp.pad(v, ((0, 0), (0, 0), (0, pad), (0, 0))).reshape(B, H, nb, BLK, Dh)
    k_mean = kb.astype(jnp.float32).mean(axis=3)
    gate = jnp.einsum('bhsd,bhnd->bhsn', q.astype(jnp.float32), k_mean)
    pos = jnp.arange(S)
    past = jnp.arange(nb)[None, :] < (pos // BLK)[:, None]
    gate = jnp.where(past, gate, -jnp.inf)
    k_sel = min(MOBA_TOPK, nb)
    sel_score, sel_idx = lax.top_k(gate, k_sel)
    sel_valid = jnp.isfinite(sel_score)

    rel_t = rel_bias.T
    bi = jnp.arange(B)[:, None, None, None]
    hi = jnp.arange(H)[None, :, None, None]
    scale = Dh ** -0.5
    offs = jnp.arange(BLK)

    def attend_chunk(t0):
        qc = lax.dynamic_slice_in_dim(q, t0, QC, axis=2)
        idx = lax.dynamic_slice_in_dim(sel_idx, t0, QC, axis=2)
        valid = lax.dynamic_slice_in_dim(sel_valid, t0, QC, axis=2)
        qpos = t0 + jnp.arange(QC)
        kg = kb[bi, hi, idx]
        vg = vb[bi, hi, idx]
        s_sel = jnp.einsum('bhqd,bhqnjd->bhqnj', qc, kg).astype(jnp.float32) * scale
        rel_sel = qpos[None, None, :, None, None] - (idx[..., None] * BLK + offs)
        s_sel = jnp.where(valid[..., None],
                          s_sel + rel_t[hi[..., None], t5_bucket(rel_sel)], -jnp.inf)
        own = t0 // BLK
        ko = lax.dynamic_index_in_dim(kb, own, axis=2, keepdims=False)
        vo = lax.dynamic_index_in_dim(vb, own, axis=2, keepdims=False)
        rel_own = qpos[:, None] - (own * BLK + offs)[None, :]
        s_own = (jnp.einsum('bhqd,bhjd->bhqj', qc, ko).astype(jnp.float32) * scale
                 + rel_t[:, t5_bucket(rel_own)])
        s_own = jnp.where(rel_own >= 0, s_own, -jnp.inf)
        logits = jnp.concatenate([s_sel.reshape(B, H, QC, k_sel * BLK), s_own], axis=-1)
        p = jax.nn.softmax(logits, axis=-1).astype(v.dtype)
        p_sel = p[..., :k_sel * BLK].reshape(B, H, QC, k_sel, BLK)
        p_own = p[..., k_sel * BLK:]
        return (jnp.einsum('bhqnj,bhqnjd->bhqd', p_sel, vg)
                + jnp.einsum('bhqj,bhjd->bhqd', p_own, vo))

    o = lax.map(attend_chunk, jnp.arange(0, S, QC))
    o = o.transpose(1, 0, 3, 2, 4).reshape(B, S, H * Dh)
    return o @ w_out

def gmlp_mixer(x, w_in, ln_g, ln_b, w_s, b_s, w_out):
    B, S, _ = x.shape
    z = jax.nn.gelu(x @ w_in, approximate=False)
    u, v = jnp.split(z, 2, axis=-1)
    v = layer_norm(v, ln_g, ln_b)
    gw = B_WIDTH // B_GROUPS
    vc = v.reshape(B, S // B_CHUNK, B_CHUNK, B_GROUPS, gw)
    ws = w_s * jnp.tril(jnp.ones((B_CHUNK, B_CHUNK), w_s.dtype))
    mixed = jnp.einsum('gts,bcsge->bctge', ws, vc) + b_s.T[None, None, :, :, None]
    y = u * mixed.reshape(B, S, B_WIDTH)
    return y @ w_out

def gla_mixer(x, w_in, w_gk_up, b_gk, norm_g, w_out):
    B, S, _ = x.shape
    proj = x @ w_in
    splits = [C_KEY_DIM, 2 * C_KEY_DIM, 2 * C_KEY_DIM + C_VAL_DIM, 2 * C_KEY_DIM + 2 * C_VAL_DIM]
    q, k, v, g, gk_low = jnp.split(proj, splits, axis=-1)
    log_a = jax.nn.log_sigmoid((gk_low @ w_gk_up + b_gk).astype(jnp.float32)) / C_GATE_NORMALIZER
    nc = S // C_CHUNK

    def heads(t, dh):
        return t.astype(jnp.float32).reshape(B, nc, C_CHUNK, C_HEADS, dh).transpose(1, 0, 3, 2, 4)

    qh = heads(q, C_DK) * (C_DK ** -0.5)
    kh = heads(k, C_DK)
    vh = heads(v, C_DV)
    ah = heads(log_a, C_DK)
    causal = jnp.tril(jnp.ones((C_CHUNK, C_CHUNK), bool))

    def step(state, inp):
        qc, kc, vc, ac = inp
        b = jnp.cumsum(ac, axis=2)
        o_inter = jnp.einsum('bhck,bhkv->bhcv', qc * jnp.exp(b), state)
        diff = b[:, :, :, None, :] - b[:, :, None, :, :]
        diff = jnp.where(causal[None, None, :, :, None], diff, -jnp.inf)
        att = jnp.einsum('bhik,bhjk,bhijk->bhij', qc, kc, jnp.exp(diff))
        o_intra = jnp.einsum('bhij,bhjv->bhiv', att, vc)
        b_last = b[:, :, -1:, :]
        new_state = (jnp.exp(b_last[:, :, 0, :])[..., None] * state
                     + jnp.einsum('bhck,bhcv->bhkv', kc * jnp.exp(b_last - b), vc))
        return new_state, o_inter + o_intra

    state0 = jnp.zeros((B, C_HEADS, C_DK, C_DV), jnp.float32)
    _, o = lax.scan(step, state0, (qh, kh, vh, ah))
    o = o.transpose(1, 0, 3, 2, 4).reshape(B, S, C_HEADS, C_DV)
    o = rms_norm(o, norm_g) * jax.nn.silu(g.reshape(B, S, C_HEADS, C_DV).astype(jnp.float32))
    return o.reshape(B, S, C_VAL_DIM).astype(x.dtype) @ w_out

def moe_ffn(x, w_router, b_router, w_gu, b_gu, w_down, b_down):
    B, S, D = x.shape
    T = B * S
    xt = x.reshape(T, D)
    logits = (xt @ w_router + b_router).astype(jnp.float32)
    top_logit, top_e = lax.top_k(logits, TOP_K)
    gate = jax.nn.softmax(top_logit, axis=-1)
    n_assign = T * TOP_K
    flat_e = top_e.reshape(-1)
    flat_tok = jnp.arange(n_assign) // TOP_K
    order = jnp.argsort(flat_e)
    e_sorted = flat_e[order]
    tok_sorted = flat_tok[order]
    gate_sorted = gate.reshape(-1)[order]
    counts = jnp.zeros((N_EXPERTS,), jnp.int32).at[flat_e].add(1)
    padded = (counts + MOE_ROW_BLOCK - 1) // MOE_ROW_BLOCK * MOE_ROW_BLOCK
    start = jnp.cumsum(counts) - counts
    pend = jnp.cumsum(padded)
    pstart = pend - padded
    dest = pstart[e_sorted] + (jnp.arange(n_assign) - start[e_sorted])
    n_blocks = -(-n_assign // MOE_ROW_BLOCK) + N_EXPERTS
    n_rows = n_blocks * MOE_ROW_BLOCK
    row_tok = jnp.full((n_rows,), T, jnp.int32).at[dest].set(tok_sorted)
    x_pad = jnp.concatenate([xt, jnp.zeros((1, D), xt.dtype)], axis=0)
    xs = x_pad[row_tok].reshape(n_blocks, MOE_ROW_BLOCK, D)
    block_e = jnp.minimum(
        jnp.searchsorted(pend, jnp.arange(n_blocks) * MOE_ROW_BLOCK, side='right'), N_EXPERTS - 1)

    def expert_block(args):
        xb, e = args
        h = xb @ w_gu[e] + b_gu[e]
        h_gate, h_up = jnp.split(h, 2, axis=-1)
        h_gate = jnp.minimum(h_gate, SWIGLU_LIMIT)
        h_up = jnp.clip(h_up, -SWIGLU_LIMIT, SWIGLU_LIMIT)
        act = h_gate * jax.nn.sigmoid(SWIGLU_ALPHA * h_gate) * (h_up + 1.0)
        return act @ w_down[e] + b_down[e]

    ys = lax.map(expert_block, (xs, block_e)).reshape(n_rows, D)
    y_assign = ys[dest] * gate_sorted[:, None].astype(ys.dtype)
    y = jax.ops.segment_sum(y_assign, tok_sorted, num_segments=T)
    return y.reshape(B, S, D)

def first_inputs(seed: int = 0) -> dict:
    key = jax.random.key(seed)
    ks = jax.random.split(key, 23)
    f32 = jnp.float32
    D = D_MODEL

    def nrm(k, shape, scale):
        return jax.random.normal(k, shape, f32) * scale

    return {
        "x": nrm(ks[0], (BATCH, SEQ, D), 1.0),
        "rel_bias": nrm(ks[1], (REL_BUCKETS, A_HEADS), 0.5),
        "a_w_in": nrm(ks[2], (N_LAYERS_A, D, 3 * D), D ** -0.5),
        "a_w_out": nrm(ks[3], (N_LAYERS_A, D, D), D ** -0.5 * DEEPNORM_BETA),
        "b_w_in": nrm(ks[4], (N_LAYERS_B, D, 2 * B_WIDTH), D ** -0.5),
        "b_ln_g": 1.0 + nrm(ks[5], (N_LAYERS_B, B_WIDTH), 0.02),
        "b_ln_b": nrm(ks[6], (N_LAYERS_B, B_WIDTH), 0.02),
        "b_w_s": nrm(ks[7], (N_LAYERS_B, B_GROUPS, B_CHUNK, B_CHUNK), B_CHUNK ** -0.5),
        "b_b_s": 1.0 + nrm(ks[8], (N_LAYERS_B, B_GROUPS, B_CHUNK), 0.02),
        "b_w_out": nrm(ks[9], (N_LAYERS_B, B_WIDTH, D), B_WIDTH ** -0.5 * DEEPNORM_BETA),
        "c_w_in": nrm(ks[10], (N_LAYERS_C, D, C_IN_WIDTH), D ** -0.5),
        "c_w_gk_up": nrm(ks[11], (N_LAYERS_C, C_GATE_RANK, C_KEY_DIM), C_GATE_RANK ** -0.5),
        "c_b_gk": nrm(ks[12], (N_LAYERS_C, C_KEY_DIM), 0.1),
        "c_norm_g": 1.0 + nrm(ks[13], (N_LAYERS_C, C_DV), 0.02),
        "c_w_out": nrm(ks[14], (N_LAYERS_C, C_VAL_DIM, D), C_VAL_DIM ** -0.5 * DEEPNORM_BETA),
        "ln_g": 1.0 + nrm(ks[15], (DEPTH, 2, D), 0.02),
        "ln_b": nrm(ks[16], (DEPTH, 2, D), 0.02),
        "moe_w_router": nrm(ks[17], (DEPTH, D, N_EXPERTS), D ** -0.5),
        "moe_b_router": nrm(ks[18], (DEPTH, N_EXPERTS), 0.01),
        "moe_w_gate_up": nrm(ks[19], (DEPTH, N_EXPERTS, D, 2 * D_EXPERT), D ** -0.5),
        "moe_b_gate_up": nrm(ks[20], (DEPTH, N_EXPERTS, 2 * D_EXPERT), 0.01),
        "moe_w_down": nrm(ks[21], (DEPTH, N_EXPERTS, D_EXPERT, D), D_EXPERT ** -0.5 * DEEPNORM_BETA),
        "moe_b_down": nrm(ks[22], (DEPTH, N_EXPERTS, D), 0.01),
    }

def first_block(x, rel_bias, a_w_in, a_w_out, b_w_in, b_ln_g, b_ln_b, b_w_s, b_b_s, b_w_out,
              c_w_in, c_w_gk_up, c_b_gk, c_norm_g, c_w_out, ln_g, ln_b,
              moe_w_router, moe_b_router, moe_w_gate_up, moe_b_gate_up, moe_w_down, moe_b_down):
    h = x
    for i in range(DEPTH):
        j = i // N_MIXERS
        mixer = i % N_MIXERS
        if mixer == 0:
            t = moba_attention(h, a_w_in[j], a_w_out[j], rel_bias)
        elif mixer == 1:
            t = gmlp_mixer(h, b_w_in[j], b_ln_g[j], b_ln_b[j], b_w_s[j], b_b_s[j], b_w_out[j])
        else:
            t = gla_mixer(h, c_w_in[j], c_w_gk_up[j], c_b_gk[j], c_norm_g[j], c_w_out[j])
        h = layer_norm(DEEPNORM_ALPHA * h + t, ln_g[i, 0], ln_b[i, 0])
        f = moe_ffn(h, moe_w_router[i], moe_b_router[i], moe_w_gate_up[i], moe_b_gate_up[i],
                    moe_w_down[i], moe_b_down[i])
        h = layer_norm(DEEPNORM_ALPHA * h + f, ln_g[i, 1], ln_b[i, 1])
    return h


DEPTH_2 = 2

N_HEADS = 16
HEAD_DIM = D_MODEL // N_HEADS
D_FF = ((8 * D_MODEL // 3 + 127) // 128) * 128
CONV_WIDTH = 3
Q_BLOCK = 128
N_MIXERS_2 = 2
N_MOD = 6
RMS_EPS = 1e-6
N_SB_LAYERS = (DEPTH_2 + 1) // 2
N_FOX_LAYERS = DEPTH_2 // 2


def rmsnorm(x, g):
    xf = x.astype(jnp.float32)
    y = xf * lax.rsqrt(jnp.mean(xf * xf, axis=-1, keepdims=True) + RMS_EPS)
    return (y * g.astype(jnp.float32)).astype(x.dtype)

def modulate(h, shift, scale):
    return h * (1.0 + scale[:, None, :]) + shift[:, None, :]

def split_heads(t):
    b, s, _ = t.shape
    return t.reshape(b, s, N_HEADS, HEAD_DIM).transpose(0, 2, 1, 3)

def merge_heads(t):
    b, h, s, d = t.shape
    return t.transpose(0, 2, 1, 3).reshape(b, s, h * d)

def stick_breaking_attention(q, k, v):
    s_len = q.shape[2]
    scale = HEAD_DIM ** -0.5
    outs = []
    for blk in range(s_len // Q_BLOCK):
        q0 = blk * Q_BLOCK
        k_end = q0 + Q_BLOCK
        qb, kb, vb = q[:, :, q0:k_end], k[:, :, :k_end], v[:, :, :k_end]
        z = jnp.einsum('bhqd,bhkd->bhqk', qb, kb).astype(jnp.float32) * scale
        t_idx = q0 + jnp.arange(Q_BLOCK)[:, None]
        s_idx = jnp.arange(k_end)[None, :]
        strict = s_idx < t_idx
        log_beta = jax.nn.log_sigmoid(z)
        log_1mb = jnp.where(strict, jax.nn.log_sigmoid(-z), 0.0)
        after = lax.cumsum(log_1mb, axis=3, reverse=True) - log_1mb
        a = jnp.where(strict, jnp.exp(log_beta + after), 0.0)
        outs.append(jnp.einsum('bhqk,bhkd->bhqd', a.astype(vb.dtype), vb))
    return jnp.concatenate(outs, axis=2)

def forgetting_attention(q, k, v, log_f):
    s_len = q.shape[2]
    scale = HEAD_DIM ** -0.5
    cum = lax.cumsum(log_f, axis=2)
    outs = []
    for blk in range(s_len // Q_BLOCK):
        q0 = blk * Q_BLOCK
        k_end = q0 + Q_BLOCK
        qb, kb, vb = q[:, :, q0:k_end], k[:, :, :k_end], v[:, :, :k_end]
        z = jnp.einsum('bhqd,bhkd->bhqk', qb, kb).astype(jnp.float32) * scale
        decay = cum[:, :, q0:k_end, None] - cum[:, :, None, :k_end]
        t_idx = q0 + jnp.arange(Q_BLOCK)[:, None]
        s_idx = jnp.arange(k_end)[None, :]
        logits = jnp.where(s_idx <= t_idx, z + decay, -jnp.inf)
        p = jax.nn.softmax(logits, axis=-1)
        outs.append(jnp.einsum('bhqk,bhkd->bhqd', p.astype(vb.dtype), vb))
    return jnp.concatenate(outs, axis=2)

def causal_depthwise_conv(h, w, b):
    s_len = h.shape[1]
    hp = jnp.pad(h, ((0, 0), (CONV_WIDTH - 1, 0), (0, 0)))
    out = b[None, None, :]
    for kk in range(CONV_WIDTH):
        out = out + w[kk][None, None, :] * hp[:, kk:kk + s_len]
    return out

def second_inputs(seed: int = 0) -> dict:
    key = jax.random.key(seed)
    ks = jax.random.split(key, 20)
    f32 = jnp.float32
    d, f, h = D_MODEL, D_FF, N_HEADS

    def nrm(k, shape, s):
        return jax.random.normal(k, shape, f32) * s

    return {
        "x": nrm(ks[0], (BATCH, SEQ, d), 1.0),
        "c": nrm(ks[1], (BATCH, d), 1.0),
        "w_mod": nrm(ks[2], (DEPTH_2, d, N_MOD * d), 0.5 * d ** -0.5),
        "b_mod": nrm(ks[3], (DEPTH_2, N_MOD * d), 0.02),
        "g_mix_pre": 1.0 + nrm(ks[4], (DEPTH_2, d), 0.05),
        "g_mix_post": 1.0 + nrm(ks[5], (DEPTH_2, d), 0.05),
        "w_qkv": nrm(ks[6], (DEPTH_2, d, 3 * d), d ** -0.5),
        "w_o": nrm(ks[7], (DEPTH_2, d, d), d ** -0.5),
        "w_fg": nrm(ks[8], (N_FOX_LAYERS, d, h), d ** -0.5),
        "b_fg": 3.0 + nrm(ks[9], (N_FOX_LAYERS, h), 0.5),
        "g_ffn_pre": 1.0 + nrm(ks[10], (DEPTH_2, d), 0.05),
        "g_ffn_post": 1.0 + nrm(ks[11], (DEPTH_2, d), 0.05),
        "w_ffn_gate": nrm(ks[12], (DEPTH_2, d, f), d ** -0.5),
        "w_ffn_up": nrm(ks[13], (DEPTH_2, d, f), d ** -0.5),
        "w_conv": nrm(ks[14], (DEPTH_2, CONV_WIDTH, f), CONV_WIDTH ** -0.5),
        "b_conv": nrm(ks[15], (DEPTH_2, f), 0.02),
        "w_ffn_down": nrm(ks[16], (DEPTH_2, f, d), f ** -0.5),
    }

def second_block(x, c, w_mod, b_mod, g_mix_pre, g_mix_post, w_qkv, w_o, w_fg, b_fg,
              g_ffn_pre, g_ffn_post, w_ffn_gate, w_ffn_up, w_conv, b_conv, w_ffn_down):
    c_act = jax.nn.silu(c)
    for i in range(DEPTH_2):
        mod = jnp.einsum('bd,dm->bm', c_act, w_mod[i]) + b_mod[i]
        sh_a, sc_a, gt_a, sh_f, sc_f, gt_f = jnp.split(mod, N_MOD, axis=-1)

        h = modulate(rmsnorm(x, g_mix_pre[i]), sh_a, sc_a)
        qkv = jnp.einsum('bsd,de->bse', h, w_qkv[i])
        q, k, v = (split_heads(t) for t in jnp.split(qkv, 3, axis=-1))
        if i % N_MIXERS_2 == 0:
            o = stick_breaking_attention(q, k, v)
        else:
            j = i // N_MIXERS_2
            f_logit = jnp.einsum('bsd,dh->bhs', h, w_fg[j]) + b_fg[j][None, :, None]
            log_f = jax.nn.log_sigmoid(f_logit.astype(jnp.float32))
            o = forgetting_attention(q, k, v, log_f)
        o = jnp.einsum('bse,ed->bsd', merge_heads(o), w_o[i])
        x = x + gt_a[:, None, :] * rmsnorm(o, g_mix_post[i])

        h = modulate(rmsnorm(x, g_ffn_pre[i]), sh_f, sc_f)
        gate = jnp.einsum('bsd,df->bsf', h, w_ffn_gate[i])
        up = jnp.einsum('bsd,df->bsf', h, w_ffn_up[i])
        gate = causal_depthwise_conv(gate, w_conv[i], b_conv[i])
        y = jnp.einsum('bsf,fd->bsd', jax.nn.silu(gate) * up, w_ffn_down[i])
        x = x + gt_f[:, None, :] * rmsnorm(y, g_ffn_post[i])
    return x


def setup_inputs(seed=0):
    out = dict(first_inputs(seed))
    for name, value in second_inputs(seed + 1).items():
        if name != "x":
            out[name + "_2"] = value
    return out


def reference(
    x, rel_bias, a_w_in, a_w_out, b_w_in, b_ln_g, b_ln_b, b_w_s, b_b_s, b_w_out, c_w_in,
    c_w_gk_up, c_b_gk, c_norm_g, c_w_out, ln_g, ln_b, moe_w_router, moe_b_router, moe_w_gate_up,
    moe_b_gate_up, moe_w_down, moe_b_down, c_2, w_mod_2, b_mod_2, g_mix_pre_2, g_mix_post_2,
    w_qkv_2, w_o_2, w_fg_2, b_fg_2, g_ffn_pre_2, g_ffn_post_2, w_ffn_gate_2, w_ffn_up_2,
    w_conv_2, b_conv_2, w_ffn_down_2,
):
    x = first_block(
        x, rel_bias, a_w_in, a_w_out, b_w_in, b_ln_g, b_ln_b, b_w_s, b_b_s, b_w_out, c_w_in,
        c_w_gk_up, c_b_gk, c_norm_g, c_w_out, ln_g, ln_b, moe_w_router, moe_b_router,
        moe_w_gate_up, moe_b_gate_up, moe_w_down, moe_b_down,
    )
    return second_block(
        x, c_2, w_mod_2, b_mod_2, g_mix_pre_2, g_mix_post_2, w_qkv_2, w_o_2, w_fg_2, b_fg_2,
        g_ffn_pre_2, g_ffn_post_2, w_ffn_gate_2, w_ffn_up_2, w_conv_2, b_conv_2, w_ffn_down_2,
    )


_drawn_inputs = setup_inputs


def setup_inputs(seed=0):
    import zlib

    import numpy as np

    out = dict(_drawn_inputs(seed))
    spreads = {}
    factors = {'moe_b_router': 2.914,
     'moe_b_gate_up': 8.0,
     'moe_b_down': 8.0,
     'g_mix_post_2': 2.725,
     'g_ffn_post_2': 2.899,
     'b_conv_2': 7.984}
    for name, (base, spread) in spreads.items():
        noise = np.random.default_rng([zlib.crc32(name.encode()), seed]).standard_normal(out[name].shape)
        drawn = base * np.exp(spread * noise) if base else spread * noise
        out[name] = __import__('jax').numpy.asarray(drawn.astype(out[name].dtype))
    for name, factor in factors.items():
        out[name] = (out[name] * factor).astype(out[name].dtype)
    return out
```

```python
from contextlib import ExitStack

import numpy as np

import concourse.bass as bass
from concourse import mybir

F32 = mybir.dt.float32
BF16 = mybir.dt.bfloat16
I32 = mybir.dt.int32
ALU = mybir.AluOpType
ACT = mybir.ActivationFunctionType
AX_X = mybir.AxisListType.X

P = 128
T = 256
TT = T // P
D = 1024
KD = D // P
HALF = 512
NG = D // P
HD2 = 64
E = 32
TOPK = 4
CAP = 64
MAX_EXTRA = 16
NIT = E + MAX_EXTRA + 1
F = 2816
FT = F // P
BUCKETS = 32
MAX_DIST = 128
ALPHA = 2.0 ** 0.25
LN_EPS = 1e-5
RMS_EPS = 1e-6
LIMIT = 7.0
SWIGLU_ALPHA = 1.702
NEG = -1e30
MODW = 6 * D
MB = 384
NMB = MODW // MB

R_WO, R_ACC, R_STREAM, R_GTG1, R_BMOD = 0, 8192, 14336, 20480, 22528
SLOT = 2048
GU_SLOTS, DN_SLOTS = 8, 4
SLOTS = GU_SLOTS + DN_SLOTS


def bucket_starts():
    exact = BUCKETS // 2
    n = np.arange(T)
    large = exact + (np.log(np.maximum(n, 1).astype(np.float32) / exact)
                     / np.float32(np.log(MAX_DIST / exact)) * (BUCKETS - exact)).astype(np.int32)
    b = np.where(n < exact, n, np.minimum(large, BUCKETS - 1))
    return [int(np.argmax(b == k)) for k in range(BUCKETS)] + [T]


def block_kernel(nc, a, out):
    with ExitStack() as ctx:
        def sb(name, shape, dt=F32):
            return ctx.enter_context(nc.sbuf_tensor(name, shape, dt))

        def sem(name):
            return ctx.enter_context(nc.semaphore(name))

        ds = bass.ds

        R = sb("big", [P, SLOTS * SLOT])
        G = sb("group_weights", [P, 2, 3 * D])
        XA = sb("x_rows", [P, TT, D])
        YB = sb("y_rows", [P, TT, D])
        XT = sb("x_cols", [P, KD, T])
        OT = sb("att_cols", [P, KD, T])
        SC = sb("scratch", [P, 8192])
        LNC = sb("ln_consts", [P, 2, D])
        GTG0 = sb("gate_gain0", [P, 2, D])
        ident = sb("ident", [P, P])
        ones = sb("ones", [P, P])
        ltri = sb("ltri", [P, P])
        ustr = sb("ustrict", [P, P])
        uinc = sb("uinc", [P, P])
        pick4 = sb("pick4", [P, P])
        identb = sb("identb", [P, P], BF16)
        mask0 = sb("mask_strict", [P, P], BF16)
        mask1 = sb("mask_causal", [P, P], BF16)
        iota64 = sb("iota64", [P, CAP])
        iotaj = sb("iotaj", [P, MAX_EXTRA + 1])
        ccrep = sb("cond_rep", [P, KD, 32])
        vcol = sb("vec_cols", [P, 2, 152])
        modc = sb("mod_cols", [P, 32])
        shc = sb("shift_cols", [P, 2, 16])
        gsc = sb("scale_cols", [P, 2, 16])
        wfg = sb("w_fg", [P, KD, 16])
        st = sb("stats", [P, 48])
        items_i = sb("items", [1, NIT + 1], I32)
        PS = ctx.enter_context(nc.psum_tensor("ps", [P, 8, HALF], F32))

        wo_r = R[:, R_WO:R_WO + 8 * D].rearrange("p (k n) -> p k n", k=KD)
        macc = R[:, R_ACC:R_ACC + MODW]
        mstream = [R[:, R_STREAM + s * KD * MB:R_STREAM + (s + 1) * KD * MB].rearrange("p (k n) -> p k n", k=KD)
                   for s in range(2)]
        gtg = [GTG0[:, :, :], R[:, R_GTG1:R_GTG1 + 2 * D].rearrange("p (a n) -> p a n", a=2)]
        bmod_rows = R[:, R_BMOD:R_BMOD + 2 * D].rearrange("p (a n) -> p a n", a=2)
        slot = [R[:, s * SLOT:(s + 1) * SLOT] for s in range(SLOTS)]

        def part(at, n):
            return SC[:, at:at + n]

        qab = part(0, 512).rearrange("p (h t) -> p h t", h=2)
        kab = part(512, 512).rearrange("p (h t) -> p h t", h=2)
        vT = part(1024, 256)
        V = part(1280, 512).rearrange("p (b s d) -> p b s d", b=2, s=2)
        Ssb = part(1792, 768)
        Pr = part(2560, 768)
        PT = part(3328, 768)
        bias_tiles = part(4096, 2048).rearrange("p (h c) -> p h c", h=8)
        ncum_b = part(4096, 4096).rearrange("p (h t) -> p h t", h=16)
        xeT = part(0, 512).rearrange("p (k s) -> p k s", k=KD)
        xe = part(1024, 512)
        hsb = part(1536, 1024)
        gs_b = part(2560, 512).rearrange("p (f s) -> p f s", s=CAP)
        us_b = part(3072, 512).rearrange("p (f s) -> p f s", s=CAP)
        ss_b = part(3584, 512).rearrange("p (f s) -> p f s", s=CAP)
        actT = part(4096, 512).rearrange("p (f s) -> p f s", s=CAP)
        ysb = part(4608, 1024)
        selx = part(5632, 128).rearrange("p (t s) -> p t s", t=2)
        selg = part(5760, 256).rearrange("p (t s) -> p t s", t=2)
        selT = part(6016, 256)
        bguT = part(6528, NIT * 16).rearrange("p (i f) -> p i f", f=16)
        posx = part(7312, 2 * NIT).rearrange("p (t i) -> p t i", t=2)
        gatx = part(7410, 2 * NIT).rearrange("p (t i) -> p t i", t=2)
        lg = part(7508, 64).rearrange("p (t e) -> p t e", t=2)
        m8 = part(7572, 16).rearrange("p (t e) -> p t e", t=2)
        ex = part(7588, 64).rearrange("p (t e) -> p t e", t=2)
        gtm = part(7652, 64).rearrange("p (t e) -> p t e", t=2)
        eqm = part(7716, 64).rearrange("p (t e) -> p t e", t=2)
        csm = part(7780, 64).rearrange("p (t e) -> p t e", t=2)
        sel = part(7844, 64).rearrange("p (t e) -> p t e", t=2)
        br = part(7908, 32)
        IE = part(7940, NIT)
        Aj = part(7990, 17)
        EXj = part(8010, 17)
        cnt = part(8030, 8)
        itf = part(8040, NIT + 1)
        posT = XT[0:E, 0, :]
        gatT = XT[0:E, 1, :]
        b_gu_rows = OT[0:E, :, :].rearrange("p k t -> p (k t)")
        b_dn_rows = G[0:E, 0, 0:D]
        w_rt = G[:, 1, 0:KD * E].rearrange("p (k e) -> p k e", k=KD)
        cv = [part(256 * s, 256) for s in range(2)]
        sl = [part(512 + 256 * s, 256) for s in range(2)]
        aT = [part(1024 + 256 * s, 256) for s in range(2)]
        junk = [part(2048 + 1024 * s, 1024) for s in range(2)]
        ssq = st[:, 0:2]
        rstd = st[:, 2:4]
        mhalf = st[:, 4:6]
        nmx = st[:, 6:10]
        psum_l = st[:, 10:14]
        mv = st[:, 14:18].rearrange("p (t v) -> p t v", t=2)
        bst = st[:, 18:42].rearrange("p (t h v) -> p t h v", t=2, h=2)
        tmp2 = st[:, 42:44]
        rcp = st[:, 44:48]
        vrow = YB
        bias_src = XT[0:8, 0, 0:32]
        bias_row = OT[0:8, 0:2, :].rearrange("p k t -> p (k t)")[:, 0:384]
        lf = part(3328, 32).rearrange("p (t h) -> p t h", t=2)
        lfb = part(3392, 32).rearrange("p (t h) -> p t h", t=2)
        bfg = part(3424, 16)
        cumT = LNC[:, 0, 0:32].rearrange("p (t h) -> p t h", t=2)
        ncumR = LNC[0:16, 1, 0:256]

        bias_d = nc.dram_tensor("bias_scratch", [8, P, 384], F32).ap()
        cum_d = nc.dram_tensor("cum_scratch", [16, T], F32).ap()

        consts_ready = sem("consts_ready")
        x_loaded = sem("x_loaded")
        small_loaded = sem("small_loaded")
        vrow_loaded = sem("vrow_loaded")
        rel_loaded = sem("rel_loaded")
        bias_row_ready = sem("bias_row_ready")
        bias_written = sem("bias_written")
        bias_loaded = sem("bias_loaded")
        vec_turned = sem("vec_turned")
        vec_ready = sem("vec_ready")
        cond_ready = sem("cond_ready")
        silu_ready = sem("silu_ready")
        cond_turned = sem("cond_turned")
        lnc_loaded = sem("lnc_loaded")
        lnc_used = sem("lnc_used")
        xt_turned = sem("xt_turned")
        xt_act = sem("xt_act")
        xt_dve = sem("xt_dve")
        xn_ready = sem("xn_ready")
        ssq_ready = sem("ssq_ready")
        var_ready = sem("var_ready")
        rstd_ready = sem("rstd_ready")
        att_w = [sem(f"att_w{s}") for s in range(2)]
        qkv_done = sem("qkv_done")
        qv_evac = sem("qv_evac")
        k_evac = sem("k_evac")
        v_turned = sem("v_turned")
        v_evac = sem("v_evac")
        sc_done = sem("sc_done")
        max_ready = sem("max_ready")
        exp_ready = sem("exp_ready")
        prob_ready = sem("prob_ready")
        pt_turned = sem("pt_turned")
        pt_evac = sem("pt_evac")
        pv_done = sem("pv_done")
        o_evac = sem("o_evac")
        lnp_ready = sem("lnp_ready")
        sp_ready = sem("sp_ready")
        r_done = sem("r_done")
        at_ready = sem("at_ready")
        mod_w = [sem(f"mod_w{s}") for s in range(2)]
        mod_mm = sem("mod_mm")
        mod_ev = sem("mod_ev")
        modfin_turned = sem("modfin_turned")
        modfin_red = sem("modfin_red")
        modfin_rows = sem("modfin_rows")
        modfin_done = sem("modfin_done")
        modvec_loaded = sem("modvec_loaded")
        wo_loaded = sem("wo_loaded")
        y_done = sem("y_done")
        y_read = sem("y_read")
        x_updated = sem("x_updated")
        rt_w = sem("rt_w")
        b_gu_loaded = sem("b_gu_loaded")
        rt_pe = sem("rt_pe")
        rt_dve = sem("rt_dve")
        rt_act = sem("rt_act")
        items_ready = sem("items_ready")
        ew = [sem(f"expert_w{s}") for s in range(SLOTS)]
        ew_used = sem("expert_w_used")
        selx_ready = sem("selx_ready")
        selg_ready = sem("selg_ready")
        gat_mm = sem("gat_mm")
        xe_ev = sem("xe_ev")
        xe_turned = sem("xe_turned")
        xeT_ready = sem("xeT_ready")
        selT_turned = sem("selT_turned")
        selT_ev = sem("selT_ev")
        h_ev = sem("h_ev")
        h_turned = sem("h_turned")
        g_ready = sem("g_ready")
        sg_ready = sem("sg_ready")
        act_ready = sem("act_ready")
        y_ev = sem("y_ev")
        sc_mm = sem("sc_mm")
        acc_done = sem("acc_done")
        zero_ready = sem("zero_ready")
        ffn_w = [sem(f"ffn_w{s}") for s in range(2)]
        ffn_dw = [sem(f"ffn_dw{s}") for s in range(2)]
        fgu_done = sem("fgu_done")
        cv_ready = sem("cv_ready")
        sl_ready = sem("sl_ready")
        fact_ready = sem("fact_ready")
        fdn_done = sem("fdn_done")
        flog_done = sem("flog_done")
        flog_dve = sem("flog_dve")
        flog_act = sem("flog_act")
        cum_done = sem("cum_done")
        ncum_ready = sem("ncum_ready")
        ncum_written = sem("ncum_written")
        ncum_loaded = sem("ncum_loaded")
        out_stored = sem("out_stored")

        def bank(b, n=HALF, rows=slice(0, P), at=0):
            return PS[rows, b, at:at + n]

        def banks(b, n):
            return PS[:, :, :].rearrange("p b n -> p (b n)")[:, b * HALF:b * HALF + n]

        w_qkv = [a["a_w_in"][0], a["w_qkv_2"][0], a["w_qkv_2"][1]]
        w_out = [a["a_w_out"][0], a["w_o_2"][0], a["w_o_2"][1]]
        rows_of = lambda ap: ap.rearrange("(k p) n -> p k n", p=P)
        x_rows = a["x"][0].rearrange("(t p) d -> p t d", p=P)

        def bcast(ap):
            return ap.partition_broadcast(P)

        blk = ctx.enter_context(nc.Block())

        @blk.sync
        def _(sp):
            def att_weights(p, g, half, s):
                src = rows_of(w_qkv[p]).rearrange("p k (c n) -> p k c n", c=3)
                for c in range(3):
                    sp.dma_start(G[:, s, c * D:(c + 1) * D].rearrange("p (k n) -> p k n", k=KD),
                                 src[:, :, c, ds(g * P, P)]).then_inc(att_w[s], 16)

            def mod_block(p, m, s):
                sp.dma_start(mstream[s], rows_of(a["w_mod_2"][p])[:, :, ds(m * MB, MB)]).then_inc(mod_w[s], 16)

            def attention_loads(p):
                att_weights(p, 0, 0, 0)
                if p == 2:
                    sp.wait_ge(fgu_done, FT)
                    sp.wait_ge(fdn_done, FT)
                att_weights(p, 1, 0, 1)
                if p == 1:
                    sp.wait_ge(ew_used, n_items * SLOTS)
                if p < 2:
                    mod_block(p, 0, 0)
                    mod_block(p, 1, 1)
                    for m in (2, 3):
                        sp.wait_ge(mod_mm, NMB * p + m - 1)
                        mod_block(p, m, m % 2)
                if p > 0:
                    if p == 2:
                        sp.wait_ge(y_done, 2)
                    sp.dma_start(wo_r, rows_of(w_out[p])).then_inc(wo_loaded, 16)
                with sp.Fori(1, NG // 2) as i:
                    for s in range(2):
                        sp.wait_ge(qkv_done, i * 2 + (NG * p + s - 1))
                        att_weights(p, i * 2 + s, i, s)
                        if p < 2:
                            for r in range(2):
                                sp.wait_ge(mod_mm, i * 4 + (NMB * p + 2 * s + r - 1))
                                mod_block(p, i * 4 + (2 * s + r), r)
                if p == 0:
                    sp.dma_start(wo_r, rows_of(w_out[p])).then_inc(wo_loaded, 16)

            def ffn_weights(L, j, s):
                for c, name in enumerate(("w_ffn_gate_2", "w_ffn_up_2")):
                    sp.dma_start(G[:, s, c * D:(c + 1) * D].rearrange("p (k n) -> p k n", k=KD),
                                 rows_of(a[name][L])[:, :, ds(j * P, P)]).then_inc(ffn_w[s], 16)

            def ffn_down(L, j, s):
                sp.dma_start(G[:, s, 2 * D:3 * D], a["w_ffn_down_2"][L][ds(j * P, P), :]).then_inc(ffn_dw[s], 16)

            def ffn_loads(L):
                for s in range(2):
                    sp.wait_ge(qkv_done, NG * (L + 1) + NG - 1 + s)
                    ffn_weights(L, s, s)
                    ffn_down(L, s, s)
                with sp.Fori(1, FT // 2) as i:
                    for s in range(2):
                        sp.wait_ge(fgu_done, i * 2 + (FT * L + s - 1))
                        ffn_weights(L, i * 2 + s, s)
                        sp.wait_ge(fdn_done, i * 2 + (FT * L + s - 1))
                        ffn_down(L, i * 2 + s, s)

            def expert_slot(e, s):
                if s < GU_SLOTS:
                    src = a["moe_w_gate_up"][0, ds(e, 1)].rearrange("a (k p) n -> p (a k) n", p=P)[:, s, :]
                    sp.dma_start(slot[s], src).then_inc(ew[s], 16)
                else:
                    d = s - GU_SLOTS
                    src = a["moe_w_down"][0, ds(e, 1)].rearrange("a (k p) n -> p (a k) n", p=P)[:, 2 * d:2 * d + 2, :]
                    sp.dma_start(slot[s].rearrange("p (k n) -> p k n", k=2), src).then_inc(ew[s], 16)

            sp.dma_start(XA[:, :, :], x_rows).then_inc(x_loaded, 16)
            attention_loads(0)
            sp.wait_ge(qkv_done, NG)
            sp.dma_start(w_rt, rows_of(a["moe_w_router"][0])).then_inc(rt_w, 16)
            sp.dma_start(b_dn_rows, a["moe_b_down"][0]).then_inc(rt_w, 16)
            sp.wait_ge(modfin_done, 1)
            for s in range(4, SLOTS):
                expert_slot(0, s)
            sp.wait_ge(y_done, 1)
            sp.dma_start(b_gu_rows, a["moe_b_gate_up"][0]).then_inc(b_gu_loaded, 16)
            for s in range(4):
                expert_slot(0, s)
            sp.wait_ge(items_ready, 1)
            n_items = sp.value_load(items_i[0:1, NIT:NIT + 1], min_val=E, max_val=E + MAX_EXTRA)
            with sp.Fori(1, n_items) as i:
                e = sp.value_load(items_i[0:1, ds(i, 1)], min_val=0, max_val=E - 1)
                for s in range(SLOTS):
                    sp.wait_ge(ew_used, i * SLOTS + (s + 1 - SLOTS))
                    expert_slot(e, s)
            attention_loads(1)
            ffn_loads(0)
            sp.wait_ge(fgu_done, FT - 1)
            sp.wait_ge(fdn_done, FT - 1)
            attention_loads(2)
            ffn_loads(1)
            sp.wait_ge(x_updated, 5)
            sp.dma_start(out[0].rearrange("(t p) d -> p t d", p=P), XA[:, :, :]).then_inc(out_stored, 16)
            sp.wait_ge(out_stored, 16)

        @blk.gpsimd
        def _(pool):
            def triangle(t, inside, outside, pattern, mult, op):
                pool.memset(t[:, :], inside)
                pool.drain()
                pool.affine_select(out=t[:, :], in_=t[:, :], compare_op=op, fill=outside, base=0,
                                   pattern=[[pattern, P]], channel_multiplier=mult)

            triangle(ident, 0.0, 1.0, -1, 1, ALU.not_equal)
            triangle(ltri, 1.0, 0.0, -1, 1, ALU.is_ge)
            triangle(ustr, 1.0, 0.0, 1, -1, ALU.is_gt)
            triangle(uinc, 1.0, 0.0, 1, -1, ALU.is_ge)
            triangle(identb, 0.0, 1.0, -1, 1, ALU.not_equal)
            triangle(mask0, 0.0, -NEG, 1, -1, ALU.is_gt)
            triangle(mask1, 0.0, NEG, -1, 1, ALU.is_ge)
            pool.memset(ones[:, :], 1.0)
            pool.memset(pick4[:, :], 0.0)
            pool.drain()
            for r in range(4):
                pool.memset(pick4[32 * r:32 * r + 1, :], 1.0)
                pool.drain()
            pool.memset(mhalf, -0.5)
            pool.iota(iota64[:, :], [[1, CAP]], 0, 0, allow_small_or_imprecise_dtypes=True)
            pool.iota(iotaj[:, :], [[1, MAX_EXTRA + 1]], 0, 0, allow_small_or_imprecise_dtypes=True)
            pool.drain()
            pool.memset(tmp2, 0.0).then_inc(consts_ready, 1)

            def to_rstd(source, scale, eps):
                pool.tensor_scalar(tmp2, source, scale, eps, ALU.mult, ALU.add)
                pool.drain()
                pool.tensor_tensor(rstd, tmp2, mhalf, ALU.pow).then_inc(rstd_ready, 1)

            for k in range(2):
                pool.wait_ge(var_ready, k + 1)
                to_rstd(mv[:, :, 1], 1.0, LN_EPS)
            for k in range(8):
                pool.wait_ge(ssq_ready, k + 1)
                to_rstd(ssq, 1.0 / D, RMS_EPS)

        @blk.tensor
        def _(pe):
            mm = pe.matmul

            def turn_rows(k):
                src = XA if k == 0 else YB
                for t in range(TT):
                    if k == 0:
                        pe.wait_ge(x_loaded, 16)
                    else:
                        pe.wait_ge(xn_ready, TT * (k - 1) + t + 1)
                    for c in range(KD):
                        last = pe.transpose(PS[:, c // 2, (c % 2) * T + t * P:(c % 2) * T + (t + 1) * P],
                                            src[:, t, c * P:(c + 1) * P], ident[:, :])
                        if t == TT - 1 and c % 2:
                            last.then_inc(xt_turned, 1)

            def qkv(p, g, half, s):
                pe.wait_ge(att_w[s], half * 48 + (48 * (NG // 2) * p + 48))
                if not (p == 0 and isinstance(g, int) and g == 0):
                    pe.wait_ge(v_evac, g + NG * p)
                w = G[:, s, :].rearrange("p (c k n) -> p c k n", c=3, k=KD)
                for c, (b, at) in enumerate(((0, 0), (1, 0), (0, T))):
                    dst = bank(b, T, at=at)
                    for k in range(KD):
                        last = mm(dst, w[:, c, k, :], XT[:, k, :], start=(k == 0), stop=(k == KD - 1))
                last.then_inc(qkv_done, 1)

            def turn_v(p, g, s):
                pe.wait_ge(qv_evac, g + (NG * p + 1))
                pe.wait_ge(k_evac, g + (NG * p + 1))
                for t in range(TT):
                    last = pe.transpose(PS[:, 1, T + t * P:T + (t + 1) * P], vT[:, t * P:(t + 1) * P], ident[:, :])
                last.then_inc(v_turned, 1)

            def scores(p, g):
                if p == 0:
                    mm(bank(2, T), qab[:, 0, P:T], kab[:, 0, :], start=True, stop=True)
                    last = mm(bank(2, P, at=T), qab[:, 0, 0:P], kab[:, 0, 0:P], start=True, stop=True)
                elif p == 1:
                    mm(bank(2), kab[:, 0, 0:P], qab[:, :, :], start=True, stop=False, skip_group_check=True)
                    mm(PS[:, 2, :].rearrange("p (h t) -> p h t", h=2)[:, :, 0:P], identb[:, :],
                       mask0[:, :].unsqueeze(1).to_broadcast([P, 2, P]), start=False, stop=True, skip_group_check=True)
                    mm(bank(3, T), kab[:, 0, P:T], qab[:, :, P:T], start=True, stop=False, skip_group_check=True)
                    last = mm(bank(3, T).rearrange("p (h t) -> p h t", h=2), identb[:, :],
                              mask0[:, :].unsqueeze(1).to_broadcast([P, 2, P]), start=False, stop=True,
                              skip_group_check=True)
                else:
                    mm(bank(2), qab[:, 0, P:T], kab[:, :, :], start=True, stop=False, skip_group_check=True)
                    mm(PS[:, 2, :].rearrange("p (h t) -> p h t", h=2)[:, :, P:T], identb[:, :],
                       mask1[:, :].unsqueeze(1).to_broadcast([P, 2, P]), start=False, stop=True, skip_group_check=True)
                    mm(bank(3, T), qab[:, 0, 0:P], kab[:, :, 0:P], start=True, stop=False, skip_group_check=True)
                    last = mm(bank(3, T).rearrange("p (h t) -> p h t", h=2), identb[:, :],
                              mask1[:, :].unsqueeze(1).to_broadcast([P, 2, P]), start=False, stop=True,
                              skip_group_check=True)
                last.then_inc(sc_done, 1)

            def turn_probs(p, g):
                pe.wait_ge(prob_ready, g + (NG * (p // 2) + 1))
                if p == 0:
                    pe.transpose(bank(4, P, at=0), Pr[:, T:T + P], ident[:, :])
                    pe.transpose(bank(4, P, at=P), Pr[:, 0:P], ident[:, :])
                    last = pe.transpose(bank(4, P, at=T), Pr[:, P:T], ident[:, :])
                else:
                    for h in range(2):
                        pe.transpose(bank(4, P, at=h * T), Pr[:, 512 + h * P:512 + (h + 1) * P], ident[:, :])
                        pe.transpose(bank(4, P, at=h * T + P), Pr[:, h * T:h * T + P], ident[:, :])
                        last = pe.transpose(bank(5, P, at=h * P), Pr[:, h * T + P:(h + 1) * T], ident[:, :])
                last.then_inc(pt_turned, 1)

            def decay_sums(g):
                pe.wait_ge(sp_ready, g + 1)
                mm(bank(2), ltri[:, :], Pr[:, 0:512], start=False, stop=False, skip_group_check=True)
                mm(PS[:, 2, :].rearrange("p (h t) -> p h t", h=2)[:, :, P:T], ones[:, :],
                   Pr[:, 512:768].rearrange("p (h t) -> p h t", h=2), start=False, stop=True, skip_group_check=True)
                mm(bank(3, T), ltri[:, :], Pr[:, 512:768], start=False, stop=True,
                   skip_group_check=True).then_inc(r_done, 1)

            def values(p, g, s):
                if p == 1:
                    pe.wait_ge(at_ready, g + 1)
                else:
                    pe.wait_ge(pt_evac, g + (NG * (p // 2) + 1))
                pe.wait_ge(v_evac, g + (NG * p + 1))
                if not (p == 0 and isinstance(g, int) and g == 0):
                    pe.wait_ge(o_evac, g + NG * p)
                if p == 0:
                    mm(bank(6, T), V[:, s, 0, :], PT[:, 0:T], start=True, stop=False, skip_group_check=True)
                    last = mm(bank(6, P, at=P), V[:, s, 1, :], PT[:, T:T + P], start=False, stop=True,
                              skip_group_check=True)
                else:
                    for h in range(2):
                        r = slice(HD2 * h, HD2 * (h + 1))
                        mm(bank(6, T, r), V[:, s, 0, r], PT[:, h * T:(h + 1) * T], start=True, stop=False,
                           skip_group_check=True)
                        last = mm(bank(6, P, r, at=P), V[:, s, 1, r], PT[:, 512 + h * P:512 + (h + 1) * P],
                                  start=False, stop=True, skip_group_check=True)
                last.then_inc(pv_done, 1)

            def modulation(p, m, mh, s):
                pe.wait_ge(mod_w[s], mh * 16 + (16 * (NMB // 2) * p + 16))
                if m is not None:
                    pe.wait_ge(mod_ev, m + (NMB * p - 1))
                for k in range(KD):
                    r = 32 * (k % 4)
                    last = mm(PS[r:r + 32, 5 + 2 * s, 0:MB], ccrep[:, k, :], mstream[s][:, k, :],
                              start=(k < 4), stop=(k >= 4))
                last.then_inc(mod_mm, 1)

            def step(p, g, half, s, first, head):
                qkv(p, g, half, s)
                if not first:
                    if p == 1:
                        decay_sums(g - 1)
                    else:
                        turn_probs(p, g - 1)
                turn_v(p, g, s)
                if p < 2:
                    modulation(p, None if (p == 0 and first) else g * 2, g, 0)
                if p == 1 and not first:
                    values(p, g - 1, 1 - s)
                scores(p, g)
                if p != 1 and not first:
                    values(p, g - 1, 1 - s)
                if p < 2:
                    modulation(p, None if (p == 0 and first) else g * 2 + 1, g, 1)

            def attention(p):
                step(p, 0, 0, 0, True, True)
                step(p, 1, 0, 1, False, True)
                with pe.Fori(1, NG // 2) as i:
                    for s in range(2):
                        step(p, i * 2 + s, i, s, False, False)
                if p == 1:
                    decay_sums(NG - 1)
                else:
                    turn_probs(p, NG - 1)
                values(p, NG - 1, 1)
                pe.wait_ge(o_evac, NG * (p + 1))

            def finish_modulation(p):
                pe.wait_ge(mod_ev, NMB * (p + 1))
                pe.wait_ge(modvec_loaded, 48 * (p + 1))
                chunks = list(range(16)) + list(range(24, 40))
                for n, c in enumerate(chunks):
                    last = pe.transpose(bank(n // 4, P, at=(n % 4) * P), macc[:, c * P:(c + 1) * P], ident[:, :])
                last.then_inc(modfin_turned, 1)
                pe.wait_ge(modfin_red, p + 1)
                for n, c in enumerate((4, 5, 10, 11)):
                    last = mm(bank(n), pick4[:, :], macc[:, c * HALF:(c + 1) * HALF], start=True, stop=True)
                last.then_inc(modfin_rows, 1)
                pe.wait_ge(modfin_done, p + 1)

            def project_out(p):
                pe.wait_ge(wo_loaded, 16 * (p + 1))
                for t in range(TT):
                    for k in range(KD):
                        for n in range(2):
                            last = mm(bank(2 * t + n), OT[:, k, t * P:(t + 1) * P], wo_r[:, k, n * HALF:(n + 1) * HALF],
                                      start=(k == 0), stop=(k == KD - 1))
                last.then_inc(y_done, 1)

            def wait_columns(k):
                pe.wait_ge(xt_act, k + 1)
                pe.wait_ge(xt_dve, k + 1)

            def feed_forward(L):
                def gate_up(j, jh, s):
                    pe.wait_ge(ffn_w[s], jh * 32 + (32 * (FT // 2) * L + 32))
                    if not (L == 0 and isinstance(j, int) and j < 2):
                        pe.wait_ge(fact_ready, j + (FT * L - 1))
                    w = G[:, s, 0:2 * D].rearrange("p (c k n) -> p c k n", c=2, k=KD)
                    for c in range(2):
                        for k in range(KD):
                            last = mm(bank(4 + s, T, at=c * T), w[:, c, k, :], XT[:, k, :],
                                      start=(k == 0), stop=(k == KD - 1))
                    last.then_inc(fgu_done, 1)

                def down(j, jh, s, first=False, end=False):
                    pe.wait_ge(ffn_dw[s], jh * 16 + (16 * (FT // 2) * L + 16))
                    pe.wait_ge(fact_ready, j + (FT * L + 1))
                    for t in range(TT):
                        for n in range(2):
                            last = mm(bank(2 * t + n), aT[s][:, t * P:(t + 1) * P],
                                      G[:, s, 2 * D + n * HALF:2 * D + (n + 1) * HALF],
                                      start=first, stop=end, skip_group_check=True)
                    last.then_inc(fdn_done, 1)

                gate_up(0, 0, 0)
                gate_up(1, 0, 1)
                down(0, 0, 0, first=True)
                with pe.Fori(1, FT // 2) as i:
                    gate_up(i * 2, i, 0)
                    down(i * 2 - 1, i - 1, 1)
                    gate_up(i * 2 + 1, i, 1)
                    down(i * 2, i, 0)
                down(FT - 1, FT // 2 - 1, 1, end=True)

            def routing():
                pe.wait_ge(rt_w, 32)
                for t in range(TT):
                    for k in range(KD):
                        last = mm(bank(4, E, at=t * E), XT[:, k, t * P:(t + 1) * P], w_rt[:, k, :],
                                  start=(k == 0), stop=(k == KD - 1))
                last.then_inc(rt_pe, 1)
                pe.wait_ge(rt_dve, 1)
                mm(bank(5, E), ustr[:, :], sel[:, 0, :], start=True, stop=True)
                mm(bank(5, E, at=E), ones[:, :], sel[:, 0, :], start=True, stop=False)
                mm(bank(5, E, at=E), ustr[:, :], sel[:, 1, :], start=False, stop=True)
                mm(bank(6, 1, slice(0, E)), sel[:, 0, :], ones[:, 0:1], start=True, stop=False)
                mm(bank(6, 1, slice(0, E)), sel[:, 1, :], ones[:, 0:1], start=False,
                   stop=True).then_inc(rt_pe, 1)
                pe.wait_ge(rt_dve, 2)
                mm(bank(7, 1, slice(0, E)), uinc[0:E, 0:E], cnt[0:E, 1:2], start=True, stop=True)
                for t in range(TT):
                    pe.transpose(bank(4, P, slice(0, E), at=t * P), posx[:, t, 0:E], ident[:, :])
                for t in range(TT):
                    last = pe.transpose(bank(4, P, slice(0, E), at=T + t * P), gatx[:, t, 0:E], ident[:, :])
                last.then_inc(rt_pe, 1)
                pe.wait_ge(rt_dve, 3)
                mm(bank(5, 17), ones[0:E, :], Aj[0:E, :], start=True, stop=True)
                mm(bank(5, 17, at=32), ones[0:E, :], EXj[0:E, :], start=True, stop=True)
                mm(bank(5, 1, at=64), ones[0:E, :], cnt[0:E, 1:2], start=True, stop=True)
                for t in range(TT):
                    mm(bank(6, 17, at=t * 17), posT[:, t * P:(t + 1) * P], IE[0:E, E:NIT], start=True, stop=True)
                    mm(bank(6, 17, at=64 + t * 17), gatT[:, t * P:(t + 1) * P], IE[0:E, E:NIT], start=True, stop=True)
                pe.wait_ge(b_gu_loaded, 16)
                for f in range(16):
                    mm(bank(f // 8, NIT, at=(f % 8) * NIT), b_gu_rows[:, f * P:(f + 1) * P], IE[0:E, 0:NIT],
                       start=True, stop=True)
                for t in range(TT):
                    for n in range(2):
                        last = mm(bank([2, 3, 4, 7][2 * t + n]), gatT[:, t * P:(t + 1) * P],
                                  b_dn_rows[:, n * HALF:(n + 1) * HALF], start=True, stop=True)
                last.then_inc(rt_pe, 1)
                pe.wait_ge(rt_dve, 4)

            def gather(j, first=False):
                pe.wait_ge(selx_ready, j + 1)
                if not first:
                    pe.wait_ge(selT_ev, j)
                for t in range(TT):
                    for n in range(2):
                        last = mm(bank(6, HALF, slice(CAP * n, CAP * (n + 1))), selx[:, t, :],
                                  XA[:, t, n * HALF:(n + 1) * HALF], start=(t == 0), stop=(t == 1))
                last.then_inc(gat_mm, 1)

            def turn_gathered(j):
                pe.wait_ge(xe_ev, j + 1)
                for c in range(4):
                    last = pe.transpose(bank(7, P, at=c * P), xe[:, c * P:(c + 1) * P], ident[:, :])
                last.then_inc(xe_turned, 1)

            def scatter(i):
                pe.wait_ge(y_ev, i + 1)
                pe.wait_ge(selT_ev, i + 1)
                for q, b in enumerate((4, 5, 0, 1)):
                    t, n = q // 2, q % 2
                    mm(bank(b), selT[:, t * P:(t + 1) * P], ysb[:, n * HALF:(n + 1) * HALF],
                       start=True, stop=True).then_inc(sc_mm, 1)

            def experts():
                pe.wait_ge(items_ready, 1)
                n_items = pe.value_load(items_i[0:1, NIT:NIT + 1], min_val=E, max_val=E + MAX_EXTRA)
                pe.wait_ge(zero_ready, 1)
                gather(0, first=True)
                turn_gathered(0)
                with pe.Fori(0, n_items) as i:
                    pe.wait_ge(xeT_ready, i + 1)
                    pe.wait_ge(acc_done, i * 4 + 1)
                    for k in range(KD):
                        pe.wait_ge(ew[k], i * 16 + 16)
                        for n in range(2):
                            for c in range(2):
                                last = mm(bank(n, HALF, slice(CAP * c, CAP * (c + 1))), xeT[:, k, :],
                                          slot[k][:, c * D + n * HALF:c * D + (n + 1) * HALF],
                                          start=(k == 0), stop=(k == KD - 1))
                        last.then_inc(ew_used, 1)
                    gather(i + 1)
                    pe.wait_ge(h_ev, i + 1)
                    for f in range(8):
                        last = pe.transpose(bank(2 + f // 4, P, at=(f % 4) * P), hsb[:, f * P:(f + 1) * P], ident[:, :])
                    last.then_inc(h_turned, 1)
                    scatter(i)
                    turn_gathered(i + 1)
                    pe.wait_ge(selg_ready, i + 1)
                    for t in range(TT):
                        last = pe.transpose(bank(6, P, at=t * P), selg[:, t, :], ident[:, :])
                    last.then_inc(selT_turned, 1)
                    pe.wait_ge(act_ready, i + 1)
                    pe.wait_ge(acc_done, i * 4 + 3)
                    for d in range(DN_SLOTS):
                        pe.wait_ge(ew[GU_SLOTS + d], i * 16 + 16)
                        for n in range(2):
                            for c in range(2):
                                last = mm(bank(4 + n, HALF, slice(CAP * c, CAP * (c + 1))), actT[:, 2 * d + c, :],
                                          slot[GU_SLOTS + d][:, c * D + n * HALF:c * D + (n + 1) * HALF],
                                          start=(d == 0), stop=(d == DN_SLOTS - 1))
                        last.then_inc(ew_used, 1)
                pe.wait_ge(acc_done, n_items * 4 + 1)
                scatter(n_items)

            def forget_gates():
                for t in range(TT):
                    for k in range(KD):
                        last = mm(bank(4, 16, at=t * 16), XT[:, k, t * P:(t + 1) * P], wfg[:, k, :],
                                  start=(k == 0), stop=(k == KD - 1))
                last.then_inc(flog_done, 1)
                pe.wait_ge(flog_dve, 2)
                mm(bank(5, 16), uinc[:, :], lf[:, 0, :], start=True, stop=True)
                mm(bank(5, 16, at=16), ones[:, :], lf[:, 0, :], start=True, stop=False)
                mm(bank(5, 16, at=16), uinc[:, :], lf[:, 1, :], start=False, stop=True)
                mm(bank(7, P, slice(0, 16)), lf[:, 0, :], uinc[:, :], start=True, stop=True)
                mm(bank(7, P, slice(0, 16), at=P), lf[:, 0, :], ones[:, :], start=True, stop=False)
                mm(bank(7, P, slice(0, 16), at=P), lf[:, 1, :], uinc[:, :], start=False,
                   stop=True).then_inc(cum_done, 1)

            pe.wait_ge(consts_ready, 1)
            pe.wait_ge(vrow_loaded, 16 * 11)
            for L in range(2):
                pe.transpose(bank(4, 64, at=L * 256), vrow[0:64, L, 0:P], ident[0:64, 0:64])
                last = pe.transpose(bank(4, 88, at=L * 256 + 64), vrow[0:88, L, P:2 * P], ident[0:88, 0:88])
            last.then_inc(vec_turned, 1)
            pe.wait_ge(silu_ready, 1)
            pe.transpose(bank(6, 8), vrow[0:8, 0, 2 * P:3 * P], ident[0:8, 0:8]).then_inc(cond_turned, 1)
            turn_rows(0)
            wait_columns(0)
            pe.wait_ge(cond_ready, 1)
            attention(0)
            finish_modulation(0)
            project_out(0)
            turn_rows(1)
            wait_columns(1)
            routing()
            experts()
            for L in range(2):
                turn_rows(2 + 2 * L)
                wait_columns(2 + 2 * L)
                if L == 1:
                    forget_gates()
                attention(1 + L)
                if L == 0:
                    finish_modulation(1)
                project_out(1 + L)
                turn_rows(3 + 2 * L)
                wait_columns(3 + 2 * L)
                feed_forward(L)

        @blk.scalar
        def _(act):
            fn = act.activation
            act.dma_start(bias_src, a["rel_bias"].rearrange("b h -> h b"), allow_slow_non_contiguous=True)\
               .then_inc(rel_loaded, 16)
            for L in range(2):
                for lo, n, name in ((0, 48, "b_mod_2"), (48, 8, "g_mix_pre_2"), (56, 8, "g_ffn_pre_2")):
                    act.dma_start(vrow[lo:lo + n, L, 0:P], a[name][L].rearrange("(r n) -> r n", n=P))\
                       .then_inc(vrow_loaded, 16)
                act.dma_start(vrow[0:66, L, P:2 * P], a["w_conv_2"][L].rearrange("w (r n) -> (w r) n", n=P))\
                   .then_inc(vrow_loaded, 16)
                act.dma_start(vrow[66:88, L, P:2 * P], a["b_conv_2"][L].rearrange("(r n) -> r n", n=P))\
                   .then_inc(vrow_loaded, 16)
            act.dma_start(vrow[0:8, 0, 2 * P:3 * P], a["c_2"][0].rearrange("(r n) -> r n", n=P))\
               .then_inc(vrow_loaded, 16)
            act.dma_start(wfg[:, :, :], rows_of(a["w_fg_2"][0])).then_inc(small_loaded, 16)
            act.dma_start(LNC[:, 0, :], bcast(a["ln_g"][0, 0])).then_inc(lnc_loaded, 16)
            act.dma_start(LNC[:, 1, :], bcast(a["ln_b"][0, 0])).then_inc(lnc_loaded, 16)

            def modulation_rows(p):
                act.dma_start(bmod_rows[:, :, :], bcast(a["b_mod_2"][p].rearrange("(c n) -> c n", n=D)[2:6:3, :]))\
                   .then_inc(modvec_loaded, 16)
                act.dma_start(gtg[p][:, 0, :], bcast(a["g_mix_post_2"][p])).then_inc(modvec_loaded, 16)
                act.dma_start(gtg[p][:, 1, :], bcast(a["g_ffn_post_2"][p])).then_inc(modvec_loaded, 16)

            modulation_rows(0)
            act.wait_ge(vrow_loaded, 16 * 11)
            fn(vrow[0:8, 0, 2 * P:3 * P], vrow[0:8, 0, 2 * P:3 * P], ACT.Silu).then_inc(silu_ready, 1)
            act.wait_ge(bias_row_ready, 1)
            act.dma_start(bias_d, bias_row.unsqueeze(1).to_broadcast([8, P, 384])).then_inc(bias_written, 16)
            act.wait_ge(bias_written, 16)
            act.dma_start(bias_tiles, bass.AP(tensor=bias_d.tensor, offset=P - 1, ap=[[383, P], [P * 384, 8], [1, T]]))\
               .then_inc(bias_loaded, 16)

            def columns(k, scale=None, shift=None):
                for c in (0, 1, 4, 5):
                    act.wait_ge(xt_turned, 4 * k + c // 2 + 1)
                    src = PS[:, c // 2, (c % 2) * T:(c % 2 + 1) * T]
                    if scale is None:
                        last = fn(XT[:, c, :], src, ACT.Copy)
                    else:
                        last = fn(XT[:, c, :], src, ACT.Identity, bias=shift[:, c:c + 1], scale=scale[:, c:c + 1])
                last.then_inc(xt_act, 1)

            def evacuate(p, g):
                act.wait_ge(qkv_done, g + (NG * p + 1))
                if p == 1:
                    for h in range(2):
                        r = slice(HD2 * h, HD2 * (h + 1))
                        fn(qab[r, h, :], PS[r, 0, 0:T], ACT.Copy, scale=HD2 ** -0.5)
                else:
                    fn(qab[:, 0, :], PS[:, 0, 0:T], ACT.Copy, scale=(P if p == 0 else HD2) ** -0.5)
                fn(vT, PS[:, 0, T:2 * T], ACT.Copy).then_inc(qv_evac, 1)

            def softplus_tail(g):
                act.wait_ge(sc_done, g + (NG + 1))
                fn(Ssb, banks(2, 768), ACT.Abs)
                act.drain()
                fn(Ssb, Ssb, ACT.Exp, scale=-1.0)
                act.drain()
                fn(Ssb, Ssb, ACT.Ln, bias=1.0).then_inc(lnp_ready, 1)

            def weights_from_sums(g):
                act.wait_ge(r_done, g + 1)
                fn(PT, banks(2, 768), ACT.Exp, scale=-1.0).then_inc(at_ready, 1)

            def softmax_exp(p, g):
                act.wait_ge(max_ready, g + (NG * (p // 2) + 1))
                segs = ((0, T), (T, P)) if p == 0 else ((0, T), (T, T), (512, P), (640, P))
                for n, (lo, w) in enumerate(segs):
                    last = fn(Pr[:, lo:lo + w], Ssb[:, lo:lo + w], ACT.Exp, bias=nmx[:, n:n + 1],
                              accum_out=psum_l[:, n:n + 1])
                last.then_inc(exp_ready, 1)

            def turned_probs(p, g):
                act.wait_ge(pt_turned, g + (NG * (p // 2) + 1))
                w = 384 if p == 0 else 768
                fn(PT[:, 0:w], banks(4, w), ACT.Copy).then_inc(pt_evac, 1)

            def mod_part(p, m, s):
                act.wait_ge(mod_mm, m + (NMB * p + 1))
                fn(macc[:, ds(m * MB, MB)], bank(5 + 2 * s, MB), ACT.Copy).then_inc(mod_ev, 1)

            def step(p, g, first):
                evacuate(p, g)
                if not first:
                    if p == 1:
                        weights_from_sums(g - 1)
                    else:
                        turned_probs(p, g - 1)
                if p < 2:
                    mod_part(p, g * 2, 0)
                if p == 1:
                    softplus_tail(g)
                else:
                    softmax_exp(p, g)
                if p < 2:
                    mod_part(p, g * 2 + 1, 1)

            def attention(p):
                step(p, 0, True)
                with act.Fori(1, NG) as g:
                    step(p, g, False)
                if p == 1:
                    weights_from_sums(NG - 1)
                else:
                    turned_probs(p, NG - 1)

            def squares(src, k):
                for t in range(TT):
                    last = fn(junk[t], src(t), ACT.Square, accum_out=ssq[:, t:t + 1])
                last.then_inc(ssq_ready, 1)

            columns(0)
            attention(0)
            columns(1)
            act.dma_start(br, bcast(a["moe_b_router"][0])).then_inc(small_loaded, 16)
            act.wait_ge(rt_dve, 1)
            for t in range(TT):
                last = fn(ex[:, t, :], lg[:, t, :], ACT.Exp, bias=nmx[:, t:t + 1])
            last.then_inc(rt_act, 1)
            act.wait_ge(lnc_used, 1)
            act.dma_start(LNC[:, 0, :], bcast(a["ln_g"][0, 1])).then_inc(lnc_loaded, 16)
            act.dma_start(LNC[:, 1, :], bcast(a["ln_b"][0, 1])).then_inc(lnc_loaded, 16)
            act.wait_ge(items_ready, 1)
            n_items = act.value_load(items_i[0:1, NIT:NIT + 1], min_val=E, max_val=E + MAX_EXTRA)

            def gathered(j):
                act.wait_ge(gat_mm, j + 1)
                fn(xe, bank(6), ACT.Copy).then_inc(xe_ev, 1)

            act.wait_ge(zero_ready, 1)
            fn(psum_l[:, 0:1], ident[:, 0:1], ACT.Copy).then_inc(y_ev, 1)
            fn(psum_l[:, 1:2], ident[:, 0:1], ACT.Copy).then_inc(selT_ev, 1)
            gathered(0)
            with act.Fori(0, n_items) as i:
                act.wait_ge(ew_used, i * SLOTS + GU_SLOTS)
                fn(hsb, banks(0, D), ACT.Copy).then_inc(h_ev, 1)
                gathered(i + 1)
                act.wait_ge(g_ready, i + 1)
                fn(ss_b, gs_b, ACT.Sigmoid, scale=SWIGLU_ALPHA).then_inc(sg_ready, 1)
                act.wait_ge(selT_turned, i + 1)
                fn(selT, bank(6, T), ACT.Copy).then_inc(selT_ev, 1)
                act.wait_ge(ew_used, i * SLOTS + SLOTS)
                fn(ysb, banks(4, D), ACT.Copy).then_inc(y_ev, 1)
            for L in range(2):
                act.wait_ge(x_updated, 2 * L + 1)
                squares(lambda t: XA[:, t, :], 4 * L)
                columns(2 + 2 * L, gsc[:, L, 0:8], shc[:, L, 0:8])
                if L == 0:
                    act.wait_ge(xt_dve, 3)
                    act.wait_ge(ew_used, n_items * SLOTS)
                    modulation_rows(1)
                if L == 1:
                    act.dma_start(bfg, bcast(a["b_fg_2"][0])).then_inc(small_loaded, 16)
                    act.wait_ge(flog_dve, 1)
                    fn(lfb, lf, ACT.Abs)
                    act.drain()
                    fn(lfb, lfb, ACT.Exp, scale=-1.0)
                    act.drain()
                    fn(lfb, lfb, ACT.Ln, bias=1.0).then_inc(flog_act, 1)
                    act.wait_ge(ncum_ready, 1)
                    act.dma_start(cum_d, ncumR).then_inc(ncum_written, 16)
                    act.wait_ge(ncum_written, 16)
                    act.dma_start(ncum_b, bcast(cum_d)).then_inc(ncum_loaded, 16)
                attention(1 + L)
                act.wait_ge(y_done, L + 2)
                squares(lambda t: PS[:, 2 * t:2 * t + 2, :].rearrange("p b n -> p (b n)"), 4 * L + 1)
                act.wait_ge(x_updated, 2 * L + 2)
                squares(lambda t: XA[:, t, :], 4 * L + 2)
                columns(3 + 2 * L, gsc[:, L, 8:16], shc[:, L, 8:16])
                with act.Fori(0, FT // 2) as i:
                    for s in range(2):
                        act.wait_ge(cv_ready, i * 2 + (FT * L + s + 1))
                        fn(sl[s], cv[s], ACT.Silu).then_inc(sl_ready, 1)
                act.wait_ge(fdn_done, FT * (L + 1))
                squares(lambda t: PS[:, 2 * t:2 * t + 2, :].rearrange("p b n -> p (b n)"), 4 * L + 3)

        @blk.vector
        def _(dve):
            tt, ts, stt = dve.tensor_tensor, dve.tensor_scalar, dve.scalar_tensor_tensor

            def columns(k, scale=None, shift=None):
                for c in (2, 3, 6, 7):
                    dve.wait_ge(xt_turned, 4 * k + c // 2 + 1)
                    src = PS[:, c // 2, (c % 2) * T:(c % 2 + 1) * T]
                    if scale is None:
                        last = dve.tensor_copy(XT[:, c, :], src)
                    else:
                        last = ts(XT[:, c, :], src, scale[:, c:c + 1], shift[:, c:c + 1], ALU.mult, ALU.add)
                last.then_inc(xt_dve, 1)

            def evacuate(p, g):
                dve.wait_ge(qkv_done, g + (NG * p + 1))
                if p == 2:
                    for h in range(2):
                        r = slice(HD2 * h, HD2 * (h + 1))
                        last = dve.tensor_copy(kab[r, h, :], PS[r, 1, 0:T])
                elif p == 1:
                    last = ts(kab[:, 0, :], PS[:, 1, 0:T], -1.0, None, ALU.mult)
                else:
                    last = dve.tensor_copy(kab[:, 0, :], PS[:, 1, 0:T])
                last.then_inc(k_evac, 1)

            def value_rows(p, g, s):
                dve.wait_ge(v_turned, g + (NG * p + 1))
                dve.tensor_copy(V[:, s, :, :], PS[:, 1, T:2 * T].rearrange("p (t d) -> p t d", t=2))\
                   .then_inc(v_evac, 1)

            def softplus_sum(g):
                dve.wait_ge(lnp_ready, g + 1)
                stt(Pr, banks(2, 768), 0.0, Ssb, ALU.min, ALU.subtract, reverse1=True).then_inc(sp_ready, 1)

            def softmax(p, g):
                dve.wait_ge(sc_done, g + (NG * p + 1))
                if p == 0:
                    tt(Ssb[:, 0:T], bank(2, T), bias_tiles[:, ds(g, 1), :].squeeze(1), ALU.add)
                    tt(Ssb[:, T:384], bank(2, P, at=T), bias_tiles[:, ds(g, 1), P:T].squeeze(1), ALU.add)
                    dve.drain()
                    dve.tensor_reduce(nmx[:, 0:1], Ssb[:, 0:T], AX_X, ALU.max, negate=True)
                    dve.tensor_reduce(nmx[:, 1:2], Ssb[:, T:384], AX_X, ALU.max, negate=True).then_inc(max_ready, 1)
                    n = 2
                else:
                    for t, at, w, wk in ((1, 0, T, T), (0, 512, P, P)):
                        for h in range(2):
                            lo = at + h * w
                            stt(Ssb[:, lo:lo + w], banks(2, 768)[:, lo:lo + w], cumT[:, t, ds(g * 2 + h, 1)],
                                ncum_b[:, ds(g * 2 + h, 1), 0:wk].squeeze(1), ALU.add, ALU.add)
                    dve.drain()
                    dve.tensor_reduce(nmx[:, 0:2], Ssb[:, 0:512].rearrange("p (h t) -> p h t", h=2), AX_X, ALU.max,
                                      negate=True)
                    dve.tensor_reduce(nmx[:, 2:4], Ssb[:, 512:768].rearrange("p (h t) -> p h t", h=2), AX_X, ALU.max,
                                      negate=True).then_inc(max_ready, 1)
                    n = 4
                dve.wait_ge(exp_ready, g + (NG * (p // 2) + 1))
                dve.reciprocal(rcp[:, 0:n], psum_l[:, 0:n])
                dve.drain()
                segs = ((0, T), (T, P)) if p == 0 else ((0, T), (T, T), (512, P), (640, P))
                for k, (lo, w) in enumerate(segs):
                    last = ts(Pr[:, lo:lo + w], Pr[:, lo:lo + w], rcp[:, k:k + 1], None, ALU.mult)
                last.then_inc(prob_ready, 1)

            def heads_out(p, g):
                dve.wait_ge(pv_done, g + (NG * p + 1))
                dve.tensor_copy(OT[:, ds(g, 1), :].squeeze(1), bank(6, T)).then_inc(o_evac, 1)

            def step(p, g, s, first):
                evacuate(p, g)
                value_rows(p, g, s)
                if p == 1 and not first:
                    heads_out(p, g - 1)
                if p == 1:
                    softplus_sum(g)
                else:
                    softmax(p, g)
                if p != 1 and not first:
                    heads_out(p, g - 1)

            def attention(p):
                step(p, 0, 0, True)
                step(p, 1, 1, False)
                with dve.Fori(1, NG // 2) as i:
                    for s in range(2):
                        step(p, i * 2 + s, s, False)
                heads_out(p, NG - 1)

            def finish_modulation(p):
                dve.wait_ge(modfin_turned, p + 1)
                for b in range(8):
                    dve.tensor_reduce(modc[:, 4 * b:4 * b + 4],
                                      bank(b).rearrange("p (c q r) -> p c q r", c=4, q=4)[:, :, :, 0], AX_X, ALU.add)
                dve.drain()
                dve.memset(tmp_inc, 0.0).then_inc(modfin_red, 1)
                for k in range(2):
                    tt(shc[:, p, 8 * k:8 * k + 8], modc[:, 16 * k:16 * k + 8], vcol[:, p, 24 * k:24 * k + 8], ALU.add)
                    tt(modc[:, 16 * k + 8:16 * k + 16], modc[:, 16 * k + 8:16 * k + 16],
                       vcol[:, p, 24 * k + 8:24 * k + 16], ALU.add)
                dve.drain()
                for k in range(2):
                    stt(gsc[:, p, 8 * k:8 * k + 8], modc[:, 16 * k + 8:16 * k + 16], 1.0,
                        vcol[:, p, 48 + 8 * k:56 + 8 * k], ALU.add, ALU.mult)
                dve.wait_ge(modfin_rows, p + 1)
                for k in range(2):
                    tt(bmod_rows[:, k, :], banks(2 * k, D), bmod_rows[:, k, :], ALU.add)
                dve.drain()
                for k in range(2):
                    last = tt(gtg[p][:, k, :], gtg[p][:, k, :], bmod_rows[:, k, :], ALU.mult)
                last.then_inc(modfin_done, 1)

            def layer_norm_stats(source, k):
                for t in range(TT):
                    stt(YB[:, t, :], XA[:, t, :], ALPHA, source(t), ALU.mult, ALU.add)
                dve.drain()
                for t in range(TT):
                    for h in range(2):
                        dve.bn_stats(bst[:, t, h, :], YB[:, t, h * HALF:(h + 1) * HALF])
                dve.drain()
                for t in range(TT):
                    last = dve.bn_aggr(mv[:, t, :], bst[:, t, :, :])
                last.then_inc(var_ready, 1)

            def layer_norm_apply(k):
                dve.wait_ge(rstd_ready, k + 1)
                for t in range(TT):
                    ts(YB[:, t, :], YB[:, t, :], mv[:, t, 0:1], rstd[:, t:t + 1], ALU.subtract, ALU.mult)
                dve.drain()
                dve.wait_ge(lnc_loaded, 32 * (k + 1))
                for t in range(TT):
                    tt(YB[:, t, :], YB[:, t, :], LNC[:, 0, :], ALU.mult)
                dve.drain()
                for t in range(TT):
                    last = tt(YB[:, t, :], YB[:, t, :], LNC[:, 1, :], ALU.add)
                    if k == 0:
                        last.then_inc(xn_ready, 1)
                dve.drain()
                for t in range(TT):
                    last = dve.tensor_copy(XA[:, t, :], YB[:, t, :])
                return last

            def normed_rows(n):
                dve.wait_ge(rstd_ready, n + 1)
                for t in range(TT):
                    ts(YB[:, t, :], XA[:, t, :], rstd[:, t:t + 1], None, ALU.mult).then_inc(xn_ready, 1)

            def add_normed(n, g):
                dve.wait_ge(rstd_ready, n + 1)
                for t in range(TT):
                    stt(YB[:, t, :], banks(2 * t, D), rstd[:, t:t + 1], g, ALU.mult, ALU.mult)
                dve.drain()
                for t in range(TT):
                    last = tt(XA[:, t, :], XA[:, t, :], YB[:, t, :], ALU.add)
                last.then_inc(x_updated, 1)

            tmp_inc = rcp[:, 3:4]
            dve.wait_ge(rel_loaded, 16)
            starts = bucket_starts()
            for b in range(BUCKETS):
                lo, hi = starts[b], starts[b + 1]
                dve.tensor_copy(bias_row[:, T - hi:T - lo], bias_src[:, b:b + 1].to_broadcast([8, hi - lo]))
            dve.memset(bias_row[:, T:384], NEG)
            dve.drain()
            dve.memset(st[0:8, 47:48], 0.0).then_inc(bias_row_ready, 1)
            dve.wait_ge(vec_turned, 1)
            for L in range(2):
                dve.tensor_copy(vcol[:, L, :], bank(4, 152, at=L * 256))
            dve.wait_ge(cond_turned, 1)
            dve.tensor_copy(ccrep[:, :, :], bank(6, 8).unsqueeze(2).to_broadcast([P, KD, 32])).then_inc(cond_ready, 1)
            dve.wait_ge(bias_row_ready, 1)
            columns(0)
            dve.wait_ge(bias_loaded, 16)
            attention(0)
            finish_modulation(0)
            dve.wait_ge(y_done, 1)
            layer_norm_stats(lambda t: banks(2 * t, D), 0)
            layer_norm_apply(0).then_inc(lnc_used, 1)
            columns(1)
            dve.wait_ge(rt_pe, 1)
            dve.wait_ge(small_loaded, 32)
            tt(lg, bank(4, 64).rearrange("p (t e) -> p t e", t=2), br.unsqueeze(1).to_broadcast([P, 2, E]), ALU.add)
            dve.drain()
            for t in range(TT):
                dve.max(m8[:, t, :], lg[:, t, :])
            dve.drain()
            for t in range(TT):
                ts(nmx[:, t:t + 1], m8[:, t, 0:1], -1.0, None, ALU.mult)
                ts(gtm[:, t, :], lg[:, t, :], m8[:, t, 3:4], None, ALU.is_gt)
                ts(eqm[:, t, :], lg[:, t, :], m8[:, t, 3:4], None, ALU.is_equal)
            dve.drain()
            for t in range(TT):
                dve.tensor_reduce(rcp[:, t:t + 1], gtm[:, t, :], AX_X, ALU.add)
            dve.drain()
            for t in range(TT):
                dve.tensor_tensor_scan(csm[:, t, :], eqm[:, t, :], eqm[:, t, :], rcp[:, t:t + 1], ALU.bypass, ALU.add)
            dve.drain()
            for t in range(TT):
                stt(csm[:, t, :], csm[:, t, :], float(TOPK), eqm[:, t, :], ALU.is_le, ALU.mult)
            dve.drain()
            tt(sel, csm, gtm, ALU.add)
            dve.drain()
            dve.memset(tmp_inc, 0.0).then_inc(rt_dve, 1)
            dve.wait_ge(rt_act, 1)
            tt(ex, ex, sel, ALU.mult)
            dve.drain()
            dve.tensor_reduce(rcp[:, 0:2], ex, AX_X, ALU.add)
            dve.drain()
            dve.reciprocal(rcp[:, 0:2], rcp[:, 0:2])
            dve.drain()
            for t in range(TT):
                ts(gatx[:, t, 0:E], ex[:, t, :], rcp[:, t:t + 1], None, ALU.mult)
            dve.wait_ge(rt_pe, 2)
            stt(posx[:, :, 0:E], bank(5, 64).rearrange("p (t e) -> p t e", t=2), 1.0, sel, ALU.add, ALU.mult)
            dve.tensor_copy(cnt[0:E, 0:1], bank(6, 1, slice(0, E)))
            dve.drain()
            ts(posx[:, :, 0:E], posx[:, :, 0:E], -1.0, None, ALU.add)
            ts(cnt[0:E, 1:2], cnt[0:E, 0:1], float(CAP), None, ALU.is_gt)
            ts(cnt[0:E, 2:3], cnt[0:E, 0:1], float(2 * CAP), None, ALU.is_gt)
            ts(cnt[0:E, 3:4], cnt[0:E, 0:1], float(3 * CAP), None, ALU.is_gt)
            dve.drain()
            tt(cnt[0:E, 1:2], cnt[0:E, 1:2], cnt[0:E, 2:3], ALU.add)
            dve.drain()
            tt(cnt[0:E, 1:2], cnt[0:E, 1:2], cnt[0:E, 3:4], ALU.add)
            dve.drain()
            dve.memset(tmp_inc, 0.0).then_inc(rt_dve, 1)
            dve.wait_ge(rt_pe, 3)
            dve.tensor_copy(cnt[0:E, 4:5], bank(7, 1, slice(0, E)))
            dve.tensor_copy(posT, bank(4, T, slice(0, E)))
            dve.tensor_copy(gatT, bank(4, T, slice(0, E), at=T))
            dve.tensor_copy(IE[0:E, 0:E], ident[0:E, 0:E])
            dve.drain()
            tt(cnt[0:E, 5:6], cnt[0:E, 4:5], cnt[0:E, 1:2], ALU.subtract)
            ts(Aj[0:E, :], iotaj[0:E, :], cnt[0:E, 4:5], None, ALU.is_ge)
            dve.drain()
            ts(IE[0:E, E:NIT], iotaj[0:E, :], cnt[0:E, 5:6], None, ALU.is_ge)
            dve.drain()
            tt(IE[0:E, E:NIT], IE[0:E, E:NIT], Aj[0:E, :], ALU.subtract)
            dve.drain()
            ts(EXj[0:E, :], IE[0:E, E:NIT], cnt[0:E, 5:6], None, ALU.mult)
            dve.drain()
            dve.memset(tmp_inc, 0.0).then_inc(rt_dve, 1)
            dve.wait_ge(rt_pe, 4)
            ts(itf[:, 0:E], iota64[:, 0:E], 0.0, None, ALU.add)
            ts(itf[:, E:NIT], bank(5, 17), float(E - 1), None, ALU.min)
            ts(itf[:, NIT:NIT + 1], bank(5, 1, at=64), float(E), None, ALU.add)
            tt(csm[:, 0, 0:17], iotaj[:, :], bank(5, 17, at=32), ALU.subtract)
            dve.drain()
            ts(csm[:, 0, 0:17], csm[:, 0, 0:17], float(CAP), float(CAP), ALU.mult, ALU.add)
            dve.tensor_copy(items_i[0:1, :], itf[0:1, :]).then_inc(items_ready, 1)
            dve.drain()
            for t in range(TT):
                tt(posx[:, t, E:NIT], bank(6, 17, at=t * 17), csm[:, 0, 0:17], ALU.subtract)
                dve.tensor_copy(gatx[:, t, E:NIT], bank(6, 17, at=64 + t * 17))
            for f2 in range(2):
                dve.tensor_copy(bguT[:, :, 8 * f2:8 * f2 + 8].rearrange("p i f -> p f i"),
                                bank(f2, 8 * NIT).rearrange("p (f i) -> p f i", f=8))
            for q, b in enumerate((2, 3, 4, 7)):
                dve.tensor_copy(YB[:, q // 2, (q % 2) * HALF:(q % 2 + 1) * HALF], bank(b))
            dve.memset(ysb, 0.0)
            dve.memset(selT, 0.0)
            dve.drain()
            dve.memset(tmp_inc, 0.0).then_inc(rt_dve, 1)
            dve.memset(nmx[:, 2:3], 0.0).then_inc(zero_ready, 1)
            dve.memset(nmx[:, 3:4], 0.0).then_inc(acc_done, 1)
            dve.wait_ge(items_ready, 1)
            n_items = dve.value_load(items_i[0:1, NIT:NIT + 1], min_val=E, max_val=E + MAX_EXTRA)

            def choose(j):
                for t in range(TT):
                    last = ts(selx[:, t, :], iota64[:, :], posx[:, t, ds(j, 1)], None, ALU.is_equal)
                last.then_inc(selx_ready, 1)

            def gathered_columns(j):
                dve.wait_ge(xe_turned, j + 1)
                dve.tensor_copy(xeT.rearrange("p (h c) s -> p c h s", h=2),
                                bank(7).rearrange("p (c h s) -> p c h s", c=4, h=2)).then_inc(xeT_ready, 1)

            def accumulate(i):
                for q, b in enumerate((4, 5, 0, 1)):
                    t, n = q // 2, q % 2
                    dve.wait_ge(sc_mm, i * 4 + (q + 1))
                    y = YB[:, t, n * HALF:(n + 1) * HALF]
                    tt(y, y, bank(b), ALU.add).then_inc(acc_done, 1)

            choose(0)
            gathered_columns(0)
            with dve.Fori(0, n_items) as i:
                dve.wait_ge(gat_mm, i + 1)
                choose(i + 1)
                dve.wait_ge(selT_ev, i + 1)
                for t in range(TT):
                    for h in range(2):
                        last = ts(selg[:, t, h * CAP:(h + 1) * CAP], iota64[:, :], posx[:, t, ds(i, 1)],
                                  gatx[:, t, ds(i, 1)], ALU.is_equal, ALU.mult)
                last.then_inc(selg_ready, 1)
                dve.wait_ge(h_turned, i + 1)
                hT = banks(2, D).rearrange("p (f c s) -> p f c s", f=8, c=2)
                bg = bguT[:, ds(i, 1), :].squeeze(1)
                tt(gs_b, hT[:, :, 0, :], bg[:, 0:8].unsqueeze(2).to_broadcast([P, 8, CAP]), ALU.add)
                tt(us_b, hT[:, :, 1, :], bg[:, 8:16].unsqueeze(2).to_broadcast([P, 8, CAP]), ALU.add)
                dve.drain()
                ts(gs_b, gs_b, LIMIT, None, ALU.min).then_inc(g_ready, 1)
                ts(us_b, us_b, LIMIT, -LIMIT, ALU.min, ALU.max)
                dve.drain()
                stt(us_b, us_b, 1.0, gs_b, ALU.add, ALU.mult)
                dve.drain()
                dve.wait_ge(sg_ready, i + 1)
                tt(actT, us_b, ss_b, ALU.mult).then_inc(act_ready, 1)
                accumulate(i)
                gathered_columns(i + 1)
            accumulate(n_items)
            dve.drain()
            for t in range(TT):
                stt(YB[:, t, :], XA[:, t, :], ALPHA, YB[:, t, :], ALU.mult, ALU.add)
            dve.drain()
            for t in range(TT):
                for h in range(2):
                    dve.bn_stats(bst[:, t, h, :], YB[:, t, h * HALF:(h + 1) * HALF])
            dve.drain()
            for t in range(TT):
                last = dve.bn_aggr(mv[:, t, :], bst[:, t, :, :])
            last.then_inc(var_ready, 1)
            layer_norm_apply(1).then_inc(x_updated, 1)
            for L in range(2):
                normed_rows(2 + 4 * L)
                if L == 0:
                    dve.memset(qab, 0.0)
                else:
                    dve.memset(kab, 0.0)
                columns(2 + 2 * L, gsc[:, L, 0:8], shc[:, L, 0:8])
                if L == 1:
                    dve.wait_ge(small_loaded, 48)
                    dve.wait_ge(flog_done, 1)
                    tt(lf, bank(4, 32).rearrange("p (t h) -> p t h", t=2),
                       bfg.unsqueeze(1).to_broadcast([P, 2, 16]), ALU.add)
                    dve.drain()
                    dve.memset(tmp_inc, 0.0).then_inc(flog_dve, 1)
                    dve.wait_ge(flog_act, 1)
                    stt(lf, lf, 0.0, lfb, ALU.min, ALU.subtract).then_inc(flog_dve, 1)
                    dve.wait_ge(cum_done, 1)
                    dve.tensor_copy(cumT, bank(5, 32).rearrange("p (t h) -> p t h", t=2))
                    ts(ncumR, bank(7, T, slice(0, 16)), -1.0, None, ALU.mult).then_inc(ncum_ready, 1)
                    dve.wait_ge(ncum_loaded, 16)
                attention(1 + L)
                if L == 0:
                    finish_modulation(1)
                add_normed(3 + 4 * L, gtg[L][:, 0, :])
                normed_rows(4 + 4 * L)
                columns(3 + 2 * L, gsc[:, L, 8:16], shc[:, L, 8:16])

                def ffn_tile(j, s, w):
                    dve.wait_ge(fgu_done, j + (FT * L + 1))
                    gate = bank(4 + s, T)
                    col = lambda r: vcol[:, L, ds(j + (64 + r * FT), 1)]
                    ts(cv[s], gate, col(2), col(3), ALU.mult, ALU.add)
                    dve.drain()
                    stt(cv[s][:, 1:T], gate[:, 0:T - 1], col(1), cv[s][:, 1:T], ALU.mult, ALU.add)
                    dve.drain()
                    stt(cv[s][:, 2:T], gate[:, 0:T - 2], col(0), cv[s][:, 2:T], ALU.mult, ALU.add)\
                        .then_inc(cv_ready, 1)
                    dve.wait_ge(sl_ready, j + (FT * L + 1))
                    if w:
                        dve.wait_ge(fdn_done, j + (FT * L - 1))
                    tt(aT[s], sl[s], bank(4 + s, T, at=T), ALU.mult).then_inc(fact_ready, 1)

                for s in range(2):
                    ffn_tile(s, s, False)
                with dve.Fori(1, FT // 2) as i:
                    for s in range(2):
                        ffn_tile(i * 2 + s, s, True)
                add_normed(5 + 4 * L, gtg[L][:, 1, :])


_INS = ["x", "rel_bias", "a_w_in", "a_w_out", "ln_g", "ln_b", "moe_w_router", "moe_b_router", "moe_w_gate_up",
        "moe_b_gate_up", "moe_w_down", "moe_b_down", "c_2", "w_mod_2", "b_mod_2", "g_mix_pre_2", "g_mix_post_2",
        "w_qkv_2", "w_o_2", "w_fg_2", "b_fg_2", "g_ffn_pre_2", "g_ffn_post_2", "w_ffn_gate_2", "w_ffn_up_2",
        "w_conv_2", "b_conv_2", "w_ffn_down_2"]


def kernel(**inputs):
    import concourse.bacc as _bacc
    from concourse.bass_utils import run_bass_kernel_spmd as _run

    nc = _bacc.Bacc("TRN2", target_bir_lowering=False, num_devices=1)
    arrays, args = {}, {}
    for name in _INS:
        x = np.ascontiguousarray(inputs[name])
        arrays[f"in_{name}"] = x
        args[name] = nc.dram_tensor(f"in_{name}", x.shape, mybir.dt.from_np(x.dtype), kind="ExternalInput").ap()
    out = nc.dram_tensor("out_0", (1, T, D), F32, kind="ExternalOutput").ap()
    block_kernel(nc, args, out)
    r = _run(nc, [arrays], core_ids=[0])
    return r.results[0]["out_0"]
```

```python
from contextlib import ExitStack

import numpy as np

import concourse.bass as bass
from concourse import mybir

F32 = mybir.dt.float32
BF16 = mybir.dt.bfloat16
I32 = mybir.dt.int32
ALU = mybir.AluOpType
ACT = mybir.ActivationFunctionType
AX_X = mybir.AxisListType.X

P = 128
T = 256
TT = T // P
D = 1024
KD = D // P
HALF = 512
NG = D // P
HD2 = 64
E = 32
TOPK = 4
CAP = 64
MAX_EXTRA = 16
NIT = E + MAX_EXTRA + 1
F = 2816
FT = F // P
BUCKETS = 32
MAX_DIST = 128
ALPHA = 2.0 ** 0.25
LN_EPS = 1e-5
RMS_EPS = 1e-6
LIMIT = 7.0
SWIGLU_ALPHA = 1.702
NEG = -1e30
MODW = 6 * D
MB = 384
NMB = MODW // MB

R_WO, R_ACC, R_STREAM, R_GTG1, R_BMOD = 0, 8192, 14336, 20480, 22528
SLOT = 2048
GU_SLOTS, DN_SLOTS = 8, 4
SLOTS = GU_SLOTS + DN_SLOTS


def bucket_starts():
    exact = BUCKETS // 2
    n = np.arange(T)
    large = exact + (np.log(np.maximum(n, 1).astype(np.float32) / exact)
                     / np.float32(np.log(MAX_DIST / exact)) * (BUCKETS - exact)).astype(np.int32)
    b = np.where(n < exact, n, np.minimum(large, BUCKETS - 1))
    return [int(np.argmax(b == k)) for k in range(BUCKETS)] + [T]


def block_kernel(nc, a, out):
    with ExitStack() as ctx:
        def sb(name, shape, dt=F32):
            return ctx.enter_context(nc.sbuf_tensor(name, shape, dt))

        def sem(name):
            return ctx.enter_context(nc.semaphore(name))

        ds = bass.ds

        R = sb("big", [P, SLOTS * SLOT])
        G = sb("group_weights", [P, 2, 3 * D])
        XA = sb("x_rows", [P, TT, D])
        YB = sb("y_rows", [P, TT, D])
        XT = sb("x_cols", [P, KD, T])
        OT = sb("att_cols", [P, KD, T])
        SC = sb("scratch", [P, 8192])
        LNC = sb("ln_consts", [P, 2, D])
        GTG0 = sb("gate_gain0", [P, 2, D])
        ident = sb("ident", [P, P])
        ones = sb("ones", [P, P])
        ltri = sb("ltri", [P, P])
        ustr = sb("ustrict", [P, P])
        uinc = sb("uinc", [P, P])

        identb = sb("identb", [P, P], BF16)
        mask0 = sb("mask_strict", [P, P], BF16)
        mask1 = sb("mask_causal", [P, P], BF16)
        iota64 = sb("iota64", [P, CAP])
        iotaj = sb("iotaj", [P, MAX_EXTRA + 1])
        cc = sb("cond_cols", [P, KD])
        vcol = sb("vec_cols", [P, 2, 152])
        modc = sb("mod_cols", [P, 32])
        shc = sb("shift_cols", [P, 2, 16])
        gsc = sb("scale_cols", [P, 2, 16])
        wfg = sb("w_fg", [P, KD, 16])
        st = sb("stats", [P, 48])
        items_i = sb("items", [1, NIT + 1], I32)
        PS = ctx.enter_context(nc.psum_tensor("ps", [P, 8, HALF], F32))

        wo_r = R[:, R_WO:R_WO + 8 * D].rearrange("p (k n) -> p k n", k=KD)
        macc = R[:, R_ACC:R_ACC + MODW]
        mstream = [R[:, R_STREAM + s * KD * MB:R_STREAM + (s + 1) * KD * MB].rearrange("p (k n) -> p k n", k=KD)
                   for s in range(2)]
        gtg = [GTG0[:, :, :], R[:, R_GTG1:R_GTG1 + 2 * D].rearrange("p (a n) -> p a n", a=2)]
        bmod_rows = R[:, R_BMOD:R_BMOD + 2 * D].rearrange("p (a n) -> p a n", a=2)
        slot = [R[:, s * SLOT:(s + 1) * SLOT] for s in range(SLOTS)]

        def part(at, n):
            return SC[:, at:at + n]

        qab = part(0, 512).rearrange("p (h t) -> p h t", h=2)
        kab = part(512, 512).rearrange("p (h t) -> p h t", h=2)
        vT = part(1024, 256)
        V = part(1280, 512).rearrange("p (b s d) -> p b s d", b=2, s=2)
        Ssb = part(1792, 768)
        Pr = part(2560, 768)
        PT = part(3328, 768)
        bias_tiles = part(4096, 2048).rearrange("p (h c) -> p h c", h=8)
        ncum_b = part(4096, 4096).rearrange("p (h t) -> p h t", h=16)
        xeT = part(0, 512).rearrange("p (k s) -> p k s", k=KD)
        xe = part(1024, 512)
        hsb = part(1536, 1024)
        gs_b = part(2560, 512).rearrange("p (f s) -> p f s", s=CAP)
        us_b = part(3072, 512).rearrange("p (f s) -> p f s", s=CAP)
        ss_b = part(3584, 512).rearrange("p (f s) -> p f s", s=CAP)
        actT = part(4096, 512).rearrange("p (f s) -> p f s", s=CAP)
        ysb = part(4608, 1024)
        selx = part(5632, 128).rearrange("p (t s) -> p t s", t=2)
        selg = part(5760, 256).rearrange("p (t s) -> p t s", t=2)
        selT = part(6016, 256)
        bguT = part(6528, NIT * 16).rearrange("p (i f) -> p i f", f=16)
        posx = part(7312, 2 * NIT).rearrange("p (t i) -> p t i", t=2)
        gatx = part(7410, 2 * NIT).rearrange("p (t i) -> p t i", t=2)
        lg = part(7508, 64).rearrange("p (t e) -> p t e", t=2)
        m8 = part(7572, 16).rearrange("p (t e) -> p t e", t=2)
        ex = part(7588, 64).rearrange("p (t e) -> p t e", t=2)
        gtm = part(7652, 64).rearrange("p (t e) -> p t e", t=2)
        eqm = part(7716, 64).rearrange("p (t e) -> p t e", t=2)
        csm = part(7780, 64).rearrange("p (t e) -> p t e", t=2)
        sel = part(7844, 64).rearrange("p (t e) -> p t e", t=2)
        br = part(7908, 32)
        IE = part(7940, NIT)
        Aj = part(7990, 17)
        EXj = part(8010, 17)
        cnt = part(8030, 8)
        itf = part(8040, NIT + 1)
        posT = XT[0:E, 0, :]
        gatT = XT[0:E, 1, :]
        b_gu_rows = OT[0:E, :, :].rearrange("p k t -> p (k t)")
        b_dn_rows = G[0:E, 0, 0:D]
        w_rt = G[:, 1, 0:KD * E].rearrange("p (k e) -> p k e", k=KD)
        cv = [part(256 * s, 256) for s in range(2)]
        sl = [part(512 + 256 * s, 256) for s in range(2)]
        aT = [part(1024 + 256 * s, 256) for s in range(2)]
        junk = [part(2048 + 1024 * s, 1024) for s in range(2)]
        ssq = st[:, 0:2]
        rstd = st[:, 2:4]
        mhalf = st[:, 4:6]
        nmx = st[:, 6:10]
        psum_l = st[:, 10:14]
        mv = st[:, 14:18].rearrange("p (t v) -> p t v", t=2)
        bst = st[:, 18:42].rearrange("p (t h v) -> p t h v", t=2, h=2)
        tmp2 = st[:, 42:44]
        rcp = st[:, 44:48]
        vrow = YB
        bias_src = XT[0:8, 0, 0:32]
        bias_row = OT[0:8, 0:2, :].rearrange("p k t -> p (k t)")[:, 0:384]
        lf = part(3328, 32).rearrange("p (t h) -> p t h", t=2)
        lfb = part(3392, 32).rearrange("p (t h) -> p t h", t=2)
        bfg = part(3424, 16)
        cumT = LNC[:, 0, 0:32].rearrange("p (t h) -> p t h", t=2)
        ncumR = LNC[0:16, 1, 0:256]

        bias_d = nc.dram_tensor("bias_scratch", [8, P, 384], F32).ap()
        cum_d = nc.dram_tensor("cum_scratch", [16, T], F32).ap()

        consts_ready = sem("consts_ready")
        x_loaded = sem("x_loaded")
        small_loaded = sem("small_loaded")
        vrow_loaded = sem("vrow_loaded")
        rel_loaded = sem("rel_loaded")
        bias_row_ready = sem("bias_row_ready")
        bias_written = sem("bias_written")
        bias_loaded = sem("bias_loaded")
        vec_turned = sem("vec_turned")
        vec_ready = sem("vec_ready")
        cond_ready = sem("cond_ready")
        silu_ready = sem("silu_ready")
        cond_turned = sem("cond_turned")
        lnc_loaded = sem("lnc_loaded")

        xt_turned = sem("xt_turned")
        xt_act = sem("xt_act")
        xt_dve = sem("xt_dve")
        xn_ready = sem("xn_ready")
        ssq_ready = sem("ssq_ready")
        var_ready = sem("var_ready")
        rstd_ready = sem("rstd_ready")
        att_w = [sem(f"att_w{s}") for s in range(2)]
        qkv_done = sem("qkv_done")
        qv_evac = sem("qv_evac")
        k_evac = sem("k_evac")
        v_turned = sem("v_turned")
        v_evac = sem("v_evac")
        sc_done = sem("sc_done")
        max_ready = sem("max_ready")
        exp_ready = sem("exp_ready")
        prob_ready = sem("prob_ready")
        pt_turned = sem("pt_turned")
        pt_evac = sem("pt_evac")
        pv_done = sem("pv_done")
        o_evac = sem("o_evac")
        lnp_ready = sem("lnp_ready")
        sp_ready = sem("sp_ready")
        r_done = sem("r_done")
        at_ready = sem("at_ready")
        mod_w = [sem(f"mod_w{s}") for s in range(2)]
        mod_summed = sem("mod_summed")
        modfin_rows = sem("modfin_rows")
        modfin_gates = sem("modfin_gates")
        modfin_turned = sem("modfin_turned")
        modfin_read = sem("modfin_read")
        modvec_loaded = sem("modvec_loaded")
        wo_loaded = sem("wo_loaded")
        y_done = sem("y_done")
        y_read = sem("y_read")
        x_updated = sem("x_updated")
        rt_w = sem("rt_w")
        b_gu_loaded = sem("b_gu_loaded")
        rt_pe = sem("rt_pe")
        rt_dve = sem("rt_dve")
        rt_act = sem("rt_act")
        items_ready = sem("items_ready")
        ew = [sem(f"expert_w{s}") for s in range(SLOTS)]
        ew_used = sem("expert_w_used")
        selx_ready = sem("selx_ready")
        selg_ready = sem("selg_ready")
        gat_mm = sem("gat_mm")
        xe_ev = sem("xe_ev")
        xe_turned = sem("xe_turned")
        xeT_ready = sem("xeT_ready")
        selT_turned = sem("selT_turned")
        selT_ev = sem("selT_ev")
        h_ev = sem("h_ev")
        h_turned = sem("h_turned")
        g_ready = sem("g_ready")
        sg_ready = sem("sg_ready")
        act_ready = sem("act_ready")
        y_ev = sem("y_ev")
        sc_mm = sem("sc_mm")
        acc_done = sem("acc_done")
        zero_ready = sem("zero_ready")
        ffn_w = [sem(f"ffn_w{s}") for s in range(2)]
        ffn_dw = [sem(f"ffn_dw{s}") for s in range(2)]
        fgu_done = sem("fgu_done")
        cv_ready = sem("cv_ready")
        sl_ready = sem("sl_ready")
        fact_ready = sem("fact_ready")
        fdn_done = sem("fdn_done")
        fy_done = sem("fy_done")
        flog_done = sem("flog_done")
        flog_dve = sem("flog_dve")
        flog_act = sem("flog_act")
        cum_done = sem("cum_done")
        ncum_ready = sem("ncum_ready")
        ncum_written = sem("ncum_written")
        ncum_loaded = sem("ncum_loaded")
        out_stored = sem("out_stored")

        def bank(b, n=HALF, rows=slice(0, P), at=0):
            return PS[rows, b, at:at + n]

        def banks(b, n):
            return PS[:, :, :].rearrange("p b n -> p (b n)")[:, b * HALF:b * HALF + n]

        w_qkv = [a["a_w_in"][0], a["w_qkv_2"][0], a["w_qkv_2"][1]]
        w_out = [a["a_w_out"][0], a["w_o_2"][0], a["w_o_2"][1]]
        rows_of = lambda ap: ap.rearrange("(k p) n -> p k n", p=P)
        x_rows = a["x"][0].rearrange("(t p) d -> p t d", p=P)

        def bcast(ap):
            return ap.partition_broadcast(P)

        blk = ctx.enter_context(nc.Block())

        @blk.sync
        def _(sp):
            def att_weights(p, g, half, s):
                src = rows_of(w_qkv[p]).rearrange("p k (c n) -> p k c n", c=3)
                for c in range(3):
                    sp.dma_start(G[:, s, c * D:(c + 1) * D].rearrange("p (k n) -> p k n", k=KD),
                                 src[:, :, c, ds(g * P, P)]).then_inc(att_w[s], 16)

            def mod_block(p, m, s):
                sp.dma_start(mstream[s], rows_of(a["w_mod_2"][p])[:, :, ds(m * MB, MB)]).then_inc(mod_w[s], 16)

            def attention_loads(p):
                att_weights(p, 0, 0, 0)
                if p == 2:
                    sp.wait_ge(fgu_done, FT)
                    sp.wait_ge(fdn_done, FT)
                att_weights(p, 1, 0, 1)
                if p == 1:
                    sp.wait_ge(ew_used, n_items * SLOTS)
                if p < 2:
                    mod_block(p, 0, 0)
                    mod_block(p, 1, 1)
                with sp.Fori(1, NG // 2) as i:
                    for s in range(2):
                        sp.wait_ge(qkv_done, i * 2 + (NG * p + s - 1))
                        att_weights(p, i * 2 + s, i, s)
                        if p < 2:
                            for r in range(2):
                                sp.wait_ge(mod_summed, i * 4 + (NMB * p + 2 * s + r - 3))
                                mod_block(p, i * 4 + (2 * s + r - 2), r)
                if p == 2:
                    sp.wait_ge(y_done, 4)
                sp.dma_start(wo_r, rows_of(w_out[p])).then_inc(wo_loaded, 16)
                if p < 2:
                    for r in range(2):
                        sp.wait_ge(mod_summed, NMB * (p + 1) + r - 3)
                        mod_block(p, NMB + r - 2, r)

            def ffn_weights(L, j, s):
                for c, name in enumerate(("w_ffn_gate_2", "w_ffn_up_2")):
                    sp.dma_start(G[:, s, c * D:(c + 1) * D].rearrange("p (k n) -> p k n", k=KD),
                                 rows_of(a[name][L])[:, :, ds(j * P, P)]).then_inc(ffn_w[s], 16)

            def ffn_down(L, j, s):
                sp.dma_start(G[:, s, 2 * D:3 * D], a["w_ffn_down_2"][L][ds(j * P, P), :]).then_inc(ffn_dw[s], 16)

            def ffn_loads(L):
                for s in range(2):
                    sp.wait_ge(qkv_done, NG * (L + 1) + NG - 1 + s)
                    ffn_weights(L, s, s)
                    ffn_down(L, s, s)
                with sp.Fori(1, FT // 2) as i:
                    for s in range(2):
                        sp.wait_ge(fgu_done, i * 2 + (FT * L + s - 1))
                        ffn_weights(L, i * 2 + s, s)
                        sp.wait_ge(fdn_done, i * 2 + (FT * L + s - 1))
                        ffn_down(L, i * 2 + s, s)

            def expert_slot(e, s):
                if s < GU_SLOTS:
                    src = a["moe_w_gate_up"][0, ds(e, 1)].rearrange("a (k p) n -> p (a k) n", p=P)[:, s, :]
                    sp.dma_start(slot[s], src).then_inc(ew[s], 16)
                else:
                    d = s - GU_SLOTS
                    src = a["moe_w_down"][0, ds(e, 1)].rearrange("a (k p) n -> p (a k) n", p=P)[:, 2 * d:2 * d + 2, :]
                    sp.dma_start(slot[s].rearrange("p (k n) -> p k n", k=2), src).then_inc(ew[s], 16)

            sp.dma_start(XA[:, :, :], x_rows).then_inc(x_loaded, 16)
            attention_loads(0)
            sp.wait_ge(qkv_done, NG)
            sp.dma_start(w_rt, rows_of(a["moe_w_router"][0])).then_inc(rt_w, 16)
            sp.dma_start(b_dn_rows, a["moe_b_down"][0]).then_inc(rt_w, 16)
            sp.wait_ge(mod_summed, NMB)
            for s in range(7, 11):
                expert_slot(0, s)
            sp.wait_ge(modfin_gates, 1)
            expert_slot(0, 11)
            sp.wait_ge(modfin_turned, 2)
            for s in range(4, 7):
                expert_slot(0, s)
            sp.wait_ge(y_done, 2)
            sp.dma_start(b_gu_rows, a["moe_b_gate_up"][0]).then_inc(b_gu_loaded, 16)
            for s in range(4):
                expert_slot(0, s)
            sp.wait_ge(items_ready, 1)
            n_items = sp.value_load(items_i[0:1, NIT:NIT + 1], min_val=E, max_val=E + MAX_EXTRA)
            with sp.Fori(1, n_items) as i:
                e = sp.value_load(items_i[0:1, ds(i, 1)], min_val=0, max_val=E - 1)
                for s in range(SLOTS):
                    sp.wait_ge(ew_used, i * SLOTS + (s + 1 - SLOTS))
                    expert_slot(e, s)
            attention_loads(1)
            ffn_loads(0)
            sp.wait_ge(fgu_done, FT - 1)
            sp.wait_ge(fdn_done, FT - 1)
            attention_loads(2)
            ffn_loads(1)
            for t in range(TT):
                sp.wait_ge(x_updated, 4 * TT + t + 1)
                sp.dma_start(out[0, t * P:(t + 1) * P, :], XA[:, t, :]).then_inc(out_stored, 16)
            sp.wait_ge(out_stored, 16 * TT)

        @blk.gpsimd
        def _(pool):
            def triangle(t, inside, outside, pattern, mult, op):
                pool.memset(t[:, :], inside)
                pool.drain()
                pool.affine_select(out=t[:, :], in_=t[:, :], compare_op=op, fill=outside, base=0,
                                   pattern=[[pattern, P]], channel_multiplier=mult)

            triangle(ident, 0.0, 1.0, -1, 1, ALU.not_equal)
            triangle(ltri, 1.0, 0.0, -1, 1, ALU.is_ge)
            triangle(ustr, 1.0, 0.0, 1, -1, ALU.is_gt)
            triangle(uinc, 1.0, 0.0, 1, -1, ALU.is_ge)
            triangle(identb, 0.0, 1.0, -1, 1, ALU.not_equal)
            triangle(mask0, 0.0, -NEG, 1, -1, ALU.is_gt)
            triangle(mask1, 0.0, NEG, -1, 1, ALU.is_ge)
            pool.memset(ones[:, :], 1.0)

            pool.memset(mhalf, -0.5)
            pool.iota(iota64[:, :], [[1, CAP]], 0, 0, allow_small_or_imprecise_dtypes=True)
            pool.iota(iotaj[:, :], [[1, MAX_EXTRA + 1]], 0, 0, allow_small_or_imprecise_dtypes=True)
            pool.drain()
            pool.memset(tmp2, 0.0).then_inc(consts_ready, 1)

            def to_rstd(t, source, scale, eps):
                pool.tensor_scalar(tmp2[:, t:t + 1], source, scale, eps, ALU.mult, ALU.add)
                pool.drain()
                pool.tensor_tensor(rstd[:, t:t + 1], tmp2[:, t:t + 1], mhalf[:, t:t + 1], ALU.pow)\
                    .then_inc(rstd_ready, 1)

            for k in range(2):
                for t in range(TT):
                    pool.wait_ge(var_ready, TT * k + t + 1)
                    to_rstd(t, mv[:, t, 1:2], 1.0, LN_EPS)
            for k in range(8):
                for t in range(TT):
                    pool.wait_ge(ssq_ready, TT * k + t + 1)
                    to_rstd(t, ssq[:, t:t + 1], 1.0 / D, RMS_EPS)

        @blk.tensor
        def _(pe):
            mm = pe.matmul

            def turn_rows(k):
                src = XA if k < 2 else YB
                for t in range(TT):
                    if k == 0:
                        pe.wait_ge(x_loaded, 16)
                    else:
                        pe.wait_ge(xn_ready, TT * (k - 1) + t + 1)
                    for c in range(KD):
                        last = pe.transpose(PS[:, 4 + c // 2, (c % 2) * T + t * P:(c % 2) * T + (t + 1) * P],
                                            src[:, t, c * P:(c + 1) * P], ident[:, :])
                        if t == TT - 1 and c % 2:
                            last.then_inc(xt_turned, 1)

            def qkv(p, g, half, s):
                pe.wait_ge(att_w[s], half * 48 + (48 * (NG // 2) * p + 48))
                if not (p == 0 and isinstance(g, int) and g == 0):
                    pe.wait_ge(v_evac, g + NG * p)
                w = G[:, s, :].rearrange("p (c k n) -> p c k n", c=3, k=KD)
                for c, (b, at) in enumerate(((0, 0), (1, 0), (0, T))):
                    dst = bank(b, T, at=at)
                    for k in range(KD):
                        last = mm(dst, w[:, c, k, :], XT[:, k, :], start=(k == 0), stop=(k == KD - 1))
                last.then_inc(qkv_done, 1)

            def turn_v(p, g, s):
                pe.wait_ge(qv_evac, g + (NG * p + 1))
                pe.wait_ge(k_evac, g + (NG * p + 1))
                for t in range(TT):
                    last = pe.transpose(PS[:, 1, T + t * P:T + (t + 1) * P], vT[:, t * P:(t + 1) * P], ident[:, :])
                last.then_inc(v_turned, 1)

            def scores(p, g):
                if p == 0:
                    mm(bank(2, T), qab[:, 0, P:T], kab[:, 0, :], start=True, stop=True)
                    last = mm(bank(2, P, at=T), qab[:, 0, 0:P], kab[:, 0, 0:P], start=True, stop=True)
                elif p == 1:
                    mm(bank(2), kab[:, 0, 0:P], qab[:, :, :], start=True, stop=False, skip_group_check=True)
                    mm(PS[:, 2, :].rearrange("p (h t) -> p h t", h=2)[:, :, 0:P], identb[:, :],
                       mask0[:, :].unsqueeze(1).to_broadcast([P, 2, P]), start=False, stop=True, skip_group_check=True)
                    mm(bank(3, T), kab[:, 0, P:T], qab[:, :, P:T], start=True, stop=False, skip_group_check=True)
                    last = mm(bank(3, T).rearrange("p (h t) -> p h t", h=2), identb[:, :],
                              mask0[:, :].unsqueeze(1).to_broadcast([P, 2, P]), start=False, stop=True,
                              skip_group_check=True)
                else:
                    mm(bank(2), qab[:, 0, P:T], kab[:, :, :], start=True, stop=False, skip_group_check=True)
                    mm(PS[:, 2, :].rearrange("p (h t) -> p h t", h=2)[:, :, P:T], identb[:, :],
                       mask1[:, :].unsqueeze(1).to_broadcast([P, 2, P]), start=False, stop=True, skip_group_check=True)
                    mm(bank(3, T), qab[:, 0, 0:P], kab[:, :, 0:P], start=True, stop=False, skip_group_check=True)
                    last = mm(bank(3, T).rearrange("p (h t) -> p h t", h=2), identb[:, :],
                              mask1[:, :].unsqueeze(1).to_broadcast([P, 2, P]), start=False, stop=True,
                              skip_group_check=True)
                last.then_inc(sc_done, 1)

            def turn_probs(p, g):
                pe.wait_ge(prob_ready, g + (NG * (p // 2) + 1))
                if p == 0:
                    pe.transpose(bank(4, P, at=0), Pr[:, T:T + P], ident[:, :])
                    pe.transpose(bank(4, P, at=P), Pr[:, 0:P], ident[:, :])
                    last = pe.transpose(bank(4, P, at=T), Pr[:, P:T], ident[:, :])
                else:
                    for h in range(2):
                        pe.transpose(bank(4, P, at=h * T), Pr[:, 512 + h * P:512 + (h + 1) * P], ident[:, :])
                        pe.transpose(bank(4, P, at=h * T + P), Pr[:, h * T:h * T + P], ident[:, :])
                        last = pe.transpose(bank(5, P, at=h * P), Pr[:, h * T + P:(h + 1) * T], ident[:, :])
                last.then_inc(pt_turned, 1)

            def decay_sums(g):
                pe.wait_ge(sp_ready, g + 1)
                mm(bank(2), ltri[:, :], Pr[:, 0:512], start=False, stop=False, skip_group_check=True)
                mm(PS[:, 2, :].rearrange("p (h t) -> p h t", h=2)[:, :, P:T], ones[:, :],
                   Pr[:, 512:768].rearrange("p (h t) -> p h t", h=2), start=False, stop=True, skip_group_check=True)
                mm(bank(3, T), ltri[:, :], Pr[:, 512:768], start=False, stop=True,
                   skip_group_check=True).then_inc(r_done, 1)

            def values(p, g, s):
                if p == 1:
                    pe.wait_ge(at_ready, g + 1)
                else:
                    pe.wait_ge(pt_evac, g + (NG * (p // 2) + 1))
                pe.wait_ge(v_evac, g + (NG * p + 1))
                if not (p == 0 and isinstance(g, int) and g == 0):
                    pe.wait_ge(o_evac, g + NG * p)
                if p == 0:
                    mm(bank(6, T), V[:, s, 0, :], PT[:, 0:T], start=True, stop=False, skip_group_check=True)
                    last = mm(bank(6, P, at=P), V[:, s, 1, :], PT[:, T:T + P], start=False, stop=True,
                              skip_group_check=True)
                else:
                    for h in range(2):
                        r = slice(HD2 * h, HD2 * (h + 1))
                        mm(bank(6, T, r), V[:, s, 0, r], PT[:, h * T:(h + 1) * T], start=True, stop=False,
                           skip_group_check=True)
                        last = mm(bank(6, P, r, at=P), V[:, s, 1, r], PT[:, 512 + h * P:512 + (h + 1) * P],
                                  start=False, stop=True, skip_group_check=True)
                last.then_inc(pv_done, 1)

            def step(p, g, half, s, first):
                qkv(p, g, half, s)
                if not first:
                    if p == 1:
                        decay_sums(g - 1)
                    else:
                        turn_probs(p, g - 1)
                turn_v(p, g, s)
                if p == 1 and not first:
                    values(p, g - 1, 1 - s)
                scores(p, g)
                if p != 1 and not first:
                    values(p, g - 1, 1 - s)
            def attention(p):
                step(p, 0, 0, 0, True)
                step(p, 1, 0, 1, False)
                with pe.Fori(1, NG // 2) as i:
                    for s in range(2):
                        step(p, i * 2 + s, i, s, False)
                if p == 1:
                    decay_sums(NG - 1)
                else:
                    turn_probs(p, NG - 1)
                values(p, NG - 1, 1)
                pe.wait_ge(o_evac, NG * (p + 1))

            def modulation_gates(p):
                pe.wait_ge(mod_summed, NMB * (p + 1))
                for n, c in enumerate((4, 5, 10, 11)):
                    last = mm(bank(4 + n), ones[:, :], macc[:, c * HALF:(c + 1) * HALF], start=True, stop=True)
                last.then_inc(modfin_rows, 1)

            def modulation_columns(p, r):
                if r == 0:
                    pe.wait_ge(modfin_gates, p + 1)
                else:
                    pe.wait_ge(modfin_read, TT * p + 1)
                for n in range(16):
                    last = pe.transpose(bank(4 + n // 4, P, at=(n % 4) * P),
                                        macc[:, (24 * r + n) * P:(24 * r + n + 1) * P], ident[:, :])
                last.then_inc(modfin_turned, 1)

            def project_out(p):
                if p < 2:
                    modulation_gates(p)
                pe.wait_ge(wo_loaded, 16 * (p + 1))
                for t in range(TT):
                    for k in range(KD):
                        if t == 1 and p < 2 and k % 4 == 0:
                            modulation_columns(p, k // 4)
                        for n in range(2):
                            last = mm(bank(2 * t + n), OT[:, k, t * P:(t + 1) * P], wo_r[:, k, n * HALF:(n + 1) * HALF],
                                      start=(k == 0), stop=(k == KD - 1))
                    last.then_inc(y_done, 1)
                if p < 2:
                    pe.wait_ge(modfin_read, TT * (p + 1))

            def wait_columns(k):
                pe.wait_ge(xt_act, k + 1)
                pe.wait_ge(xt_dve, k + 1)

            def feed_forward(L):
                def gate_up(j, jh, s):
                    pe.wait_ge(ffn_w[s], jh * 32 + (32 * (FT // 2) * L + 32))
                    if not (L == 0 and isinstance(j, int) and j < 2):
                        pe.wait_ge(fact_ready, j + (FT * L - 1))
                    w = G[:, s, 0:2 * D].rearrange("p (c k n) -> p c k n", c=2, k=KD)
                    for c in range(2):
                        for k in range(KD):
                            last = mm(bank(4 + s, T, at=c * T), w[:, c, k, :], XT[:, k, :],
                                      start=(k == 0), stop=(k == KD - 1))
                    last.then_inc(fgu_done, 1)

                def down(j, jh, s, first=False, end=False):
                    pe.wait_ge(ffn_dw[s], jh * 16 + (16 * (FT // 2) * L + 16))
                    pe.wait_ge(fact_ready, j + (FT * L + 1))
                    for t in range(TT):
                        for n in range(2):
                            last = mm(bank(2 * t + n), aT[s][:, t * P:(t + 1) * P],
                                      G[:, s, 2 * D + n * HALF:2 * D + (n + 1) * HALF],
                                      start=first, stop=end, skip_group_check=True)
                        if end and t == 0:
                            last.then_inc(fy_done, 1)
                    last.then_inc(fdn_done, 1)

                gate_up(0, 0, 0)
                gate_up(1, 0, 1)
                down(0, 0, 0, first=True)
                with pe.Fori(1, FT // 2) as i:
                    gate_up(i * 2, i, 0)
                    down(i * 2 - 1, i - 1, 1)
                    gate_up(i * 2 + 1, i, 1)
                    down(i * 2, i, 0)
                down(FT - 1, FT // 2 - 1, 1, end=True)

            def routing():
                pe.wait_ge(rt_w, 32)
                for t in range(TT):
                    for k in range(KD):
                        last = mm(bank(4, E, at=t * E), XT[:, k, t * P:(t + 1) * P], w_rt[:, k, :],
                                  start=(k == 0), stop=(k == KD - 1))
                last.then_inc(rt_pe, 1)
                pe.wait_ge(rt_dve, 1)
                mm(bank(5, E), ustr[:, :], sel[:, 0, :], start=True, stop=True)
                mm(bank(5, E, at=E), ones[:, :], sel[:, 0, :], start=True, stop=False)
                mm(bank(5, E, at=E), ustr[:, :], sel[:, 1, :], start=False, stop=True)
                mm(bank(6, 1, slice(0, E)), sel[:, 0, :], ones[:, 0:1], start=True, stop=False)
                mm(bank(6, 1, slice(0, E)), sel[:, 1, :], ones[:, 0:1], start=False,
                   stop=True).then_inc(rt_pe, 1)
                pe.wait_ge(rt_dve, 2)
                mm(bank(7, 1, slice(0, E)), uinc[0:E, 0:E], cnt[0:E, 1:2], start=True, stop=True)
                for t in range(TT):
                    pe.transpose(bank(4, P, slice(0, E), at=t * P), posx[:, t, 0:E], ident[:, :])
                for t in range(TT):
                    last = pe.transpose(bank(4, P, slice(0, E), at=T + t * P), gatx[:, t, 0:E], ident[:, :])
                last.then_inc(rt_pe, 1)
                pe.wait_ge(rt_dve, 3)
                mm(bank(5, 17), ones[0:E, :], Aj[0:E, :], start=True, stop=True)
                mm(bank(5, 17, at=32), ones[0:E, :], EXj[0:E, :], start=True, stop=True)
                mm(bank(5, 1, at=64), ones[0:E, :], cnt[0:E, 1:2], start=True, stop=True)
                for t in range(TT):
                    mm(bank(6, 17, at=t * 17), posT[:, t * P:(t + 1) * P], IE[0:E, E:NIT], start=True, stop=True)
                    mm(bank(6, 17, at=64 + t * 17), gatT[:, t * P:(t + 1) * P], IE[0:E, E:NIT], start=True, stop=True)
                pe.wait_ge(b_gu_loaded, 16)
                for f in range(16):
                    mm(bank(f // 8, NIT, at=(f % 8) * NIT), b_gu_rows[:, f * P:(f + 1) * P], IE[0:E, 0:NIT],
                       start=True, stop=True)
                for t in range(TT):
                    for n in range(2):
                        last = mm(bank([2, 3, 4, 7][2 * t + n]), gatT[:, t * P:(t + 1) * P],
                                  b_dn_rows[:, n * HALF:(n + 1) * HALF], start=True, stop=True)
                last.then_inc(rt_pe, 1)
                pe.wait_ge(rt_dve, 4)

            def gather(j, first=False):
                pe.wait_ge(selx_ready, j + 1)
                if not first:
                    pe.wait_ge(selT_ev, j)
                for t in range(TT):
                    for n in range(2):
                        last = mm(bank(6, HALF, slice(CAP * n, CAP * (n + 1))), selx[:, t, :],
                                  XA[:, t, n * HALF:(n + 1) * HALF], start=(t == 0), stop=(t == 1))
                last.then_inc(gat_mm, 1)

            def turn_gathered(j):
                pe.wait_ge(xe_ev, j + 1)
                for c in range(4):
                    last = pe.transpose(bank(7, P, at=c * P), xe[:, c * P:(c + 1) * P], ident[:, :])
                last.then_inc(xe_turned, 1)

            def scatter(i):
                pe.wait_ge(y_ev, i + 1)
                pe.wait_ge(selT_ev, i + 1)
                for q, b in enumerate((4, 5, 0, 1)):
                    t, n = q // 2, q % 2
                    mm(bank(b), selT[:, t * P:(t + 1) * P], ysb[:, n * HALF:(n + 1) * HALF],
                       start=True, stop=True).then_inc(sc_mm, 1)

            def experts():
                pe.wait_ge(items_ready, 1)
                n_items = pe.value_load(items_i[0:1, NIT:NIT + 1], min_val=E, max_val=E + MAX_EXTRA)
                pe.wait_ge(zero_ready, 1)
                gather(0, first=True)
                turn_gathered(0)
                with pe.Fori(0, n_items) as i:
                    pe.wait_ge(xeT_ready, i + 1)
                    pe.wait_ge(acc_done, i * 4 + 1)
                    for k in range(KD):
                        pe.wait_ge(ew[k], i * 16 + 16)
                        for n in range(2):
                            for c in range(2):
                                last = mm(bank(n, HALF, slice(CAP * c, CAP * (c + 1))), xeT[:, k, :],
                                          slot[k][:, c * D + n * HALF:c * D + (n + 1) * HALF],
                                          start=(k == 0), stop=(k == KD - 1))
                        last.then_inc(ew_used, 1)
                    gather(i + 1)
                    pe.wait_ge(h_ev, i + 1)
                    for f in range(8):
                        last = pe.transpose(bank(2 + f // 4, P, at=(f % 4) * P), hsb[:, f * P:(f + 1) * P], ident[:, :])
                    last.then_inc(h_turned, 1)
                    scatter(i)
                    turn_gathered(i + 1)
                    pe.wait_ge(selg_ready, i + 1)
                    for t in range(TT):
                        last = pe.transpose(bank(6, P, at=t * P), selg[:, t, :], ident[:, :])
                    last.then_inc(selT_turned, 1)
                    pe.wait_ge(act_ready, i + 1)
                    pe.wait_ge(acc_done, i * 4 + 3)
                    for d in range(DN_SLOTS):
                        pe.wait_ge(ew[GU_SLOTS + d], i * 16 + 16)
                        for n in range(2):
                            for c in range(2):
                                last = mm(bank(4 + n, HALF, slice(CAP * c, CAP * (c + 1))), actT[:, 2 * d + c, :],
                                          slot[GU_SLOTS + d][:, c * D + n * HALF:c * D + (n + 1) * HALF],
                                          start=(d == 0), stop=(d == DN_SLOTS - 1))
                        last.then_inc(ew_used, 1)
                pe.wait_ge(acc_done, n_items * 4 + 1)
                scatter(n_items)

            def forget_gates():
                for t in range(TT):
                    for k in range(KD):
                        last = mm(bank(4, 16, at=t * 16), XT[:, k, t * P:(t + 1) * P], wfg[:, k, :],
                                  start=(k == 0), stop=(k == KD - 1))
                last.then_inc(flog_done, 1)
                pe.wait_ge(flog_dve, 2)
                mm(bank(5, 16), uinc[:, :], lf[:, 0, :], start=True, stop=True)
                mm(bank(5, 16, at=16), ones[:, :], lf[:, 0, :], start=True, stop=False)
                mm(bank(5, 16, at=16), uinc[:, :], lf[:, 1, :], start=False, stop=True)
                mm(bank(7, P, slice(0, 16)), lf[:, 0, :], uinc[:, :], start=True, stop=True)
                mm(bank(7, P, slice(0, 16), at=P), lf[:, 0, :], ones[:, :], start=True, stop=False)
                mm(bank(7, P, slice(0, 16), at=P), lf[:, 1, :], uinc[:, :], start=False,
                   stop=True).then_inc(cum_done, 1)

            pe.wait_ge(consts_ready, 1)
            pe.wait_ge(vrow_loaded, 16 * 11)
            for L in range(2):
                pe.transpose(bank(4, 64, at=L * 256), vrow[0:64, L, 0:P], ident[0:64, 0:64])
                last = pe.transpose(bank(4, 88, at=L * 256 + 64), vrow[0:88, L, P:2 * P], ident[0:88, 0:88])
            last.then_inc(vec_turned, 1)
            pe.wait_ge(silu_ready, 1)
            pe.transpose(bank(6, 8), vrow[0:8, 0, 2 * P:3 * P], ident[0:8, 0:8]).then_inc(cond_turned, 1)
            pe.wait_ge(cond_ready, 1)
            turn_rows(0)
            wait_columns(0)
            attention(0)
            project_out(0)
            turn_rows(1)
            wait_columns(1)
            routing()
            experts()
            for L in range(2):
                turn_rows(2 + 2 * L)
                wait_columns(2 + 2 * L)
                if L == 1:
                    forget_gates()
                attention(1 + L)
                project_out(1 + L)
                turn_rows(3 + 2 * L)
                wait_columns(3 + 2 * L)
                feed_forward(L)

        @blk.scalar
        def _(act):
            fn = act.activation
            act.dma_start(bias_src, a["rel_bias"].rearrange("b h -> h b"), allow_slow_non_contiguous=True)\
               .then_inc(rel_loaded, 16)
            for L in range(2):
                for lo, n, name in ((0, 48, "b_mod_2"), (48, 8, "g_mix_pre_2"), (56, 8, "g_ffn_pre_2")):
                    act.dma_start(vrow[lo:lo + n, L, 0:P], a[name][L].rearrange("(r n) -> r n", n=P))\
                       .then_inc(vrow_loaded, 16)
                act.dma_start(vrow[0:66, L, P:2 * P], a["w_conv_2"][L].rearrange("w (r n) -> (w r) n", n=P))\
                   .then_inc(vrow_loaded, 16)
                act.dma_start(vrow[66:88, L, P:2 * P], a["b_conv_2"][L].rearrange("(r n) -> r n", n=P))\
                   .then_inc(vrow_loaded, 16)
            act.dma_start(vrow[0:8, 0, 2 * P:3 * P], a["c_2"][0].rearrange("(r n) -> r n", n=P))\
               .then_inc(vrow_loaded, 16)
            act.dma_start(wfg[:, :, :], rows_of(a["w_fg_2"][0])).then_inc(small_loaded, 16)
            act.dma_start(LNC[:, 0, :], bcast(a["ln_g"][0, 0])).then_inc(lnc_loaded, 16)
            act.dma_start(LNC[:, 1, :], bcast(a["ln_b"][0, 0])).then_inc(lnc_loaded, 16)

            def modulation_rows(p):
                act.dma_start(bmod_rows[:, :, :], bcast(a["b_mod_2"][p].rearrange("(c n) -> c n", n=D)[2:6:3, :]))\
                   .then_inc(modvec_loaded, 16)
                act.dma_start(gtg[p][:, 0, :], bcast(a["g_mix_post_2"][p])).then_inc(modvec_loaded, 16)
                act.dma_start(gtg[p][:, 1, :], bcast(a["g_ffn_post_2"][p])).then_inc(modvec_loaded, 16)

            modulation_rows(0)
            act.wait_ge(vrow_loaded, 16 * 11)
            fn(vrow[0:8, 0, 2 * P:3 * P], vrow[0:8, 0, 2 * P:3 * P], ACT.Silu).then_inc(silu_ready, 1)
            act.wait_ge(bias_row_ready, 1)
            act.dma_start(bias_d, bias_row.unsqueeze(1).to_broadcast([8, P, 384])).then_inc(bias_written, 16)
            act.wait_ge(bias_written, 16)
            act.dma_start(bias_tiles, bass.AP(tensor=bias_d.tensor, offset=P - 1, ap=[[383, P], [P * 384, 8], [1, T]]))\
               .then_inc(bias_loaded, 16)

            def columns(k, scale=None, shift=None):
                for c in (0, 1, 4, 5):
                    act.wait_ge(xt_turned, 4 * k + c // 2 + 1)
                    src = PS[:, 4 + c // 2, (c % 2) * T:(c % 2 + 1) * T]
                    if scale is None:
                        last = fn(XT[:, c, :], src, ACT.Copy)
                    else:
                        last = fn(XT[:, c, :], src, ACT.Identity, bias=shift[:, c:c + 1], scale=scale[:, c:c + 1])
                last.then_inc(xt_act, 1)

            def evacuate(p, g):
                act.wait_ge(qkv_done, g + (NG * p + 1))
                if p == 1:
                    for h in range(2):
                        r = slice(HD2 * h, HD2 * (h + 1))
                        fn(qab[r, h, :], PS[r, 0, 0:T], ACT.Copy, scale=HD2 ** -0.5)
                else:
                    fn(qab[:, 0, :], PS[:, 0, 0:T], ACT.Copy, scale=(P if p == 0 else HD2) ** -0.5)
                fn(vT, PS[:, 0, T:2 * T], ACT.Copy).then_inc(qv_evac, 1)

            def softplus_tail(g):
                act.wait_ge(sc_done, g + (NG + 1))
                fn(Ssb, banks(2, 768), ACT.Abs)
                act.drain()
                fn(Ssb, Ssb, ACT.Exp, scale=-1.0)
                act.drain()
                fn(Ssb, Ssb, ACT.Ln, bias=1.0).then_inc(lnp_ready, 1)

            def weights_from_sums(g):
                act.wait_ge(r_done, g + 1)
                fn(PT, banks(2, 768), ACT.Exp, scale=-1.0).then_inc(at_ready, 1)

            def softmax_exp(p, g):
                act.wait_ge(max_ready, g + (NG * (p // 2) + 1))
                segs = ((0, T), (T, P)) if p == 0 else ((0, T), (T, T), (512, P), (640, P))
                for n, (lo, w) in enumerate(segs):
                    last = fn(Pr[:, lo:lo + w], Ssb[:, lo:lo + w], ACT.Exp, bias=nmx[:, n:n + 1],
                              accum_out=psum_l[:, n:n + 1])
                last.then_inc(exp_ready, 1)

            def turned_probs(p, g):
                act.wait_ge(pt_turned, g + (NG * (p // 2) + 1))
                w = 384 if p == 0 else 768
                fn(PT[:, 0:w], banks(4, w), ACT.Copy).then_inc(pt_evac, 1)



            def step(p, g, first):
                evacuate(p, g)
                if not first:
                    if p == 1:
                        weights_from_sums(g - 1)
                    else:
                        turned_probs(p, g - 1)
                if p == 1:
                    softplus_tail(g)
                else:
                    softmax_exp(p, g)

            def attention(p):
                step(p, 0, True)
                with act.Fori(1, NG) as g:
                    step(p, g, False)
                if p == 1:
                    weights_from_sums(NG - 1)
                else:
                    turned_probs(p, NG - 1)

            def squares(src, *ready):
                for t in range(TT):
                    act.wait_ge(*ready[t])
                    fn(junk[t], src(t), ACT.Square, accum_out=ssq[:, t:t + 1]).then_inc(ssq_ready, 1)

            def product(t):
                return banks(2 * t, D)

            def x_row(t):
                return XA[:, t, :]

            columns(0)
            attention(0)
            columns(1)
            act.dma_start(br, bcast(a["moe_b_router"][0])).then_inc(small_loaded, 16)
            act.wait_ge(rt_dve, 1)
            for t in range(TT):
                last = fn(ex[:, t, :], lg[:, t, :], ACT.Exp, bias=nmx[:, t:t + 1])
            last.then_inc(rt_act, 1)
            act.wait_ge(xn_ready, TT)
            act.dma_start(LNC[:, 0, :], bcast(a["ln_g"][0, 1])).then_inc(lnc_loaded, 16)
            act.dma_start(LNC[:, 1, :], bcast(a["ln_b"][0, 1])).then_inc(lnc_loaded, 16)
            act.wait_ge(items_ready, 1)
            n_items = act.value_load(items_i[0:1, NIT:NIT + 1], min_val=E, max_val=E + MAX_EXTRA)

            def gathered(j):
                act.wait_ge(gat_mm, j + 1)
                fn(xe, bank(6), ACT.Copy).then_inc(xe_ev, 1)

            act.wait_ge(zero_ready, 1)
            fn(psum_l[:, 0:1], ident[:, 0:1], ACT.Copy).then_inc(y_ev, 1)
            fn(psum_l[:, 1:2], ident[:, 0:1], ACT.Copy).then_inc(selT_ev, 1)
            gathered(0)
            with act.Fori(0, n_items) as i:
                act.wait_ge(ew_used, i * SLOTS + GU_SLOTS)
                fn(hsb, banks(0, D), ACT.Copy).then_inc(h_ev, 1)
                gathered(i + 1)
                act.wait_ge(g_ready, i + 1)
                fn(ss_b, gs_b, ACT.Sigmoid, scale=SWIGLU_ALPHA).then_inc(sg_ready, 1)
                act.wait_ge(selT_turned, i + 1)
                fn(selT, bank(6, T), ACT.Copy).then_inc(selT_ev, 1)
                act.wait_ge(ew_used, i * SLOTS + SLOTS)
                fn(ysb, banks(4, D), ACT.Copy).then_inc(y_ev, 1)
            for L in range(2):
                squares(x_row, (x_updated, 4 * L + 1), (x_updated, 4 * L + 2))
                columns(2 + 2 * L, gsc[:, L, 0:8], shc[:, L, 0:8])
                if L == 0:
                    act.wait_ge(xt_dve, 3)
                    act.wait_ge(ew_used, n_items * SLOTS)
                    modulation_rows(1)
                if L == 1:
                    act.dma_start(bfg, bcast(a["b_fg_2"][0])).then_inc(small_loaded, 16)
                    act.wait_ge(flog_dve, 1)
                    fn(lfb, lf, ACT.Abs)
                    act.drain()
                    fn(lfb, lfb, ACT.Exp, scale=-1.0)
                    act.drain()
                    fn(lfb, lfb, ACT.Ln, bias=1.0).then_inc(flog_act, 1)
                    act.wait_ge(ncum_ready, 1)
                    act.dma_start(cum_d, ncumR).then_inc(ncum_written, 16)
                    act.wait_ge(ncum_written, 16)
                    act.dma_start(ncum_b, bcast(cum_d)).then_inc(ncum_loaded, 16)
                attention(1 + L)
                squares(product, (y_done, 2 * L + 3), (y_done, 2 * L + 4))
                squares(x_row, (x_updated, 4 * L + 3), (x_updated, 4 * L + 4))
                columns(3 + 2 * L, gsc[:, L, 8:16], shc[:, L, 8:16])
                with act.Fori(0, FT // 2) as i:
                    for s in range(2):
                        act.wait_ge(cv_ready, i * 2 + (FT * L + s + 1))
                        fn(sl[s], cv[s], ACT.Silu).then_inc(sl_ready, 1)
                squares(product, (fy_done, L + 1), (fdn_done, FT * (L + 1)))

        @blk.vector
        def _(dve):
            tt, ts, stt = dve.tensor_tensor, dve.tensor_scalar, dve.scalar_tensor_tensor

            def columns(k, scale=None, shift=None):
                for c in (2, 3, 6, 7):
                    dve.wait_ge(xt_turned, 4 * k + c // 2 + 1)
                    src = PS[:, 4 + c // 2, (c % 2) * T:(c % 2 + 1) * T]
                    if scale is None:
                        last = dve.tensor_copy(XT[:, c, :], src)
                    else:
                        last = ts(XT[:, c, :], src, scale[:, c:c + 1], shift[:, c:c + 1], ALU.mult, ALU.add)
                last.then_inc(xt_dve, 1)

            def evacuate(p, g):
                dve.wait_ge(qkv_done, g + (NG * p + 1))
                if p == 2:
                    for h in range(2):
                        r = slice(HD2 * h, HD2 * (h + 1))
                        last = dve.tensor_copy(kab[r, h, :], PS[r, 1, 0:T])
                elif p == 1:
                    last = ts(kab[:, 0, :], PS[:, 1, 0:T], -1.0, None, ALU.mult)
                else:
                    last = dve.tensor_copy(kab[:, 0, :], PS[:, 1, 0:T])
                last.then_inc(k_evac, 1)

            def value_rows(p, g, s):
                dve.wait_ge(v_turned, g + (NG * p + 1))
                dve.tensor_copy(V[:, s, :, :], PS[:, 1, T:2 * T].rearrange("p (t d) -> p t d", t=2))\
                   .then_inc(v_evac, 1)

            def softplus_sum(g):
                dve.wait_ge(lnp_ready, g + 1)
                stt(Pr, banks(2, 768), 0.0, Ssb, ALU.min, ALU.subtract, reverse1=True).then_inc(sp_ready, 1)

            def softmax(p, g):
                dve.wait_ge(sc_done, g + (NG * p + 1))
                if p == 0:
                    tt(Ssb[:, 0:T], bank(2, T), bias_tiles[:, ds(g, 1), :].squeeze(1), ALU.add)
                    tt(Ssb[:, T:384], bank(2, P, at=T), bias_tiles[:, ds(g, 1), P:T].squeeze(1), ALU.add)
                    dve.drain()
                    dve.tensor_reduce(nmx[:, 0:1], Ssb[:, 0:T], AX_X, ALU.max, negate=True)
                    dve.tensor_reduce(nmx[:, 1:2], Ssb[:, T:384], AX_X, ALU.max, negate=True).then_inc(max_ready, 1)
                    n = 2
                else:
                    for t, at, w, wk in ((1, 0, T, T), (0, 512, P, P)):
                        for h in range(2):
                            lo = at + h * w
                            stt(Ssb[:, lo:lo + w], banks(2, 768)[:, lo:lo + w], cumT[:, t, ds(g * 2 + h, 1)],
                                ncum_b[:, ds(g * 2 + h, 1), 0:wk].squeeze(1), ALU.add, ALU.add)
                    dve.drain()
                    dve.tensor_reduce(nmx[:, 0:2], Ssb[:, 0:512].rearrange("p (h t) -> p h t", h=2), AX_X, ALU.max,
                                      negate=True)
                    dve.tensor_reduce(nmx[:, 2:4], Ssb[:, 512:768].rearrange("p (h t) -> p h t", h=2), AX_X, ALU.max,
                                      negate=True).then_inc(max_ready, 1)
                    n = 4
                dve.wait_ge(exp_ready, g + (NG * (p // 2) + 1))
                dve.reciprocal(rcp[:, 0:n], psum_l[:, 0:n])
                dve.drain()
                segs = ((0, T), (T, P)) if p == 0 else ((0, T), (T, T), (512, P), (640, P))
                for k, (lo, w) in enumerate(segs):
                    last = ts(Pr[:, lo:lo + w], Pr[:, lo:lo + w], rcp[:, k:k + 1], None, ALU.mult)
                last.then_inc(prob_ready, 1)

            def heads_out(p, g):
                dve.wait_ge(pv_done, g + (NG * p + 1))
                dve.tensor_copy(OT[:, ds(g, 1), :].squeeze(1), bank(6, T)).then_inc(o_evac, 1)

            def modulation(p, g, r):
                dve.wait_ge(mod_w[r], g * 16 + (16 * (NMB // 2) * p + 16))
                w, acc = mstream[r], bank(5 + 2 * r, MB)
                ts(acc, w[:, 0, :], cc[:, 0:1], None, ALU.mult)
                dve.drain()
                for k in range(1, KD - 1):
                    stt(acc, w[:, k, :], cc[:, k:k + 1], acc, ALU.mult, ALU.add)
                    dve.drain()
                stt(macc[:, ds(g * (2 * MB) + r * MB, MB)], w[:, KD - 1, :], cc[:, KD - 1:KD], acc,
                    ALU.mult, ALU.add).then_inc(mod_summed, 1)

            def step(p, g, s, first):
                evacuate(p, g)
                value_rows(p, g, s)
                if p == 1 and not first:
                    heads_out(p, g - 1)
                if p == 1:
                    modulation(p, g, 0)
                    softplus_sum(g)
                else:
                    softmax(p, g)
                if p != 1 and not first:
                    heads_out(p, g - 1)
                if p == 0:
                    modulation(p, g, 0)
                if p < 2:
                    modulation(p, g, 1)

            def attention(p):
                step(p, 0, 0, True)
                step(p, 1, 1, False)
                with dve.Fori(1, NG // 2) as i:
                    for s in range(2):
                        step(p, i * 2 + s, s, False)
                heads_out(p, NG - 1)

            def modulation_gates(p):
                dve.wait_ge(modvec_loaded, 48 * (p + 1))
                dve.wait_ge(modfin_rows, p + 1)
                for k in range(2):
                    tt(banks(4 + 2 * k, D), banks(4 + 2 * k, D), bmod_rows[:, k, :], ALU.add)
                dve.drain()
                for k in range(2):
                    last = tt(gtg[p][:, k, :], banks(4 + 2 * k, D), gtg[p][:, k, :], ALU.mult)
                last.then_inc(modfin_gates, 1)

            def modulation_columns(p, r):
                dve.wait_ge(modfin_turned, TT * p + r + 1)
                for b in range(4):
                    last = dve.tensor_reduce(modc[:, 4 * b:4 * b + 4], bank(4 + b).rearrange("p (c q) -> p c q", c=4),
                                             AX_X, ALU.add)
                last.then_inc(modfin_read, 1)
                dve.drain()
                tt(shc[:, p, 8 * r:8 * r + 8], modc[:, 0:8], vcol[:, p, 24 * r:24 * r + 8], ALU.add)
                tt(modc[:, 8:16], modc[:, 8:16], vcol[:, p, 24 * r + 8:24 * r + 16], ALU.add)
                dve.drain()
                stt(gsc[:, p, 8 * r:8 * r + 8], modc[:, 8:16], 1.0, vcol[:, p, 48 + 8 * r:56 + 8 * r],
                    ALU.add, ALU.mult)

            def layer_norm_stats(t, source):
                y = banks(2 * t, D)
                stt(y, XA[:, t, :], ALPHA, source, ALU.mult, ALU.add)
                dve.drain()
                for h in range(2):
                    dve.bn_stats(bst[:, t, h, :], y[:, h * HALF:(h + 1) * HALF])
                dve.drain()
                dve.bn_aggr(mv[:, t, :], bst[:, t, :, :]).then_inc(var_ready, 1)

            def layer_norm_apply(k, t):
                y = banks(2 * t, D)
                dve.wait_ge(lnc_loaded, 32 * (k + 1))
                dve.drain()
                stt(y, y, mv[:, t, 0:1], LNC[:, 0, :], ALU.subtract, ALU.mult)
                dve.drain()
                dve.wait_ge(rstd_ready, TT * k + t + 1)
                return stt(XA[:, t, :], y, rstd[:, t:t + 1], LNC[:, 1, :], ALU.mult, ALU.add)

            def normed_rows(n, t):
                dve.wait_ge(rstd_ready, TT * n + t + 1)
                ts(YB[:, t, :], XA[:, t, :], rstd[:, t:t + 1], None, ALU.mult).then_inc(xn_ready, 1)

            def add_normed(n, t, g):
                y = banks(2 * t, D)
                dve.wait_ge(rstd_ready, TT * n + t + 1)
                stt(y, y, rstd[:, t:t + 1], g, ALU.mult, ALU.mult)
                dve.drain()
                tt(XA[:, t, :], XA[:, t, :], y, ALU.add).then_inc(x_updated, 1)

            tmp_inc = rcp[:, 3:4]
            dve.wait_ge(rel_loaded, 16)
            starts = bucket_starts()
            for b in range(BUCKETS):
                lo, hi = starts[b], starts[b + 1]
                dve.tensor_copy(bias_row[:, T - hi:T - lo], bias_src[:, b:b + 1].to_broadcast([8, hi - lo]))
            dve.memset(bias_row[:, T:384], NEG)
            dve.drain()
            dve.memset(st[0:8, 47:48], 0.0).then_inc(bias_row_ready, 1)
            dve.wait_ge(vec_turned, 1)
            for L in range(2):
                dve.tensor_copy(vcol[:, L, :], bank(4, 152, at=L * 256))
            dve.wait_ge(cond_turned, 1)
            dve.tensor_copy(cc[:, :], bank(6, KD)).then_inc(cond_ready, 1)
            dve.wait_ge(bias_row_ready, 1)
            columns(0)
            dve.wait_ge(bias_loaded, 16)
            attention(0)
            modulation_gates(0)
            for t in range(TT):
                modulation_columns(0, t)
                dve.wait_ge(y_done, t + 1)
                layer_norm_stats(t, banks(2 * t, D))
                layer_norm_apply(0, t).then_inc(xn_ready, 1)
            columns(1)
            dve.wait_ge(rt_pe, 1)
            dve.wait_ge(small_loaded, 32)
            tt(lg, bank(4, 64).rearrange("p (t e) -> p t e", t=2), br.unsqueeze(1).to_broadcast([P, 2, E]), ALU.add)
            dve.drain()
            for t in range(TT):
                dve.max(m8[:, t, :], lg[:, t, :])
            dve.drain()
            for t in range(TT):
                ts(nmx[:, t:t + 1], m8[:, t, 0:1], -1.0, None, ALU.mult)
                ts(gtm[:, t, :], lg[:, t, :], m8[:, t, 3:4], None, ALU.is_gt)
                ts(eqm[:, t, :], lg[:, t, :], m8[:, t, 3:4], None, ALU.is_equal)
            dve.drain()
            for t in range(TT):
                dve.tensor_reduce(rcp[:, t:t + 1], gtm[:, t, :], AX_X, ALU.add)
            dve.drain()
            for t in range(TT):
                dve.tensor_tensor_scan(csm[:, t, :], ones[:, 0:E], eqm[:, t, :], rcp[:, t:t + 1], ALU.mult, ALU.add)
            dve.drain()
            for t in range(TT):
                stt(csm[:, t, :], csm[:, t, :], float(TOPK), eqm[:, t, :], ALU.is_le, ALU.mult)
            dve.drain()
            tt(sel, csm, gtm, ALU.add)
            dve.drain()
            dve.memset(tmp_inc, 0.0).then_inc(rt_dve, 1)
            dve.wait_ge(rt_act, 1)
            tt(ex, ex, sel, ALU.mult)
            dve.drain()
            dve.tensor_reduce(rcp[:, 0:2], ex, AX_X, ALU.add)
            dve.drain()
            dve.reciprocal(rcp[:, 0:2], rcp[:, 0:2])
            dve.drain()
            for t in range(TT):
                ts(gatx[:, t, 0:E], ex[:, t, :], rcp[:, t:t + 1], None, ALU.mult)
            dve.wait_ge(rt_pe, 2)
            stt(posx[:, :, 0:E], bank(5, 64).rearrange("p (t e) -> p t e", t=2), 1.0, sel, ALU.add, ALU.mult)
            dve.tensor_copy(cnt[0:E, 0:1], bank(6, 1, slice(0, E)))
            dve.drain()
            ts(posx[:, :, 0:E], posx[:, :, 0:E], -1.0, None, ALU.add)
            ts(cnt[0:E, 1:2], cnt[0:E, 0:1], float(CAP), None, ALU.is_gt)
            ts(cnt[0:E, 2:3], cnt[0:E, 0:1], float(2 * CAP), None, ALU.is_gt)
            ts(cnt[0:E, 3:4], cnt[0:E, 0:1], float(3 * CAP), None, ALU.is_gt)
            dve.drain()
            tt(cnt[0:E, 1:2], cnt[0:E, 1:2], cnt[0:E, 2:3], ALU.add)
            dve.drain()
            tt(cnt[0:E, 1:2], cnt[0:E, 1:2], cnt[0:E, 3:4], ALU.add)
            dve.drain()
            dve.memset(tmp_inc, 0.0).then_inc(rt_dve, 1)
            dve.wait_ge(rt_pe, 3)
            dve.tensor_copy(cnt[0:E, 4:5], bank(7, 1, slice(0, E)))
            dve.tensor_copy(posT, bank(4, T, slice(0, E)))
            dve.tensor_copy(gatT, bank(4, T, slice(0, E), at=T))
            dve.tensor_copy(IE[0:E, 0:E], ident[0:E, 0:E])
            dve.drain()
            tt(cnt[0:E, 5:6], cnt[0:E, 4:5], cnt[0:E, 1:2], ALU.subtract)
            ts(Aj[0:E, :], iotaj[0:E, :], cnt[0:E, 4:5], None, ALU.is_ge)
            dve.drain()
            ts(IE[0:E, E:NIT], iotaj[0:E, :], cnt[0:E, 5:6], None, ALU.is_ge)
            dve.drain()
            tt(IE[0:E, E:NIT], IE[0:E, E:NIT], Aj[0:E, :], ALU.subtract)
            dve.drain()
            ts(EXj[0:E, :], IE[0:E, E:NIT], cnt[0:E, 5:6], None, ALU.mult)
            dve.drain()
            dve.memset(tmp_inc, 0.0).then_inc(rt_dve, 1)
            dve.wait_ge(rt_pe, 4)
            ts(itf[:, 0:E], iota64[:, 0:E], 0.0, None, ALU.add)
            ts(itf[:, E:NIT], bank(5, 17), float(E - 1), None, ALU.min)
            ts(itf[:, NIT:NIT + 1], bank(5, 1, at=64), float(E), None, ALU.add)
            tt(csm[:, 0, 0:17], iotaj[:, :], bank(5, 17, at=32), ALU.subtract)
            dve.drain()
            ts(csm[:, 0, 0:17], csm[:, 0, 0:17], float(CAP), float(CAP), ALU.mult, ALU.add)
            dve.tensor_copy(items_i[0:1, :], itf[0:1, :]).then_inc(items_ready, 1)
            dve.drain()
            for t in range(TT):
                tt(posx[:, t, E:NIT], bank(6, 17, at=t * 17), csm[:, 0, 0:17], ALU.subtract)
                dve.tensor_copy(gatx[:, t, E:NIT], bank(6, 17, at=64 + t * 17))
            for f2 in range(2):
                dve.tensor_copy(bguT[:, :, 8 * f2:8 * f2 + 8].rearrange("p i f -> p f i"),
                                bank(f2, 8 * NIT).rearrange("p (f i) -> p f i", f=8))
            for q, b in enumerate((2, 3, 4, 7)):
                dve.tensor_copy(YB[:, q // 2, (q % 2) * HALF:(q % 2 + 1) * HALF], bank(b))
            dve.memset(ysb, 0.0)
            dve.memset(selT, 0.0)
            dve.drain()
            dve.memset(tmp_inc, 0.0).then_inc(rt_dve, 1)
            dve.memset(nmx[:, 2:3], 0.0).then_inc(zero_ready, 1)
            dve.memset(nmx[:, 3:4], 0.0).then_inc(acc_done, 1)
            dve.wait_ge(items_ready, 1)
            n_items = dve.value_load(items_i[0:1, NIT:NIT + 1], min_val=E, max_val=E + MAX_EXTRA)

            def choose(j):
                for t in range(TT):
                    last = ts(selx[:, t, :], iota64[:, :], posx[:, t, ds(j, 1)], None, ALU.is_equal)
                last.then_inc(selx_ready, 1)

            def gathered_columns(j):
                dve.wait_ge(xe_turned, j + 1)
                dve.tensor_copy(xeT.rearrange("p (h c) s -> p c h s", h=2),
                                bank(7).rearrange("p (c h s) -> p c h s", c=4, h=2)).then_inc(xeT_ready, 1)

            def accumulate(i):
                for q, b in enumerate((4, 5, 0, 1)):
                    t, n = q // 2, q % 2
                    dve.wait_ge(sc_mm, i * 4 + (q + 1))
                    y = YB[:, t, n * HALF:(n + 1) * HALF]
                    tt(y, y, bank(b), ALU.add).then_inc(acc_done, 1)

            choose(0)
            gathered_columns(0)
            with dve.Fori(0, n_items) as i:
                dve.wait_ge(gat_mm, i + 1)
                choose(i + 1)
                dve.wait_ge(selT_ev, i + 1)
                for t in range(TT):
                    for h in range(2):
                        last = ts(selg[:, t, h * CAP:(h + 1) * CAP], iota64[:, :], posx[:, t, ds(i, 1)],
                                  gatx[:, t, ds(i, 1)], ALU.is_equal, ALU.mult)
                last.then_inc(selg_ready, 1)
                dve.wait_ge(h_turned, i + 1)
                hT = banks(2, D).rearrange("p (f c s) -> p f c s", f=8, c=2)
                bg = bguT[:, ds(i, 1), :].squeeze(1)
                tt(gs_b, hT[:, :, 0, :], bg[:, 0:8].unsqueeze(2).to_broadcast([P, 8, CAP]), ALU.add)
                tt(us_b, hT[:, :, 1, :], bg[:, 8:16].unsqueeze(2).to_broadcast([P, 8, CAP]), ALU.add)
                dve.drain()
                ts(gs_b, gs_b, LIMIT, None, ALU.min).then_inc(g_ready, 1)
                ts(us_b, us_b, LIMIT, -LIMIT, ALU.min, ALU.max)
                dve.drain()
                stt(us_b, us_b, 1.0, gs_b, ALU.add, ALU.mult)
                dve.drain()
                dve.wait_ge(sg_ready, i + 1)
                tt(actT, us_b, ss_b, ALU.mult).then_inc(act_ready, 1)
                accumulate(i)
                gathered_columns(i + 1)
            accumulate(n_items)
            dve.drain()
            for t in range(TT):
                layer_norm_stats(t, YB[:, t, :])
                layer_norm_apply(1, t).then_inc(x_updated, 1)
            for L in range(2):
                for t in range(TT):
                    normed_rows(2 + 4 * L, t)
                if L == 0:
                    dve.memset(qab, 0.0)
                else:
                    dve.memset(kab, 0.0)
                columns(2 + 2 * L, gsc[:, L, 0:8], shc[:, L, 0:8])
                if L == 1:
                    dve.wait_ge(small_loaded, 48)
                    dve.wait_ge(flog_done, 1)
                    tt(lf, bank(4, 32).rearrange("p (t h) -> p t h", t=2),
                       bfg.unsqueeze(1).to_broadcast([P, 2, 16]), ALU.add)
                    dve.drain()
                    dve.memset(tmp_inc, 0.0).then_inc(flog_dve, 1)
                    dve.wait_ge(flog_act, 1)
                    stt(lf, lf, 0.0, lfb, ALU.min, ALU.subtract).then_inc(flog_dve, 1)
                    dve.wait_ge(cum_done, 1)
                    dve.tensor_copy(cumT, bank(5, 32).rearrange("p (t h) -> p t h", t=2))
                    ts(ncumR, bank(7, T, slice(0, 16)), -1.0, None, ALU.mult).then_inc(ncum_ready, 1)
                    dve.wait_ge(ncum_loaded, 16)
                attention(1 + L)
                if L == 0:
                    modulation_gates(1)
                for t in range(TT):
                    if L == 0:
                        modulation_columns(1, t)
                    if t == 1:
                        normed_rows(4 + 4 * L, 0)
                    add_normed(3 + 4 * L, t, gtg[L][:, 0, :])
                normed_rows(4 + 4 * L, 1)
                columns(3 + 2 * L, gsc[:, L, 8:16], shc[:, L, 8:16])

                def ffn_tile(j, s, w):
                    dve.wait_ge(fgu_done, j + (FT * L + 1))
                    gate = bank(4 + s, T)
                    col = lambda r: vcol[:, L, ds(j + (64 + r * FT), 1)]
                    ts(cv[s], gate, col(2), col(3), ALU.mult, ALU.add)
                    dve.drain()
                    stt(cv[s][:, 1:T], gate[:, 0:T - 1], col(1), cv[s][:, 1:T], ALU.mult, ALU.add)
                    dve.drain()
                    stt(cv[s][:, 2:T], gate[:, 0:T - 2], col(0), cv[s][:, 2:T], ALU.mult, ALU.add)\
                        .then_inc(cv_ready, 1)
                    dve.wait_ge(sl_ready, j + (FT * L + 1))
                    if w:
                        dve.wait_ge(fdn_done, j + (FT * L - 1))
                    tt(aT[s], sl[s], bank(4 + s, T, at=T), ALU.mult).then_inc(fact_ready, 1)

                for s in range(2):
                    ffn_tile(s, s, False)
                with dve.Fori(1, FT // 2) as i:
                    for s in range(2):
                        ffn_tile(i * 2 + s, s, True)
                for t in range(TT):
                    add_normed(5 + 4 * L, t, gtg[L][:, 1, :])


_INS = ["x", "rel_bias", "a_w_in", "a_w_out", "ln_g", "ln_b", "moe_w_router", "moe_b_router", "moe_w_gate_up",
        "moe_b_gate_up", "moe_w_down", "moe_b_down", "c_2", "w_mod_2", "b_mod_2", "g_mix_pre_2", "g_mix_post_2",
        "w_qkv_2", "w_o_2", "w_fg_2", "b_fg_2", "g_ffn_pre_2", "g_ffn_post_2", "w_ffn_gate_2", "w_ffn_up_2",
        "w_conv_2", "b_conv_2", "w_ffn_down_2"]


def kernel(**inputs):
    import concourse.bacc as _bacc
    from concourse.bass_utils import run_bass_kernel_spmd as _run

    nc = _bacc.Bacc("TRN2", target_bir_lowering=False, num_devices=1)
    arrays, args = {}, {}
    for name in _INS:
        x = np.ascontiguousarray(inputs[name])
        arrays[f"in_{name}"] = x
        args[name] = nc.dram_tensor(f"in_{name}", x.shape, mybir.dt.from_np(x.dtype), kind="ExternalInput").ap()
    out = nc.dram_tensor("out_0", (1, T, D), F32, kind="ExternalOutput").ap()
    block_kernel(nc, args, out)
    r = _run(nc, [arrays], core_ids=[0])
    return r.results[0]["out_0"]
```

```python
from contextlib import ExitStack

import numpy as np

import concourse.bass as bass
from concourse import mybir

F32 = mybir.dt.float32
F32R = mybir.dt.float32r
BF16 = mybir.dt.bfloat16
I32 = mybir.dt.int32
ALU = mybir.AluOpType
ACT = mybir.ActivationFunctionType
AX_X = mybir.AxisListType.X

P = 128
T = 256
TT = T // P
D = 1024
KD = D // P
HALF = 512
NG = D // P
HD2 = 64
E = 32
TOPK = 4
CAP = 64
MAX_EXTRA = 16
NIT = E + MAX_EXTRA + 1
F = 2816
FT = F // P
BUCKETS = 32
MAX_DIST = 128
ALPHA = 2.0 ** 0.25
LN_EPS = 1e-5
RMS_EPS = 1e-6
LIMIT = 7.0
SWIGLU_ALPHA = 1.702
NEG = -1e30
MODW = 6 * D
MB = 384
NMB = MODW // MB

R_WO, R_ACC, R_STREAM, R_GTG1, R_BMOD = 0, 8192, 14336, 20480, 22528
SLOT = 2048
GU_SLOTS, DN_SLOTS = 8, 4
SLOTS = GU_SLOTS + DN_SLOTS
V_BANK = (3, 4, 7)


def bucket_starts():
    exact = BUCKETS // 2
    n = np.arange(T)
    large = exact + (np.log(np.maximum(n, 1).astype(np.float32) / exact)
                     / np.float32(np.log(MAX_DIST / exact)) * (BUCKETS - exact)).astype(np.int32)
    b = np.where(n < exact, n, np.minimum(large, BUCKETS - 1))
    return [int(np.argmax(b == k)) for k in range(BUCKETS)] + [T]


def block_kernel(nc, a, out):
    with ExitStack() as ctx:
        def sb(name, shape, dt=F32):
            return ctx.enter_context(nc.sbuf_tensor(name, shape, dt))

        def sem(name):
            return ctx.enter_context(nc.semaphore(name))

        ds = bass.ds


        G = sb("group_weights", [P, 2, 3 * D])
        XA = sb("x_rows", [P, TT, D])
        YB = sb("y_rows", [P, TT, D])
        XT = sb("x_cols", [P, KD, T])
        OT = sb("att_cols", [P, KD, T])
        SC = sb("scratch", [P, 8192])
        LNC = sb("ln_consts", [P, 2, D])
        GTG0 = sb("gate_gain0", [P, 2, D])
        ident = sb("ident", [P, P])
        ones = sb("ones", [P, P])
        ltri = sb("ltri", [P, P])
        ustr = sb("ustrict", [P, P])
        uinc = sb("uinc", [P, P])

        identb = sb("identb", [P, P], BF16)
        mask0 = sb("mask_strict", [P, P], BF16)
        mask1 = sb("mask_causal", [P, P], BF16)
        iota64 = sb("iota64", [P, CAP])
        iotaj = sb("iotaj", [P, MAX_EXTRA + 1])
        cc = sb("cond_cols", [P, KD])
        vcol = sb("vec_cols", [P, 2, 152])
        modc = sb("mod_cols", [P, 32])
        shc = sb("shift_cols", [P, 2, 16])
        gsc = sb("scale_cols", [P, 2, 16])
        wfg = sb("w_fg", [P, KD, 16])
        st = sb("stats", [P, 48])
        items_i = sb("items", [1, NIT + 1], I32)
        with nc.sbuf_tensor("big", [P, SLOTS * SLOT], F32) as R:
            pass
        dhi, dlo = ([sb(f"down_split{2 * n + s}", [P, D]) for s in range(2)] for n in range(2))
        acts = [sb(f"act_split{s}", [P, 2, T]) for s in range(2)]
        sb("big_before_splits", [P, R_ACC - 4 * D - 4 * T])
        xs = sb("x_split", [P, KD, 2, T])
        wlo1, wlo0, whi0, whi1 = (sb(f"w_split{n}", [P, 2 * D]) for n in range(4))
        whi, wlo = [whi0[:, :], whi1[:, :]], [wlo0[:, :], wlo1[:, :]]
        sb("big_after_splits", [P, SLOTS * SLOT - R_ACC - 2 * KD * T - 8 * D])
        PS = ctx.enter_context(nc.psum_tensor("ps", [P, 8, HALF], F32))

        wo_r = R[:, R_WO:R_WO + 8 * D].rearrange("p (k n) -> p k n", k=KD)
        macc = R[:, R_ACC:R_ACC + MODW]
        mstream = [R[:, R_STREAM + s * KD * MB:R_STREAM + (s + 1) * KD * MB].rearrange("p (k n) -> p k n", k=KD)
                   for s in range(2)]
        gtg = [GTG0[:, :, :], R[:, R_GTG1:R_GTG1 + 2 * D].rearrange("p (a n) -> p a n", a=2)]
        bmod_rows = R[:, R_BMOD:R_BMOD + 2 * D].rearrange("p (a n) -> p a n", a=2)

        slot = [R[:, s * SLOT:(s + 1) * SLOT] for s in range(SLOTS)]

        def part(at, n):
            return SC[:, at:at + n]

        qab = part(0, 512).rearrange("p (h t) -> p h t", h=2)
        kab = part(512, 512).rearrange("p (h t) -> p h t", h=2)
        vT = part(1024, 256)
        V = part(1280, 512).rearrange("p (b s d) -> p b s d", b=2, s=2)
        Ssb = part(1792, 768)
        Pr = part(2560, 768)
        PT = part(3328, 768)
        bias_tiles = part(4096, 2048).rearrange("p (h c) -> p h c", h=8)
        ncum_b = part(4096, 4096).rearrange("p (h t) -> p h t", h=16)
        xeT = part(0, 512).rearrange("p (k s) -> p k s", k=KD)
        xe = part(1024, 512)
        hsb = part(1536, 1024)
        gs_b = part(2560, 512).rearrange("p (f s) -> p f s", s=CAP)
        us_b = part(3072, 512).rearrange("p (f s) -> p f s", s=CAP)
        ss_b = part(3584, 512).rearrange("p (f s) -> p f s", s=CAP)
        actT = part(4096, 512).rearrange("p (f s) -> p f s", s=CAP)
        ysb = part(4608, 1024)
        selx = part(5632, 128).rearrange("p (t s) -> p t s", t=2)
        selg = part(5760, 256).rearrange("p (t s) -> p t s", t=2)
        selT = part(6016, 256)
        bguT = part(6528, NIT * 16).rearrange("p (i f) -> p i f", f=16)
        posx = part(7312, 2 * NIT).rearrange("p (t i) -> p t i", t=2)
        gatx = part(7410, 2 * NIT).rearrange("p (t i) -> p t i", t=2)
        lg = part(7508, 64).rearrange("p (t e) -> p t e", t=2)
        m8 = part(7572, 16).rearrange("p (t e) -> p t e", t=2)
        ex = part(7588, 64).rearrange("p (t e) -> p t e", t=2)
        gtm = part(7652, 64).rearrange("p (t e) -> p t e", t=2)
        eqm = part(7716, 64).rearrange("p (t e) -> p t e", t=2)
        csm = part(7780, 64).rearrange("p (t e) -> p t e", t=2)
        sel = part(7844, 64).rearrange("p (t e) -> p t e", t=2)
        br = part(7908, 32)
        IE = part(7940, NIT)
        Aj = part(7990, 17)
        EXj = part(8010, 17)
        cnt = part(8030, 8)
        itf = part(8040, NIT + 1)
        posT = XT[0:E, 0, :]
        gatT = selT[0:E, :]
        b_gu_rows = OT[0:E, :, :].rearrange("p k t -> p (k t)")
        b_dn_rows = ysb[0:E, :]
        w_rt = G[:, 1, 0:KD * E].rearrange("p (k e) -> p k e", k=KD)
        cv = [part(256 * s, 256) for s in range(2)]
        sl = [part(512 + 256 * s, 256) for s in range(2)]
        aT = [part(1024 + 256 * s, 256) for s in range(2)]
        junk = [part(2048 + 1024 * s, 1024) for s in range(2)]
        gu = part(4096, 4 * T).rearrange("p (s c t) -> p s c t", s=2, c=2)
        ssq = st[:, 0:2]
        rstd = st[:, 2:4]
        mhalf = st[:, 4:6]
        nmx = st[:, 6:10]
        psum_l = st[:, 10:14]
        mv = st[:, 14:18].rearrange("p (t v) -> p t v", t=2)
        bst = st[:, 18:42].rearrange("p (t h v) -> p t h v", t=2, h=2)
        tmp2 = st[:, 42:44]
        rcp = st[:, 44:48]
        vrow = YB
        bias_src = XT[0:8, 0, 0:32]
        bias_row = OT[0:8, 0:2, :].rearrange("p k t -> p (k t)")[:, 0:384]
        lf = part(3328, 32).rearrange("p (t h) -> p t h", t=2)
        lfb = part(3392, 32).rearrange("p (t h) -> p t h", t=2)
        bfg = part(3424, 16)
        cumT = LNC[:, 0, 0:32].rearrange("p (t h) -> p t h", t=2)
        ncumR = LNC[0:16, 1, 0:256]

        bias_d = nc.dram_tensor("bias_scratch", [8, P, 384], F32).ap()
        cum_d = nc.dram_tensor("cum_scratch", [16, T], F32).ap()

        consts_ready = sem("consts_ready")
        x_loaded = sem("x_loaded")
        small_loaded = sem("small_loaded")
        vrow_loaded = sem("vrow_loaded")
        rel_loaded = sem("rel_loaded")
        bias_row_ready = sem("bias_row_ready")
        bias_written = sem("bias_written")
        bias_loaded = sem("bias_loaded")
        vec_turned = sem("vec_turned")
        vec_ready = sem("vec_ready")
        cond_ready = sem("cond_ready")
        silu_ready = sem("silu_ready")

        lnc_loaded = sem("lnc_loaded")

        xt_turned = sem("xt_turned")
        xt_act = sem("xt_act")
        xt_dve = sem("xt_dve")
        xn_ready = sem("xn_ready")
        ssq_ready = sem("ssq_ready")
        var_ready = sem("var_ready")
        rstd_ready = sem("rstd_ready")
        att_w = [sem(f"att_w{s}") for s in range(2)]
        qk_done = sem("qk_done")
        qkv_done = sem("qkv_done")
        q_evac = sem("q_evac")
        vT_ready = sem("vT_ready")
        k_evac = sem("k_evac")
        v_turned = sem("v_turned")
        v_evac = sem("v_evac")
        sc_done = sem("sc_done")
        max_ready = sem("max_ready")
        exp_ready = sem("exp_ready")
        prob_ready = sem("prob_ready")
        pt_turned = sem("pt_turned")
        pt_evac = sem("pt_evac")
        pv_done = sem("pv_done")
        o_evac = sem("o_evac")
        lnp_ready = sem("lnp_ready")
        sp_ready = sem("sp_ready")
        r_done = sem("r_done")
        at_ready = sem("at_ready")
        mod_w = [sem(f"mod_w{s}") for s in range(2)]
        mod_summed = sem("mod_summed")
        modfin_rows = sem("modfin_rows")
        modfin_gates = sem("modfin_gates")
        modfin_turned = sem("modfin_turned")
        modfin_read = sem("modfin_read")
        modvec_loaded = sem("modvec_loaded")
        wo_loaded = sem("wo_loaded")
        y_done = sem("y_done")
        y_read = sem("y_read")
        x_updated = sem("x_updated")
        rt_w = sem("rt_w")
        b_gu_loaded = sem("b_gu_loaded")
        b_dn_loaded = sem("b_dn_loaded")
        ysb_zeroed = sem("ysb_zeroed")
        rt_pe = sem("rt_pe")
        rt_dve = sem("rt_dve")
        rt_act = sem("rt_act")
        items_ready = sem("items_ready")
        ew = [sem(f"expert_w{s}") for s in range(SLOTS)]
        ew_used = sem("expert_w_used")
        selx_ready = sem("selx_ready")
        selg_ready = sem("selg_ready")
        gat_mm = sem("gat_mm")
        xe_ev = sem("xe_ev")
        xe_turned = sem("xe_turned")
        xeT_ready = sem("xeT_ready")
        selT_turned = sem("selT_turned")
        selT_ev = sem("selT_ev")
        h_ev = sem("h_ev")
        h_turned = sem("h_turned")
        g_ready = sem("g_ready")
        sg_ready = sem("sg_ready")
        act_ready = sem("act_ready")
        y_ev = sem("y_ev")
        sc_mm = sem("sc_mm")
        acc_done = sem("acc_done")
        zero_ready = sem("zero_ready")
        ffn_w = [sem(f"ffn_w{s}") for s in range(2)]
        ffn_dw = [sem(f"ffn_dw{s}") for s in range(2)]
        dhi_ready = sem("dhi_ready")
        dlo_ready = sem("dlo_ready")
        whi_ready = sem("whi_ready")
        wlo_ready = sem("wlo_ready")
        xlo_ready = sem("xlo_ready")
        fgu_done = sem("fgu_done")
        cv_ready = sem("cv_ready")
        sl_ready = sem("sl_ready")
        fact_ready = sem("fact_ready")
        fdn_done = sem("fdn_done")
        fy_done = sem("fy_done")
        flog_done = sem("flog_done")
        flog_dve = sem("flog_dve")
        flog_act = sem("flog_act")
        cum_done = sem("cum_done")
        ncum_ready = sem("ncum_ready")
        ncum_written = sem("ncum_written")
        ncum_loaded = sem("ncum_loaded")
        out_stored = sem("out_stored")

        def bank(b, n=HALF, rows=slice(0, P), at=0):
            return PS[rows, b, at:at + n]

        def banks(b, n):
            return PS[:, :, :].rearrange("p b n -> p (b n)")[:, b * HALF:b * HALF + n]

        w_qkv = [a["a_w_in"][0], a["w_qkv_2"][0], a["w_qkv_2"][1]]
        w_out = [a["a_w_out"][0], a["w_o_2"][0], a["w_o_2"][1]]
        rows_of = lambda ap: ap.rearrange("(k p) n -> p k n", p=P)
        x_rows = a["x"][0].rearrange("(t p) d -> p t d", p=P)

        def bcast(ap):
            return ap.partition_broadcast(P)

        blk = ctx.enter_context(nc.Block())

        @blk.sync
        def _(sp):
            def att_weights(p, g, half, s):
                src = rows_of(w_qkv[p]).rearrange("p k (c n) -> p k c n", c=3)
                for c in range(3):
                    sp.dma_start(G[:, s, c * D:(c + 1) * D].rearrange("p (k n) -> p k n", k=KD),
                                 src[:, :, c, ds(g * P, P)]).then_inc(att_w[s], 16)

            def mod_block(p, m, s):
                sp.dma_start(mstream[s], rows_of(a["w_mod_2"][p])[:, :, ds(m * MB, MB)]).then_inc(mod_w[s], 16)

            def attention_loads(p):
                att_weights(p, 0, 0, 0)
                if p == 2:
                    sp.wait_ge(fgu_done, FT)
                    sp.wait_ge(fdn_done, FT)
                att_weights(p, 1, 0, 1)
                if p == 1:
                    sp.wait_ge(ew_used, n_items * SLOTS)
                if p < 2:
                    mod_block(p, 0, 0)
                    mod_block(p, 1, 1)
                with sp.Fori(1, NG // 2) as i:
                    for s in range(2):
                        sp.wait_ge(qkv_done, i * 2 + (NG * p + s - 1))
                        att_weights(p, i * 2 + s, i, s)
                        if p < 2:
                            for r in range(2):
                                sp.wait_ge(mod_summed, i * 4 + (NMB * p + 2 * s + r - 3))
                                mod_block(p, i * 4 + (2 * s + r - 2), r)
                if p == 2:
                    sp.wait_ge(y_done, 4)
                sp.dma_start(wo_r, rows_of(w_out[p])).then_inc(wo_loaded, 16)
                if p < 2:
                    for r in range(2):
                        sp.wait_ge(mod_summed, NMB * (p + 1) + r - 3)
                        mod_block(p, NMB + r - 2, r)
                    sp.dma_start(bmod_rows[:, :, :], bcast(a["b_mod_2"][p].rearrange("(c n) -> c n", n=D)[2:6:3, :]))\
                      .then_inc(modvec_loaded, 16)
                    sp.dma_start(gtg[p][:, 0, :], bcast(a["g_mix_post_2"][p])).then_inc(modvec_loaded, 16)
                    sp.dma_start(gtg[p][:, 1, :], bcast(a["g_ffn_post_2"][p])).then_inc(modvec_loaded, 16)
                if p == 0:
                    sp.dma_start(LNC[:, 0, :], bcast(a["ln_g"][0, 0])).then_inc(lnc_loaded, 16)
                    sp.dma_start(LNC[:, 1, :], bcast(a["ln_b"][0, 0])).then_inc(lnc_loaded, 16)

            def ffn_weights(L, j, s):
                for c, name in enumerate(("w_ffn_gate_2", "w_ffn_up_2")):
                    sp.dma_start(G[:, s, c * D:(c + 1) * D].rearrange("p (k n) -> p k n", k=KD),
                                 rows_of(a[name][L])[:, :, ds(j * P, P)]).then_inc(ffn_w[s], 16)

            def ffn_down(L, j, s):
                sp.dma_start(G[:, s, 2 * D:3 * D], a["w_ffn_down_2"][L][ds(j * P, P), :]).then_inc(ffn_dw[s], 16)

            def ffn_loads(L):
                for s in range(2):
                    sp.wait_ge(qkv_done, NG * (L + 1) + NG - 1 + s)
                    ffn_weights(L, s, s)
                    ffn_down(L, s, s)
                sp.wait_ge(wlo_ready, FT * L + 1)
                ffn_weights(L, 2, 0)
                with sp.Fori(1, FT // 2 - 1) as i:
                    for s in range(2):
                        sp.wait_ge(wlo_ready, i * 2 + (FT * L + s))
                        ffn_weights(L, i * 2 + (s + 1), 1 - s)
                        sp.wait_ge(dlo_ready, i * 2 + (FT * L + s - 1))
                        ffn_down(L, i * 2 + s, s)
                sp.wait_ge(wlo_ready, FT * L + FT - 2)
                ffn_weights(L, FT - 1, 1)
                for s in range(2):
                    sp.wait_ge(dlo_ready, FT * L + FT - 3 + s)
                    ffn_down(L, FT - 2 + s, s)

            def expert_slot(e, s):
                if s < GU_SLOTS:
                    src = a["moe_w_gate_up"][0, ds(e, 1)].rearrange("a (k p) n -> p (a k) n", p=P)[:, s, :]
                    sp.dma_start(slot[s], src).then_inc(ew[s], 16)
                else:
                    d = s - GU_SLOTS
                    src = a["moe_w_down"][0, ds(e, 1)].rearrange("a (k p) n -> p (a k) n", p=P)[:, 2 * d:2 * d + 2, :]
                    sp.dma_start(slot[s].rearrange("p (k n) -> p k n", k=2), src).then_inc(ew[s], 16)

            sp.dma_start(XA[:, :, :], x_rows).then_inc(x_loaded, 16)
            attention_loads(0)
            sp.wait_ge(qkv_done, NG)
            sp.dma_start(w_rt, rows_of(a["moe_w_router"][0])).then_inc(rt_w, 16)
            sp.wait_ge(mod_summed, NMB)
            for s in range(7, 11):
                expert_slot(0, s)
            sp.wait_ge(modfin_gates, 1)
            expert_slot(0, 11)
            sp.wait_ge(ysb_zeroed, 1)
            sp.dma_start(b_dn_rows, a["moe_b_down"][0]).then_inc(b_dn_loaded, 16)
            sp.wait_ge(y_done, 2)
            sp.dma_start(b_gu_rows, a["moe_b_gate_up"][0]).then_inc(b_gu_loaded, 16)
            for s in range(4):
                expert_slot(0, s)
            sp.wait_ge(modfin_turned, 2)
            for s in range(4, 7):
                expert_slot(0, s)
            sp.wait_ge(items_ready, 1)
            n_items = sp.value_load(items_i[0:1, NIT:NIT + 1], min_val=E, max_val=E + MAX_EXTRA)
            with sp.Fori(1, n_items) as i:
                e = sp.value_load(items_i[0:1, ds(i, 1)], min_val=0, max_val=E - 1)
                for s in range(SLOTS):
                    sp.wait_ge(ew_used, i * SLOTS + (s + 1 - SLOTS))
                    expert_slot(e, s)
            attention_loads(1)
            ffn_loads(0)
            sp.wait_ge(fgu_done, FT - 1)
            sp.wait_ge(fdn_done, FT - 1)
            attention_loads(2)
            ffn_loads(1)
            for t in range(TT):
                sp.wait_ge(x_updated, 4 * TT + t + 1)
                sp.dma_start(out[0, t * P:(t + 1) * P, :], XA[:, t, :]).then_inc(out_stored, 16)
            sp.wait_ge(out_stored, 16 * TT)

        @blk.gpsimd
        def _(pool):
            def triangle(t, inside, outside, pattern, mult, op):
                pool.memset(t[:, :], inside)
                pool.drain()
                pool.affine_select(out=t[:, :], in_=t[:, :], compare_op=op, fill=outside, base=0,
                                   pattern=[[pattern, P]], channel_multiplier=mult)

            triangle(ident, 0.0, 1.0, -1, 1, ALU.not_equal)
            triangle(ltri, 1.0, 0.0, -1, 1, ALU.is_ge)
            triangle(ustr, 1.0, 0.0, 1, -1, ALU.is_gt)
            triangle(uinc, 1.0, 0.0, 1, -1, ALU.is_ge)
            triangle(identb, 0.0, 1.0, -1, 1, ALU.not_equal)
            triangle(mask0, 0.0, -NEG, 1, -1, ALU.is_gt)
            triangle(mask1, 0.0, NEG, -1, 1, ALU.is_ge)
            pool.memset(ones[:, :], 1.0)

            pool.memset(mhalf, -0.5)
            pool.iota(iota64[:, :], [[1, CAP]], 0, 0, allow_small_or_imprecise_dtypes=True)
            pool.iota(iotaj[:, :], [[1, MAX_EXTRA + 1]], 0, 0, allow_small_or_imprecise_dtypes=True)
            pool.drain()
            pool.memset(tmp2, 0.0).then_inc(consts_ready, 1)

            def to_rstd(t, source, scale, eps):
                pool.tensor_scalar(tmp2[:, t:t + 1], source, scale, eps, ALU.mult, ALU.add)
                pool.drain()
                pool.tensor_tensor(rstd[:, t:t + 1], tmp2[:, t:t + 1], mhalf[:, t:t + 1], ALU.pow)\
                    .then_inc(rstd_ready, 1)

            pool.wait_ge(y_done, 1)
            pool.memset(YB[:, :, :], 0.0)
            pool.memset(selT, 0.0)
            pool.memset(ysb, 0.0).then_inc(ysb_zeroed, 1)
            for k in range(2):
                for t in range(TT):
                    pool.wait_ge(var_ready, TT * k + t + 1)
                    to_rstd(t, mv[:, t, 1:2], 1.0, LN_EPS)
            for k in range(8):
                for t in range(TT):
                    pool.wait_ge(ssq_ready, TT * k + t + 1)
                    to_rstd(t, ssq[:, t:t + 1], 1.0 / D, RMS_EPS)

        @blk.tensor
        def _(pe):
            mm = pe.matmul

            def turn_rows(k):
                src = XA if k < 2 else YB
                for t in range(TT):
                    if k == 0:
                        pe.wait_ge(x_loaded, 16)
                    else:
                        pe.wait_ge(xn_ready, TT * (k - 1) + t + 1)
                    for c in range(KD):
                        last = pe.transpose(PS[:, 4 + c // 2, (c % 2) * T + t * P:(c % 2) * T + (t + 1) * P],
                                            src[:, t, c * P:(c + 1) * P], ident[:, :])
                        if t == TT - 1 and c % 2:
                            last.then_inc(xt_turned, 1)

            def qkv(p, g, half, s, before_v):
                pe.wait_ge(att_w[s], half * 48 + (48 * (NG // 2) * p + 48))
                w = G[:, s, :].rearrange("p (c k n) -> p c k n", c=3, k=KD)
                for c, b in enumerate((0, 1, V_BANK[p])):
                    if c == 2:
                        last.then_inc(qk_done, 1)
                        before_v()
                        if not (p == 0 and isinstance(g, int) and g == 0):
                            pe.wait_ge(v_evac, g + NG * p)
                    for k in range(KD):
                        last = mm(bank(b, T), w[:, c, k, :], XT[:, k, :], start=(k == 0), stop=(k == KD - 1))
                last.then_inc(qkv_done, 1)

            def turn_vectors():
                pe.wait_ge(vrow_loaded, 16 * 11)
                for L in range(2):
                    pe.transpose(bank(2, 64, at=L * 256), vrow[0:64, L, 0:P], ident[0:64, 0:64])
                    pe.transpose(bank(2, 88, at=L * 256 + 64), vrow[0:88, L, P:2 * P], ident[0:88, 0:88])
                pe.wait_ge(silu_ready, 1)
                pe.transpose(bank(6, 8), vrow[0:8, 0, 2 * P:3 * P], ident[0:8, 0:8]).then_inc(vec_turned, 1)
                pe.wait_ge(cond_ready, 1)

            def turn_v(p, g, s):
                pe.wait_ge(vT_ready, g + (NG * p + 1))
                for t in range(TT):
                    last = pe.transpose(bank(V_BANK[p], P, at=T + t * P), vT[:, t * P:(t + 1) * P], ident[:, :])
                last.then_inc(v_turned, 1)

            def scores(p, g, first):
                pe.wait_ge(q_evac, g + (NG * p + 1))
                pe.wait_ge(k_evac, g + (NG * p + 1))
                if p == 1 and not first:
                    pe.wait_ge(at_ready, g)
                if p == 0:
                    mm(bank(2, T), qab[:, 0, P:T], kab[:, 0, :], start=True, stop=True)
                    last = mm(bank(2, P, at=T), qab[:, 0, 0:P], kab[:, 0, 0:P], start=True, stop=True)
                elif p == 1:
                    mm(bank(2), kab[:, 0, 0:P], qab[:, :, :], start=True, stop=False, skip_group_check=True)
                    mm(PS[:, 2, :].rearrange("p (h t) -> p h t", h=2)[:, :, 0:P], identb[:, :],
                       mask0[:, :].unsqueeze(1).to_broadcast([P, 2, P]), start=False, stop=True, skip_group_check=True)
                    mm(bank(3, T), kab[:, 0, P:T], qab[:, :, P:T], start=True, stop=False, skip_group_check=True)
                    last = mm(bank(3, T).rearrange("p (h t) -> p h t", h=2), identb[:, :],
                              mask0[:, :].unsqueeze(1).to_broadcast([P, 2, P]), start=False, stop=True,
                              skip_group_check=True)
                else:
                    mm(bank(2), qab[:, 0, P:T], kab[:, :, :], start=True, stop=False, skip_group_check=True)
                    mm(PS[:, 2, :].rearrange("p (h t) -> p h t", h=2)[:, :, P:T], identb[:, :],
                       mask1[:, :].unsqueeze(1).to_broadcast([P, 2, P]), start=False, stop=True, skip_group_check=True)
                    mm(bank(3, T), qab[:, 0, 0:P], kab[:, :, 0:P], start=True, stop=False, skip_group_check=True)
                    last = mm(bank(3, T).rearrange("p (h t) -> p h t", h=2), identb[:, :],
                              mask1[:, :].unsqueeze(1).to_broadcast([P, 2, P]), start=False, stop=True,
                              skip_group_check=True)
                last.then_inc(sc_done, 1)

            def turn_probs(p, g):
                pe.wait_ge(prob_ready, g + (NG * (p // 2) + 1))
                if p == 0:
                    pe.transpose(bank(4, P, at=0), Pr[:, T:T + P], ident[:, :])
                    pe.transpose(bank(4, P, at=P), Pr[:, 0:P], ident[:, :])
                    last = pe.transpose(bank(4, P, at=T), Pr[:, P:T], ident[:, :])
                else:
                    for h in range(2):
                        pe.transpose(bank(4, P, at=h * T), Pr[:, 512 + h * P:512 + (h + 1) * P], ident[:, :])
                        pe.transpose(bank(4, P, at=h * T + P), Pr[:, h * T:h * T + P], ident[:, :])
                        last = pe.transpose(bank(5, P, at=h * P), Pr[:, h * T + P:(h + 1) * T], ident[:, :])
                last.then_inc(pt_turned, 1)

            def decay_sums(g):
                pe.wait_ge(sp_ready, g + 1)
                mm(bank(2), ltri[:, :], Pr[:, 0:512], start=False, stop=False, skip_group_check=True)
                mm(PS[:, 2, :].rearrange("p (h t) -> p h t", h=2)[:, :, P:T], ones[:, :],
                   Pr[:, 512:768].rearrange("p (h t) -> p h t", h=2), start=False, stop=True, skip_group_check=True)
                mm(bank(3, T), ltri[:, :], Pr[:, 512:768], start=False, stop=True,
                   skip_group_check=True).then_inc(r_done, 1)

            def values(p, g, s):
                if p == 1:
                    pe.wait_ge(at_ready, g + 1)
                else:
                    pe.wait_ge(pt_evac, g + (NG * (p // 2) + 1))
                pe.wait_ge(v_evac, g + (NG * p + 1))
                if not (p == 0 and isinstance(g, int) and g == 0):
                    pe.wait_ge(o_evac, g + NG * p)
                if p == 0:
                    mm(bank(6, T), V[:, s, 0, :], PT[:, 0:T], start=True, stop=False, skip_group_check=True)
                    last = mm(bank(6, P, at=P), V[:, s, 1, :], PT[:, T:T + P], start=False, stop=True,
                              skip_group_check=True)
                else:
                    for h in range(2):
                        r = slice(HD2 * h, HD2 * (h + 1))
                        mm(bank(6, T, r), V[:, s, 0, r], PT[:, h * T:(h + 1) * T], start=True, stop=False,
                           skip_group_check=True)
                        last = mm(bank(6, P, r, at=P), V[:, s, 1, r], PT[:, 512 + h * P:512 + (h + 1) * P],
                                  start=False, stop=True, skip_group_check=True)
                last.then_inc(pv_done, 1)

            def step(p, g, half, s, first):
                def before_v():
                    if not first:
                        if p == 1:
                            decay_sums(g - 1)
                        else:
                            turn_probs(p, g - 1)

                qkv(p, g, half, s, before_v)
                if p == 0 and first:
                    turn_vectors()
                scores(p, g, first)
                turn_v(p, g, s)
                if not first:
                    values(p, g - 1, 1 - s)
            def attention(p):
                step(p, 0, 0, 0, True)
                step(p, 1, 0, 1, False)
                with pe.Fori(1, NG // 2) as i:
                    for s in range(2):
                        step(p, i * 2 + s, i, s, False)
                if p == 1:
                    decay_sums(NG - 1)
                else:
                    turn_probs(p, NG - 1)
                values(p, NG - 1, 1)
                pe.wait_ge(o_evac, NG * (p + 1))

            def modulation_gates(p):
                pe.wait_ge(mod_summed, NMB * (p + 1))
                for n, c in enumerate((4, 5, 10, 11)):
                    last = mm(bank(4 + n), ones[:, :], macc[:, c * HALF:(c + 1) * HALF], start=True, stop=True)
                last.then_inc(modfin_rows, 1)

            def modulation_columns(p, r):
                if r == 0:
                    pe.wait_ge(modfin_gates, p + 1)
                else:
                    pe.wait_ge(modfin_read, TT * p + 1)
                for n in range(16):
                    last = pe.transpose(bank(4 + n // 4, P, at=(n % 4) * P),
                                        macc[:, (24 * r + n) * P:(24 * r + n + 1) * P], ident[:, :])
                last.then_inc(modfin_turned, 1)

            def project_out(p):
                pe.wait_ge(wo_loaded, 16 * (p + 1))
                for t in range(TT):
                    for k in range(KD):
                        if p < 2 and (t, k) == ((1, 0), (0, KD // 2))[p]:
                            modulation_gates(p)
                        if p < 2 and (t, k) == ((1, KD // 2), (1, 0))[p]:
                            modulation_columns(p, 0)
                        if p == 1 and (t, k) == (1, KD // 2):
                            modulation_columns(p, 1)
                        for n in range(2):
                            last = mm(bank(2 * t + n), OT[:, k, t * P:(t + 1) * P], wo_r[:, k, n * HALF:(n + 1) * HALF],
                                      start=(k == 0), stop=(k == KD - 1))
                    last.then_inc(y_done, 1)
                if p == 0:
                    modulation_columns(p, 1)
                if p < 2:
                    pe.wait_ge(modfin_read, TT * (p + 1))

            def wait_columns(k):
                pe.wait_ge(xt_act, k + 1)
                pe.wait_ge(xt_dve, k + 1)

            def feed_forward(L):
                def gate_up(j, s):
                    pe.wait_ge(wlo_ready, j + (FT * L + 1))
                    if not (L == 0 and isinstance(j, int) and j < 2):
                        pe.wait_ge(fact_ready, j + (FT * L - 1))
                    hi = whi[s].rearrange("p (c k n) -> p c k n", c=2, k=KD)
                    lo = wlo[s].rearrange("p (c k n) -> p c k n", c=2, k=KD)
                    for c in range(2):
                        for k in range(KD):
                            mm(bank(4 + 2 * s + c), hi[:, c, k, :].bitcast(F32R),
                               xs[:, k, :, :].bitcast(F32R), start=(k == 0), stop=False,
                               skip_group_check=True)
                            last = mm(bank(4 + 2 * s + c, T), lo[:, c, k, :].bitcast(F32R),
                                      xs[:, k, 0, :].bitcast(F32R), start=False, stop=(k == KD - 1),
                                      skip_group_check=True)
                    last.then_inc(fgu_done, 1)

                def down(j, s, first=False, end=False):
                    pe.wait_ge(dlo_ready, j + (FT * L + 1))
                    pe.wait_ge(fact_ready, j + (FT * L + 1))
                    for t in range(TT):
                        for q, (h, w) in enumerate(((0, dhi), (0, dlo), (1, dhi))):
                            for n in range(2):
                                last = mm(bank(2 * t + n), acts[s][:, h, t * P:(t + 1) * P].bitcast(F32R),
                                          w[s][:, n * HALF:(n + 1) * HALF].bitcast(F32R),
                                          start=(first and q == 0), stop=(end and q == 2), skip_group_check=True)
                        if end and t == 0:
                            last.then_inc(fy_done, 1)
                    last.then_inc(fdn_done, 1)

                pe.wait_ge(xlo_ready, L + 1)
                gate_up(0, 0)
                gate_up(1, 1)
                down(0, 0, first=True)
                with pe.Fori(1, FT // 2) as i:
                    gate_up(i * 2, 0)
                    down(i * 2 - 1, 1)
                    gate_up(i * 2 + 1, 1)
                    down(i * 2, 0)
                down(FT - 1, 1, end=True)

            def routing():
                pe.wait_ge(rt_w, 16)
                for t in range(TT):
                    for k in range(KD):
                        last = mm(bank(4, E, at=t * E), XT[:, k, t * P:(t + 1) * P], w_rt[:, k, :],
                                  start=(k == 0), stop=(k == KD - 1))
                last.then_inc(rt_pe, 1)
                pe.wait_ge(rt_dve, 1)
                mm(bank(5, E), ustr[:, :], sel[:, 0, :], start=True, stop=True)
                mm(bank(5, E, at=E), ones[:, :], sel[:, 0, :], start=True, stop=False)
                mm(bank(5, E, at=E), ustr[:, :], sel[:, 1, :], start=False, stop=True)
                mm(bank(6, 1, slice(0, E)), sel[:, 0, :], ones[:, 0:1], start=True, stop=False)
                mm(bank(6, 1, slice(0, E)), sel[:, 1, :], ones[:, 0:1], start=False,
                   stop=True).then_inc(rt_pe, 1)
                pe.wait_ge(rt_dve, 2)
                mm(bank(7, 1, slice(0, E)), uinc[0:E, 0:E], cnt[0:E, 1:2], start=True, stop=True)
                for t in range(TT):
                    pe.transpose(bank(4, P, slice(0, E), at=t * P), posx[:, t, 0:E], ident[:, :])
                for t in range(TT):
                    last = pe.transpose(bank(4, P, slice(0, E), at=T + t * P), gatx[:, t, 0:E], ident[:, :])
                last.then_inc(rt_pe, 1)
                pe.wait_ge(rt_dve, 3)
                mm(bank(5, 17), ones[0:E, :], Aj[0:E, :], start=True, stop=True)
                mm(bank(5, 17, at=32), ones[0:E, :], EXj[0:E, :], start=True, stop=True)
                mm(bank(5, 1, at=64), ones[0:E, :], cnt[0:E, 1:2], start=True, stop=True)
                for t in range(TT):
                    mm(bank(6, 17, at=t * 17), posT[:, t * P:(t + 1) * P], IE[0:E, E:NIT], start=True, stop=True)
                    last = mm(bank(6, 17, at=64 + t * 17), gatT[:, t * P:(t + 1) * P], IE[0:E, E:NIT],
                              start=True, stop=True)
                last.then_inc(rt_pe, 1)
                pe.wait_ge(b_gu_loaded, 16)
                for f in range(16):
                    last = mm(bank(f // 8, NIT, at=(f % 8) * NIT), b_gu_rows[:, f * P:(f + 1) * P], IE[0:E, 0:NIT],
                              start=True, stop=True)
                last.then_inc(rt_pe, 1)

            def gather(j, first=False):
                pe.wait_ge(selx_ready, j + 1)
                if not first:
                    pe.wait_ge(selT_ev, j)
                for t in range(TT):
                    for n in range(2):
                        last = mm(bank(6, HALF, slice(CAP * n, CAP * (n + 1))), selx[:, t, :],
                                  XA[:, t, n * HALF:(n + 1) * HALF], start=(t == 0), stop=(t == 1))
                last.then_inc(gat_mm, 1)

            def turn_gathered(j):
                pe.wait_ge(xe_ev, j + 1)
                for c in range(4):
                    last = pe.transpose(bank(7, P, at=c * P), xe[:, c * P:(c + 1) * P], ident[:, :])
                last.then_inc(xe_turned, 1)

            def scatter(i):
                pe.wait_ge(y_ev, i + 1)
                pe.wait_ge(selT_ev, i + 1)
                for q, b in enumerate((4, 5, 0, 1)):
                    t, n = q // 2, q % 2
                    mm(bank(b), selT[:, t * P:(t + 1) * P], ysb[:, n * HALF:(n + 1) * HALF],
                       start=True, stop=True).then_inc(sc_mm, 1)

            def experts():
                pe.wait_ge(items_ready, 1)
                n_items = pe.value_load(items_i[0:1, NIT:NIT + 1], min_val=E, max_val=E + MAX_EXTRA)
                pe.wait_ge(b_dn_loaded, 16)
                gather(0, first=True)
                turn_gathered(0)
                with pe.Fori(0, n_items) as i:
                    pe.wait_ge(xeT_ready, i + 1)
                    pe.wait_ge(acc_done, i * 4 + 1)
                    for k in range(KD):
                        pe.wait_ge(ew[k], i * 16 + 16)
                        for n in range(2):
                            for c in range(2):
                                last = mm(bank(n, HALF, slice(CAP * c, CAP * (c + 1))), xeT[:, k, :],
                                          slot[k][:, c * D + n * HALF:c * D + (n + 1) * HALF],
                                          start=(k == 0), stop=(k == KD - 1))
                        last.then_inc(ew_used, 1)
                    gather(i + 1)
                    pe.wait_ge(h_ev, i + 1)
                    for f in range(8):
                        last = pe.transpose(bank(2 + f // 4, P, at=(f % 4) * P), hsb[:, f * P:(f + 1) * P], ident[:, :])
                    last.then_inc(h_turned, 1)
                    scatter(i)
                    turn_gathered(i + 1)
                    pe.wait_ge(selg_ready, i + 1)
                    for t in range(TT):
                        last = pe.transpose(bank(6, P, at=t * P), selg[:, t, :], ident[:, :])
                    last.then_inc(selT_turned, 1)
                    pe.wait_ge(act_ready, i + 1)
                    pe.wait_ge(acc_done, i * 4 + 3)
                    for d in range(DN_SLOTS):
                        pe.wait_ge(ew[GU_SLOTS + d], i * 16 + 16)
                        for n in range(2):
                            for c in range(2):
                                last = mm(bank(4 + n, HALF, slice(CAP * c, CAP * (c + 1))), actT[:, 2 * d + c, :],
                                          slot[GU_SLOTS + d][:, c * D + n * HALF:c * D + (n + 1) * HALF],
                                          start=(d == 0), stop=(d == DN_SLOTS - 1))
                        last.then_inc(ew_used, 1)
                pe.wait_ge(acc_done, n_items * 4 + 1)
                scatter(n_items)

            def forget_gates():
                for t in range(TT):
                    for k in range(KD):
                        last = mm(bank(4, 16, at=t * 16), XT[:, k, t * P:(t + 1) * P], wfg[:, k, :],
                                  start=(k == 0), stop=(k == KD - 1))
                last.then_inc(flog_done, 1)
                pe.wait_ge(flog_dve, 2)
                mm(bank(5, 16), uinc[:, :], lf[:, 0, :], start=True, stop=True)
                mm(bank(5, 16, at=16), ones[:, :], lf[:, 0, :], start=True, stop=False)
                mm(bank(5, 16, at=16), uinc[:, :], lf[:, 1, :], start=False, stop=True)
                mm(bank(6, P, slice(0, 16)), lf[:, 0, :], uinc[:, :], start=True, stop=True)
                mm(bank(6, P, slice(0, 16), at=P), lf[:, 0, :], ones[:, :], start=True, stop=False)
                mm(bank(6, P, slice(0, 16), at=P), lf[:, 1, :], uinc[:, :], start=False,
                   stop=True).then_inc(cum_done, 1)

            pe.wait_ge(consts_ready, 1)
            turn_rows(0)
            wait_columns(0)
            attention(0)
            project_out(0)
            turn_rows(1)
            wait_columns(1)
            routing()
            experts()
            for L in range(2):
                turn_rows(2 + 2 * L)
                wait_columns(2 + 2 * L)
                if L == 1:
                    forget_gates()
                attention(1 + L)
                project_out(1 + L)
                turn_rows(3 + 2 * L)
                wait_columns(3 + 2 * L)
                feed_forward(L)

        @blk.scalar
        def _(act):
            fn = act.activation
            def down_high(L, j, jh, s):
                act.wait_ge(ffn_dw[s], jh * 16 + (16 * (FT // 2) * L + 16))
                if not (isinstance(j, int) and j < 2):
                    act.wait_ge(fdn_done, j + (FT * L - 1))
                fn(dhi[s][:, :].bitcast(F32R), G[:, s, 2 * D:3 * D], ACT.Copy).then_inc(dhi_ready, 1)

            act.dma_start(bias_src, a["rel_bias"].rearrange("b h -> h b"), allow_slow_non_contiguous=True)\
               .then_inc(rel_loaded, 16)
            for L in range(2):
                for lo, n, name in ((0, 48, "b_mod_2"), (48, 8, "g_mix_pre_2"), (56, 8, "g_ffn_pre_2")):
                    act.dma_start(vrow[lo:lo + n, L, 0:P], a[name][L].rearrange("(r n) -> r n", n=P))\
                       .then_inc(vrow_loaded, 16)
                act.dma_start(vrow[0:66, L, P:2 * P], a["w_conv_2"][L].rearrange("w (r n) -> (w r) n", n=P))\
                   .then_inc(vrow_loaded, 16)
                act.dma_start(vrow[66:88, L, P:2 * P], a["b_conv_2"][L].rearrange("(r n) -> r n", n=P))\
                   .then_inc(vrow_loaded, 16)
            act.dma_start(vrow[0:8, 0, 2 * P:3 * P], a["c_2"][0].rearrange("(r n) -> r n", n=P))\
               .then_inc(vrow_loaded, 16)
            act.dma_start(wfg[:, :, :], rows_of(a["w_fg_2"][0])).then_inc(small_loaded, 16)
            act.wait_ge(bias_row_ready, 1)
            act.dma_start(bias_d, bias_row.unsqueeze(1).to_broadcast([8, P, 384])).then_inc(bias_written, 16)

            def columns(k, scale=None, shift=None, split=False):
                for c in (0, 1, 4, 5):
                    act.wait_ge(xt_turned, 4 * k + c // 2 + 1)
                    src = PS[:, 4 + c // 2, (c % 2) * T:(c % 2 + 1) * T]
                    if scale is None:
                        last = fn(XT[:, c, :], src, ACT.Copy)
                    else:
                        last = fn(XT[:, c, :], src, ACT.Identity, bias=shift[:, c:c + 1], scale=scale[:, c:c + 1])
                    if split:
                        last = fn(xs[:, c, 0, :].bitcast(F32R), src, ACT.Identity, bias=shift[:, c:c + 1],
                                  scale=scale[:, c:c + 1])
                last.then_inc(xt_act, 1)

            def weights_high(L, j, jh, s):
                act.wait_ge(ffn_w[s], jh * 32 + (32 * (FT // 2) * L + 32))
                if not (isinstance(j, int) and j < 2):
                    act.wait_ge(fgu_done, j + (FT * L - 1))
                fn(whi[s].bitcast(F32R), G[:, s, 0:2 * D], ACT.Copy).then_inc(whi_ready, 1)

            def evacuate(p, g):
                act.wait_ge(qk_done, g + (NG * p + 1))
                if p == 1:
                    for h in range(2):
                        r = slice(HD2 * h, HD2 * (h + 1))
                        last = fn(qab[r, h, :], PS[r, 0, 0:T], ACT.Copy, scale=HD2 ** -0.5)
                else:
                    last = fn(qab[:, 0, :], PS[:, 0, 0:T], ACT.Copy, scale=(P if p == 0 else HD2) ** -0.5)
                last.then_inc(q_evac, 1)
                if p < 2:
                    fn(kab[:, 0, :], PS[:, 1, 0:T], ACT.Copy, scale=1.0 - 2.0 * p).then_inc(k_evac, 1)

            def value_columns(p, g):
                act.wait_ge(qkv_done, g + (NG * p + 1))
                fn(vT, bank(V_BANK[p], T), ACT.Copy).then_inc(vT_ready, 1)

            def value_rows(p, g, s):
                act.wait_ge(v_turned, g + (NG * p + 1))
                fn(V[:, s, :, :], bank(V_BANK[p], T, at=T).rearrange("p (t d) -> p t d", t=2), ACT.Copy).then_inc(v_evac, 1)

            def heads_out(p, g):
                act.wait_ge(pv_done, g + (NG * p + 1))
                fn(OT[:, ds(g, 1), :].squeeze(1), bank(6, T), ACT.Copy).then_inc(o_evac, 1)

            def softplus_tail(g):
                act.wait_ge(sc_done, g + (NG + 1))
                fn(Ssb, banks(2, 768), ACT.Abs)
                act.drain()
                fn(Ssb, Ssb, ACT.Exp, scale=-1.0)
                act.drain()
                fn(Ssb, Ssb, ACT.Ln, bias=1.0).then_inc(lnp_ready, 1)

            def weights_from_sums(g):
                act.wait_ge(r_done, g + 1)
                fn(PT, banks(2, 768), ACT.Exp, scale=-1.0).then_inc(at_ready, 1)

            def softmax_exp(p, g):
                act.wait_ge(max_ready, g + (NG * (p // 2) + 1))
                segs = ((0, T), (T, P)) if p == 0 else ((0, T), (T, T), (512, P), (640, P))
                for n, (lo, w) in enumerate(segs):
                    last = fn(Pr[:, lo:lo + w], Ssb[:, lo:lo + w], ACT.Exp, bias=nmx[:, n:n + 1],
                              accum_out=psum_l[:, n:n + 1])
                last.then_inc(exp_ready, 1)

            def turned_probs(p, g):
                act.wait_ge(pt_turned, g + (NG * (p // 2) + 1))
                w = 384 if p == 0 else 768
                fn(PT[:, 0:w], banks(4, w), ACT.Copy).then_inc(pt_evac, 1)



            def step(p, g, s, first):
                evacuate(p, g)
                if not first:
                    if p == 1:
                        weights_from_sums(g - 1)
                    else:
                        turned_probs(p, g - 1)
                value_columns(p, g)
                if p < 2:
                    value_rows(p, g, s)
                if p == 1:
                    if not first:
                        heads_out(p, g - 1)
                    softplus_tail(g)
                else:
                    softmax_exp(p, g)
                    if p == 0 and not first:
                        heads_out(p, g - 1)

            def attention(p):
                step(p, 0, 0, True)
                step(p, 1, 1, False)
                with act.Fori(1, NG // 2) as i:
                    for s in range(2):
                        step(p, i * 2 + s, s, False)
                if p == 1:
                    weights_from_sums(NG - 1)
                else:
                    turned_probs(p, NG - 1)
                if p < 2:
                    heads_out(p, NG - 1)

            def squares(src, *ready):
                for t in range(TT):
                    act.wait_ge(*ready[t])
                    fn(junk[t], src(t), ACT.Square, accum_out=ssq[:, t:t + 1]).then_inc(ssq_ready, 1)

            def product(t):
                return banks(2 * t, D)

            def x_row(t):
                return XA[:, t, :]

            columns(0)
            act.wait_ge(vrow_loaded, 16 * 11)
            fn(vrow[0:8, 0, 2 * P:3 * P], vrow[0:8, 0, 2 * P:3 * P], ACT.Silu).then_inc(silu_ready, 1)
            act.wait_ge(bias_written, 16)
            act.dma_start(bias_tiles, bass.AP(tensor=bias_d.tensor, offset=P - 1, ap=[[383, P], [P * 384, 8], [1, T]]))\
               .then_inc(bias_loaded, 16)
            attention(0)
            columns(1)
            act.dma_start(br, bcast(a["moe_b_router"][0])).then_inc(small_loaded, 16)
            act.wait_ge(rt_dve, 1)
            for t in range(TT):
                last = fn(ex[:, t, :], lg[:, t, :], ACT.Exp, bias=nmx[:, t:t + 1])
            last.then_inc(rt_act, 1)
            act.wait_ge(xn_ready, TT)
            act.dma_start(LNC[:, 0, :], bcast(a["ln_g"][0, 1])).then_inc(lnc_loaded, 16)
            act.dma_start(LNC[:, 1, :], bcast(a["ln_b"][0, 1])).then_inc(lnc_loaded, 16)
            act.wait_ge(items_ready, 1)
            n_items = act.value_load(items_i[0:1, NIT:NIT + 1], min_val=E, max_val=E + MAX_EXTRA)

            def gathered(j):
                act.wait_ge(gat_mm, j + 1)
                fn(xe, bank(6), ACT.Copy).then_inc(xe_ev, 1)

            act.wait_ge(zero_ready, 1)
            fn(psum_l[:, 0:1], ident[:, 0:1], ACT.Copy).then_inc(y_ev, 1)
            fn(psum_l[:, 1:2], ident[:, 0:1], ACT.Copy).then_inc(selT_ev, 1)
            gathered(0)
            with act.Fori(0, n_items) as i:
                act.wait_ge(ew_used, i * SLOTS + GU_SLOTS)
                fn(hsb, banks(0, D), ACT.Copy).then_inc(h_ev, 1)
                gathered(i + 1)
                act.wait_ge(g_ready, i + 1)
                fn(ss_b, gs_b, ACT.Sigmoid, scale=SWIGLU_ALPHA).then_inc(sg_ready, 1)
                act.wait_ge(selT_turned, i + 1)
                fn(selT, bank(6, T), ACT.Copy).then_inc(selT_ev, 1)
                act.wait_ge(ew_used, i * SLOTS + SLOTS)
                fn(ysb, banks(4, D), ACT.Copy).then_inc(y_ev, 1)
            for L in range(2):
                squares(x_row, (x_updated, 4 * L + 1), (x_updated, 4 * L + 2))
                columns(2 + 2 * L, gsc[:, L, 0:8], shc[:, L, 0:8])
                if L == 1:
                    act.dma_start(bfg, bcast(a["b_fg_2"][0])).then_inc(small_loaded, 16)
                    act.wait_ge(flog_dve, 1)
                    fn(lfb, lf, ACT.Abs)
                    act.drain()
                    fn(lfb, lfb, ACT.Exp, scale=-1.0)
                    act.drain()
                    fn(lfb, lfb, ACT.Ln, bias=1.0).then_inc(flog_act, 1)
                    act.wait_ge(ncum_ready, 1)
                    act.dma_start(cum_d, ncumR).then_inc(ncum_written, 16)
                    act.wait_ge(ncum_written, 16)
                    act.dma_start(ncum_b, bcast(cum_d)).then_inc(ncum_loaded, 16)
                attention(1 + L)
                if L == 0:
                    act.wait_ge(mod_summed, 2 * NMB)
                for s in range(2):
                    weights_high(L, s, 0, s)
                squares(product, (y_done, 2 * L + 3), (y_done, 2 * L + 4))
                squares(x_row, (x_updated, 4 * L + 3), (x_updated, 4 * L + 4))
                columns(3 + 2 * L, gsc[:, L, 8:16], shc[:, L, 8:16], split=True)

                def silu_tile(j, s):
                    act.wait_ge(cv_ready, j + (FT * L + 1))
                    fn(sl[s], cv[s], ACT.Silu).then_inc(sl_ready, 1)

                down_high(L, 0, 0, 0)
                for s in range(2):
                    weights_high(L, s + 2, 1, s)
                    silu_tile(s, s)
                    down_high(L, s + 1, s, 1 - s)
                with act.Fori(1, FT // 2 - 1) as i:
                    for s in range(2):
                        weights_high(L, i * 2 + (s + 2), i + 1, s)
                        silu_tile(i * 2 + s, s)
                        down_high(L, i * 2 + (s + 1), i + s, 1 - s)
                silu_tile(FT - 2, 0)
                down_high(L, FT - 1, FT // 2 - 1, 1)
                silu_tile(FT - 1, 1)
                squares(product, (fy_done, L + 1), (fdn_done, FT * (L + 1)))

        @blk.vector
        def _(dve):
            tt, ts, stt = dve.tensor_tensor, dve.tensor_scalar, dve.scalar_tensor_tensor

            def columns(k, scale=None, shift=None, split=False):
                for c in (2, 3, 6, 7):
                    dve.wait_ge(xt_turned, 4 * k + c // 2 + 1)
                    src = PS[:, 4 + c // 2, (c % 2) * T:(c % 2 + 1) * T]
                    if scale is None:
                        last = dve.tensor_copy(XT[:, c, :], src)
                    else:
                        last = ts(XT[:, c, :], src, scale[:, c:c + 1], shift[:, c:c + 1], ALU.mult, ALU.add)
                    if split:
                        last = ts(xs[:, c, 0, :].bitcast(F32R), src, scale[:, c:c + 1], shift[:, c:c + 1],
                                  ALU.mult, ALU.add)
                last.then_inc(xt_dve, 1)

            def columns_low(L):
                dve.drain()
                dve.wait_ge(xt_act, 4 + 2 * L)
                for h in range(2):
                    k = slice(4 * h, 4 * h + 4)
                    last = tt(xs[:, k, 1, :].bitcast(F32R), XT[:, k, :], xs[:, k, 0, :], ALU.subtract)
                last.then_inc(xlo_ready, 1)

            def down_low(L, j, s):
                dve.wait_ge(dhi_ready, j + (FT * L + 1))
                tt(dlo[s][:, :].bitcast(F32R), G[:, s, 2 * D:3 * D], dhi[s][:, :], ALU.subtract)\
                    .then_inc(dlo_ready, 1)

            def weights_low(L, j, s):
                dve.wait_ge(whi_ready, j + (FT * L + 1))
                tt(wlo[s].bitcast(F32R), G[:, s, 0:2 * D], whi[s], ALU.subtract).then_inc(wlo_ready, 1)

            def evacuate(p, g):
                dve.wait_ge(qk_done, g + (NG * p + 1))
                for h in range(2):
                    r = slice(HD2 * h, HD2 * (h + 1))
                    last = dve.tensor_copy(kab[r, h, :], PS[r, 1, 0:T])
                last.then_inc(k_evac, 1)

            def value_rows(p, g, s):
                dve.wait_ge(v_turned, g + (NG * p + 1))
                dve.tensor_copy(V[:, s, :, :], bank(V_BANK[p], T, at=T).rearrange("p (t d) -> p t d", t=2))\
                   .then_inc(v_evac, 1)

            def softplus_sum(g):
                dve.wait_ge(lnp_ready, g + 1)
                stt(Pr, banks(2, 768), 0.0, Ssb, ALU.min, ALU.subtract, reverse1=True).then_inc(sp_ready, 1)

            def softmax(p, g):
                dve.wait_ge(sc_done, g + (NG * p + 1))
                if p == 0:
                    tt(Ssb[:, 0:T], bank(2, T), bias_tiles[:, ds(g, 1), :].squeeze(1), ALU.add)
                    tt(Ssb[:, T:384], bank(2, P, at=T), bias_tiles[:, ds(g, 1), P:T].squeeze(1), ALU.add)
                    dve.drain()
                    dve.tensor_reduce(nmx[:, 0:1], Ssb[:, 0:T], AX_X, ALU.max, negate=True)
                    dve.tensor_reduce(nmx[:, 1:2], Ssb[:, T:384], AX_X, ALU.max, negate=True).then_inc(max_ready, 1)
                    n = 2
                else:
                    for t, at, w, wk in ((1, 0, T, T), (0, 512, P, P)):
                        for h in range(2):
                            lo = at + h * w
                            stt(Ssb[:, lo:lo + w], banks(2, 768)[:, lo:lo + w], cumT[:, t, ds(g * 2 + h, 1)],
                                ncum_b[:, ds(g * 2 + h, 1), 0:wk].squeeze(1), ALU.add, ALU.add)
                    dve.drain()
                    dve.tensor_reduce(nmx[:, 0:2], Ssb[:, 0:512].rearrange("p (h t) -> p h t", h=2), AX_X, ALU.max,
                                      negate=True)
                    dve.tensor_reduce(nmx[:, 2:4], Ssb[:, 512:768].rearrange("p (h t) -> p h t", h=2), AX_X, ALU.max,
                                      negate=True).then_inc(max_ready, 1)
                    n = 4
                dve.wait_ge(exp_ready, g + (NG * (p // 2) + 1))
                dve.reciprocal(rcp[:, 0:n], psum_l[:, 0:n])
                dve.drain()
                segs = ((0, T), (T, P)) if p == 0 else ((0, T), (T, T), (512, P), (640, P))
                for k, (lo, w) in enumerate(segs):
                    last = ts(Pr[:, lo:lo + w], Pr[:, lo:lo + w], rcp[:, k:k + 1], None, ALU.mult)
                last.then_inc(prob_ready, 1)

            def heads_out(p, g):
                dve.wait_ge(pv_done, g + (NG * p + 1))
                dve.tensor_copy(OT[:, ds(g, 1), :].squeeze(1), bank(6, T)).then_inc(o_evac, 1)

            def modulation(p, g, r):
                dve.drain()
                dve.wait_ge(mod_w[r], g * 16 + (16 * (NMB // 2) * p + 16))
                w, acc = mstream[r], bank(5 + 2 * r, MB)
                ts(acc, w[:, 0, :], cc[:, 0:1], None, ALU.mult)
                dve.drain()
                for k in range(1, KD - 1):
                    stt(acc, w[:, k, :], cc[:, k:k + 1], acc, ALU.mult, ALU.add)
                    dve.drain()
                stt(macc[:, ds(g * (2 * MB) + r * MB, MB)], w[:, KD - 1, :], cc[:, KD - 1:KD], acc,
                    ALU.mult, ALU.add).then_inc(mod_summed, 1)

            def step(p, g, s, first):
                if p == 2:
                    evacuate(p, g)
                    value_rows(p, g, s)
                if p == 1:
                    softplus_sum(g)
                else:
                    softmax(p, g)
                if p == 2 and not first:
                    heads_out(p, g - 1)
                if p < 2:
                    modulation(p, g, 0)
                    modulation(p, g, 1)

            def attention(p):
                step(p, 0, 0, True)
                step(p, 1, 1, False)
                with dve.Fori(1, NG // 2) as i:
                    for s in range(2):
                        step(p, i * 2 + s, s, False)
                if p == 2:
                    heads_out(p, NG - 1)

            def modulation_gates(p):
                dve.wait_ge(modvec_loaded, 48 * (p + 1))
                dve.wait_ge(modfin_rows, p + 1)
                for k in range(2):
                    tt(banks(4 + 2 * k, D), banks(4 + 2 * k, D), bmod_rows[:, k, :], ALU.add)
                dve.drain()
                for k in range(2):
                    last = tt(gtg[p][:, k, :], banks(4 + 2 * k, D), gtg[p][:, k, :], ALU.mult)
                last.then_inc(modfin_gates, 1)

            def modulation_columns(p, r):
                dve.wait_ge(modfin_turned, TT * p + r + 1)
                for b in range(4):
                    last = dve.tensor_reduce(modc[:, 4 * b:4 * b + 4], bank(4 + b).rearrange("p (c q) -> p c q", c=4),
                                             AX_X, ALU.add)
                last.then_inc(modfin_read, 1)
                dve.drain()
                tt(shc[:, p, 8 * r:8 * r + 8], modc[:, 0:8], vcol[:, p, 24 * r:24 * r + 8], ALU.add)
                tt(modc[:, 8:16], modc[:, 8:16], vcol[:, p, 24 * r + 8:24 * r + 16], ALU.add)
                dve.drain()
                stt(gsc[:, p, 8 * r:8 * r + 8], modc[:, 8:16], 1.0, vcol[:, p, 48 + 8 * r:56 + 8 * r],
                    ALU.add, ALU.mult)

            def layer_norm_stats(t, source):
                y = banks(2 * t, D)
                stt(y, XA[:, t, :], ALPHA, source, ALU.mult, ALU.add)
                dve.drain()
                for h in range(2):
                    dve.bn_stats(bst[:, t, h, :], y[:, h * HALF:(h + 1) * HALF])
                dve.drain()
                dve.bn_aggr(mv[:, t, :], bst[:, t, :, :]).then_inc(var_ready, 1)

            def layer_norm_apply(k, t):
                y = banks(2 * t, D)
                dve.wait_ge(lnc_loaded, 32 * (k + 1))
                dve.drain()
                stt(y, y, mv[:, t, 0:1], LNC[:, 0, :], ALU.subtract, ALU.mult)
                dve.drain()
                dve.wait_ge(rstd_ready, TT * k + t + 1)
                return stt(XA[:, t, :], y, rstd[:, t:t + 1], LNC[:, 1, :], ALU.mult, ALU.add)

            def normed_rows(n, t):
                dve.wait_ge(rstd_ready, TT * n + t + 1)
                ts(YB[:, t, :], XA[:, t, :], rstd[:, t:t + 1], None, ALU.mult).then_inc(xn_ready, 1)

            def add_normed(n, t, g):
                y = banks(2 * t, D)
                dve.wait_ge(rstd_ready, TT * n + t + 1)
                stt(y, y, rstd[:, t:t + 1], g, ALU.mult, ALU.mult)
                dve.drain()
                tt(XA[:, t, :], XA[:, t, :], y, ALU.add).then_inc(x_updated, 1)

            tmp_inc = rcp[:, 3:4]
            dve.wait_ge(rel_loaded, 16)
            starts = bucket_starts()
            for b in range(BUCKETS):
                lo, hi = starts[b], starts[b + 1]
                dve.tensor_copy(bias_row[:, T - hi:T - lo], bias_src[:, b:b + 1].to_broadcast([8, hi - lo]))
            dve.memset(bias_row[:, T:384], NEG)
            dve.drain()
            dve.memset(st[0:8, 47:48], 0.0).then_inc(bias_row_ready, 1)
            dve.wait_ge(bias_row_ready, 1)
            columns(0)
            dve.wait_ge(vec_turned, 1)
            for L in range(2):
                dve.tensor_copy(vcol[:, L, :], bank(2, 152, at=L * 256))
            dve.tensor_copy(cc[:, :], bank(6, KD)).then_inc(cond_ready, 1)
            dve.wait_ge(bias_loaded, 16)
            attention(0)
            for t in range(TT):
                dve.wait_ge(y_done, t + 1)
                layer_norm_stats(t, banks(2 * t, D))
                if t == 1:
                    modulation_columns(0, 1)
                layer_norm_apply(0, t).then_inc(xn_ready, 1)
                if t == 0:
                    modulation_gates(0)
                    modulation_columns(0, 0)
            columns(1)
            dve.wait_ge(rt_pe, 1)
            dve.wait_ge(small_loaded, 32)
            tt(lg, bank(4, 64).rearrange("p (t e) -> p t e", t=2), br.unsqueeze(1).to_broadcast([P, 2, E]), ALU.add)
            dve.drain()
            for t in range(TT):
                dve.max(m8[:, t, :], lg[:, t, :])
            dve.drain()
            for t in range(TT):
                ts(nmx[:, t:t + 1], m8[:, t, 0:1], -1.0, None, ALU.mult)
                ts(gtm[:, t, :], lg[:, t, :], m8[:, t, 3:4], None, ALU.is_gt)
                ts(eqm[:, t, :], lg[:, t, :], m8[:, t, 3:4], None, ALU.is_equal)
            dve.drain()
            for t in range(TT):
                dve.tensor_reduce(rcp[:, t:t + 1], gtm[:, t, :], AX_X, ALU.add)
            dve.drain()
            for t in range(TT):
                dve.tensor_tensor_scan(csm[:, t, :], ones[:, 0:E], eqm[:, t, :], rcp[:, t:t + 1], ALU.mult, ALU.add)
            dve.drain()
            for t in range(TT):
                stt(csm[:, t, :], csm[:, t, :], float(TOPK), eqm[:, t, :], ALU.is_le, ALU.mult)
            dve.drain()
            tt(sel, csm, gtm, ALU.add)
            dve.drain()
            dve.memset(tmp_inc, 0.0).then_inc(rt_dve, 1)
            dve.wait_ge(rt_act, 1)
            tt(ex, ex, sel, ALU.mult)
            dve.drain()
            dve.tensor_reduce(rcp[:, 0:2], ex, AX_X, ALU.add)
            dve.drain()
            dve.reciprocal(rcp[:, 0:2], rcp[:, 0:2])
            dve.drain()
            for t in range(TT):
                ts(gatx[:, t, 0:E], ex[:, t, :], rcp[:, t:t + 1], None, ALU.mult)
            dve.wait_ge(rt_pe, 2)
            stt(posx[:, :, 0:E], bank(5, 64).rearrange("p (t e) -> p t e", t=2), 1.0, sel, ALU.add, ALU.mult)
            dve.tensor_copy(cnt[0:E, 0:1], bank(6, 1, slice(0, E)))
            dve.drain()
            ts(posx[:, :, 0:E], posx[:, :, 0:E], -1.0, None, ALU.add)
            ts(cnt[0:E, 1:2], cnt[0:E, 0:1], float(CAP), None, ALU.is_gt)
            ts(cnt[0:E, 2:3], cnt[0:E, 0:1], float(2 * CAP), None, ALU.is_gt)
            ts(cnt[0:E, 3:4], cnt[0:E, 0:1], float(3 * CAP), None, ALU.is_gt)
            dve.drain()
            tt(cnt[0:E, 1:2], cnt[0:E, 1:2], cnt[0:E, 2:3], ALU.add)
            dve.drain()
            tt(cnt[0:E, 1:2], cnt[0:E, 1:2], cnt[0:E, 3:4], ALU.add)
            dve.drain()
            dve.memset(tmp_inc, 0.0).then_inc(rt_dve, 1)
            dve.wait_ge(rt_pe, 3)
            dve.tensor_copy(cnt[0:E, 4:5], bank(7, 1, slice(0, E)))
            dve.tensor_copy(posT, bank(4, T, slice(0, E)))
            dve.tensor_copy(gatT, bank(4, T, slice(0, E), at=T))
            dve.tensor_copy(IE[0:E, 0:E], ident[0:E, 0:E])
            dve.drain()
            tt(cnt[0:E, 5:6], cnt[0:E, 4:5], cnt[0:E, 1:2], ALU.subtract)
            ts(Aj[0:E, :], iotaj[0:E, :], cnt[0:E, 4:5], None, ALU.is_ge)
            dve.drain()
            ts(IE[0:E, E:NIT], iotaj[0:E, :], cnt[0:E, 5:6], None, ALU.is_ge)
            dve.drain()
            tt(IE[0:E, E:NIT], IE[0:E, E:NIT], Aj[0:E, :], ALU.subtract)
            dve.drain()
            ts(EXj[0:E, :], IE[0:E, E:NIT], cnt[0:E, 5:6], None, ALU.mult)
            dve.drain()
            dve.memset(tmp_inc, 0.0).then_inc(rt_dve, 1)
            dve.wait_ge(rt_pe, 4)
            ts(itf[:, 0:E], iota64[:, 0:E], 0.0, None, ALU.add)
            ts(itf[:, E:NIT], bank(5, 17), float(E - 1), None, ALU.min)
            ts(itf[:, NIT:NIT + 1], bank(5, 1, at=64), float(E), None, ALU.add)
            tt(csm[:, 0, 0:17], iotaj[:, :], bank(5, 17, at=32), ALU.subtract)
            dve.drain()
            ts(csm[:, 0, 0:17], csm[:, 0, 0:17], float(CAP), float(CAP), ALU.mult, ALU.add)
            dve.tensor_copy(items_i[0:1, :], itf[0:1, :]).then_inc(items_ready, 1)
            dve.drain()
            for t in range(TT):
                tt(posx[:, t, E:NIT], bank(6, 17, at=t * 17), csm[:, 0, 0:17], ALU.subtract)
                dve.tensor_copy(gatx[:, t, E:NIT], bank(6, 17, at=64 + t * 17))
            dve.memset(nmx[:, 2:3], 0.0).then_inc(zero_ready, 1)
            dve.drain()
            dve.wait_ge(items_ready, 1)
            n_items = dve.value_load(items_i[0:1, NIT:NIT + 1], min_val=E, max_val=E + MAX_EXTRA)

            def choose(j):
                for t in range(TT):
                    last = ts(selx[:, t, :], iota64[:, :], posx[:, t, ds(j, 1)], None, ALU.is_equal)
                last.then_inc(selx_ready, 1)

            def gathered_columns(j):
                dve.wait_ge(xe_turned, j + 1)
                dve.tensor_copy(xeT.rearrange("p (h c) s -> p c h s", h=2),
                                bank(7).rearrange("p (c h s) -> p c h s", c=4, h=2)).then_inc(xeT_ready, 1)

            def accumulate(i):
                for q, b in enumerate((4, 5, 0, 1)):
                    t, n = q // 2, q % 2
                    dve.wait_ge(sc_mm, i * 4 + (q + 1))
                    y = YB[:, t, n * HALF:(n + 1) * HALF]
                    tt(y, y, bank(b), ALU.add).then_inc(acc_done, 1)

            choose(0)
            dve.wait_ge(rt_pe, 5)
            for f2 in range(2):
                dve.tensor_copy(bguT[:, :, 8 * f2:8 * f2 + 8].rearrange("p i f -> p f i"),
                                bank(f2, 8 * NIT).rearrange("p (f i) -> p f i", f=8))
            dve.drain()
            dve.memset(nmx[:, 3:4], 0.0).then_inc(acc_done, 1)
            gathered_columns(0)
            with dve.Fori(0, n_items) as i:
                dve.wait_ge(gat_mm, i + 1)
                choose(i + 1)
                dve.wait_ge(selT_ev, i + 1)
                for t in range(TT):
                    for h in range(2):
                        last = ts(selg[:, t, h * CAP:(h + 1) * CAP], iota64[:, :], posx[:, t, ds(i, 1)],
                                  gatx[:, t, ds(i, 1)], ALU.is_equal, ALU.mult)
                last.then_inc(selg_ready, 1)
                dve.wait_ge(h_turned, i + 1)
                hT = banks(2, D).rearrange("p (f c s) -> p f c s", f=8, c=2)
                bg = bguT[:, ds(i, 1), :].squeeze(1)
                tt(gs_b, hT[:, :, 0, :], bg[:, 0:8].unsqueeze(2).to_broadcast([P, 8, CAP]), ALU.add)
                tt(us_b, hT[:, :, 1, :], bg[:, 8:16].unsqueeze(2).to_broadcast([P, 8, CAP]), ALU.add)
                dve.drain()
                ts(gs_b, gs_b, LIMIT, None, ALU.min).then_inc(g_ready, 1)
                ts(us_b, us_b, LIMIT, -LIMIT, ALU.min, ALU.max)
                dve.drain()
                stt(us_b, us_b, 1.0, gs_b, ALU.add, ALU.mult)
                dve.drain()
                dve.wait_ge(sg_ready, i + 1)
                tt(actT, us_b, ss_b, ALU.mult).then_inc(act_ready, 1)
                accumulate(i)
                gathered_columns(i + 1)
            accumulate(n_items)
            dve.drain()
            for t in range(TT):
                layer_norm_stats(t, YB[:, t, :])
                layer_norm_apply(1, t).then_inc(x_updated, 1)
            for L in range(2):
                for t in range(TT):
                    normed_rows(2 + 4 * L, t)
                if L == 0:
                    dve.memset(qab, 0.0)
                else:
                    dve.memset(kab, 0.0)
                columns(2 + 2 * L, gsc[:, L, 0:8], shc[:, L, 0:8])
                if L == 1:
                    dve.wait_ge(small_loaded, 48)
                    dve.wait_ge(flog_done, 1)
                    tt(lf, bank(4, 32).rearrange("p (t h) -> p t h", t=2),
                       bfg.unsqueeze(1).to_broadcast([P, 2, 16]), ALU.add)
                    dve.drain()
                    dve.memset(tmp_inc, 0.0).then_inc(flog_dve, 1)
                    dve.wait_ge(flog_act, 1)
                    stt(lf, lf, 0.0, lfb, ALU.min, ALU.subtract).then_inc(flog_dve, 1)
                    dve.wait_ge(cum_done, 1)
                    dve.tensor_copy(cumT, bank(5, 32).rearrange("p (t h) -> p t h", t=2))
                    ts(ncumR, bank(6, T, slice(0, 16)), -1.0, None, ALU.mult).then_inc(ncum_ready, 1)
                    dve.wait_ge(ncum_loaded, 16)
                attention(1 + L)
                weights_low(L, 0, 0)
                if L == 0:
                    modulation_gates(1)
                for t in range(TT):
                    if L == 0:
                        modulation_columns(1, t)
                    if t == 1:
                        normed_rows(4 + 4 * L, 0)
                    add_normed(3 + 4 * L, t, gtg[L][:, 0, :])
                normed_rows(4 + 4 * L, 1)
                columns(3 + 2 * L, gsc[:, L, 8:16], shc[:, L, 8:16], split=True)
                columns_low(L)
                weights_low(L, 1, 1)
                down_low(L, 0, 0)

                def ffn_tile(j, s, w, low=None):
                    dve.wait_ge(fgu_done, j + (FT * L + 1))
                    gate, up = gu[:, s, 0, :], gu[:, s, 1, :]
                    dve.tensor_reduce(gu[:, s, :, :], PS[:, 4 + 2 * s:6 + 2 * s, :].rearrange("p c (h t) -> p c t h", h=2),
                                      AX_X, ALU.add)
                    dve.drain()
                    col = lambda r: vcol[:, L, ds(j + (64 + r * FT), 1)]
                    ts(cv[s], gate, col(2), col(3), ALU.mult, ALU.add)
                    dve.drain()
                    stt(cv[s][:, 1:T], gate[:, 0:T - 1], col(1), cv[s][:, 1:T], ALU.mult, ALU.add)
                    dve.drain()
                    stt(cv[s][:, 2:T], gate[:, 0:T - 2], col(0), cv[s][:, 2:T], ALU.mult, ALU.add)\
                        .then_inc(cv_ready, 1)
                    if low is not None:
                        weights_low(L, low, s)
                    dve.wait_ge(sl_ready, j + (FT * L + 1))
                    if w:
                        dve.wait_ge(fdn_done, j + (FT * L - 1))
                    tt(aT[s], sl[s], up, ALU.mult)
                    tt(acts[s][:, 0, :].bitcast(F32R), sl[s], up, ALU.mult)
                    dve.drain()
                    tt(acts[s][:, 1, :].bitcast(F32R), aT[s], acts[s][:, 0, :], ALU.subtract).then_inc(fact_ready, 1)

                for s in range(2):
                    ffn_tile(s, s, False, s + 2)
                    down_low(L, s + 1, 1 - s)
                with dve.Fori(1, FT // 2 - 1) as i:
                    for s in range(2):
                        ffn_tile(i * 2 + s, s, True, i * 2 + (s + 2))
                        down_low(L, i * 2 + (s + 1), 1 - s)
                ffn_tile(FT - 2, 0, True)
                down_low(L, FT - 1, 1)
                ffn_tile(FT - 1, 1, True)
                for t in range(TT):
                    add_normed(5 + 4 * L, t, gtg[L][:, 1, :])


_INS = ["x", "rel_bias", "a_w_in", "a_w_out", "ln_g", "ln_b", "moe_w_router", "moe_b_router", "moe_w_gate_up",
        "moe_b_gate_up", "moe_w_down", "moe_b_down", "c_2", "w_mod_2", "b_mod_2", "g_mix_pre_2", "g_mix_post_2",
        "w_qkv_2", "w_o_2", "w_fg_2", "b_fg_2", "g_ffn_pre_2", "g_ffn_post_2", "w_ffn_gate_2", "w_ffn_up_2",
        "w_conv_2", "b_conv_2", "w_ffn_down_2"]


def kernel(**inputs):
    import concourse.bacc as _bacc
    from concourse.bass_utils import run_bass_kernel_spmd as _run

    nc = _bacc.Bacc("TRN2", target_bir_lowering=False, num_devices=1)
    arrays, args = {}, {}
    for name in _INS:
        x = np.ascontiguousarray(inputs[name])
        arrays[f"in_{name}"] = x
        args[name] = nc.dram_tensor(f"in_{name}", x.shape, mybir.dt.from_np(x.dtype), kind="ExternalInput").ap()
    out = nc.dram_tensor("out_0", (1, T, D), F32, kind="ExternalOutput").ap()
    block_kernel(nc, args, out)
    r = _run(nc, [arrays], core_ids=[0])
    return r.results[0]["out_0"]
```
